# Optimizing a Trainium2 kernel written in Bass

```python
import jax, jax.numpy as jnp
from jax import lax
import numpy as np

D_MODEL = 1024
BATCH = 1
SEQ = 256
DEPTH = 2

GRID_W = 64
CTX_LEN = 256
EPS = 1e-6
MLA_HEADS = 8
Q_LORA = 256
KV_LORA = 128
QK_NOPE = 64
QK_ROPE = 32
V_HEAD = 64
QK_HEAD = QK_NOPE + QK_ROPE
ROPE_BASE = 10000.0
Q_BLOCK = 128
FNET_GROUPS = 4
FNET_GROUP_DIM = 64
FNET_C = FNET_GROUPS * FNET_GROUP_DIM
CONV_C = 256
CONV_W = 31
N_BRANCH = 3
PEER_HEADS = 8
N_KEYS = 128
N_EXPERTS = N_KEYS * N_KEYS
D_KEY = 128
PEER_TOPK = 16
PEER_CHUNK = 128
KV_IN = KV_LORA + QK_ROPE
REST_SPLITS = [Q_LORA, Q_LORA + FNET_C, Q_LORA + FNET_C + 2 * CONV_C]
IN_COLS = KV_IN + Q_LORA + FNET_C + 2 * CONV_C + N_BRANCH * D_MODEL


def rmsnorm(x, g):
    xf = x.astype(jnp.float32)
    y = xf * lax.rsqrt(jnp.mean(xf * xf, axis=-1, keepdims=True) + EPS)
    return (y * g.astype(jnp.float32)).astype(x.dtype)

def layernorm(x, g, b):
    xf = x.astype(jnp.float32)
    mu = jnp.mean(xf, axis=-1, keepdims=True)
    var = jnp.mean(jnp.square(xf - mu), axis=-1, keepdims=True)
    y = (xf - mu) * lax.rsqrt(var + EPS)
    return (y * g.astype(jnp.float32) + b.astype(jnp.float32)).astype(x.dtype)

def adaln(cond, w_mod, b_mod):
    return jnp.split(jax.nn.silu(cond) @ w_mod + b_mod, 6, axis=-1)

def modulate(h, shift, scale):
    return h * (1.0 + scale[:, None, :]) + shift[:, None, :]

def axial_rope_tables(n, dtype):
    rows = n // GRID_W
    row = jnp.repeat(jnp.arange(rows, dtype=jnp.float32), GRID_W)
    col = jnp.tile(jnp.arange(GRID_W, dtype=jnp.float32), rows)
    half = QK_ROPE // 2
    inv = ROPE_BASE ** (-jnp.arange(0, half, 2, dtype=jnp.float32) / half)
    ar = row[:, None] * inv
    ac = col[:, None] * inv
    ang = jnp.concatenate([ar, ar, ac, ac], axis=-1)
    return jnp.cos(ang).astype(dtype), jnp.sin(ang).astype(dtype)

def _rotate_half(z):
    z1, z2 = jnp.split(z, 2, axis=-1)
    return jnp.concatenate([-z2, z1], axis=-1)

def apply_axial_rope(z, cos, sin):
    zr, zc = jnp.split(z, 2, axis=-1)
    rot = jnp.concatenate([_rotate_half(zr), _rotate_half(zc)], axis=-1)
    return z * cos[:, None, :] + rot * sin[:, None, :]

def mla_q(cq, lp, rope):
    b, t, _ = cq.shape
    q = (rmsnorm(cq, lp['g_cq']) @ lp['w_uq']).reshape(b, t, MLA_HEADS, QK_HEAD)
    q = rmsnorm(q, lp['g_qn'])
    if rope is not None:
        q = jnp.concatenate([q[..., :QK_NOPE], apply_axial_rope(q[..., QK_NOPE:], *rope)], axis=-1)
    return q

def mla_kv(z, lp, rope):
    b, t, _ = z.shape
    ckv, kr = jnp.split(z, [KV_LORA], axis=-1)
    kv = (rmsnorm(ckv, lp['g_ckv']) @ lp['w_ukv']).reshape(b, t, MLA_HEADS, QK_NOPE + V_HEAD)
    k_nope, v = kv[..., :QK_NOPE], kv[..., QK_NOPE:]
    k_rope = jnp.broadcast_to(kr[:, :, None, :], (b, t, MLA_HEADS, QK_ROPE))
    k = rmsnorm(jnp.concatenate([k_nope, k_rope], axis=-1), lp['g_kn'])
    if rope is not None:
        k = jnp.concatenate([k[..., :QK_NOPE], apply_axial_rope(k[..., QK_NOPE:], *rope)], axis=-1)
    return k, v

def softmax_attend(q, k, v):
    s = jnp.einsum('bqhd,bkhd->bhqk', q, k).astype(jnp.float32) * (QK_HEAD ** -0.5)
    p = jax.nn.softmax(s, axis=-1).astype(v.dtype)
    return jnp.einsum('bhqk,bkhd->bqhd', p, v)

def latent_attention(q, k, v):
    b, s, h, _ = q.shape
    nb = s // Q_BLOCK
    qb = q.reshape(b, nb, Q_BLOCK, h, QK_HEAD).transpose(1, 0, 2, 3, 4)
    o = lax.map(lambda qi: softmax_attend(qi, k, v), qb)
    return o.transpose(1, 0, 2, 3, 4).reshape(b, s, h * V_HEAD)

def fourier_mix(z):
    b, t, _ = z.shape
    zz = z.astype(jnp.float32).reshape(b, t, FNET_GROUPS, FNET_GROUP_DIM)
    f = jnp.fft.fft2(zz, axes=(1, 3), norm='ortho').real
    return f.reshape(b, t, FNET_C).astype(z.dtype)

def conformer_conv(z, lp):
    a, g = jnp.split(z, 2, axis=-1)
    u = a * jax.nn.sigmoid(g)
    u = lax.conv_general_dilated(u, lp['w_dw'], window_strides=(1,), padding=[(CONV_W // 2, CONV_W // 2)],
                                 dimension_numbers=('NWC', 'WIO', 'NWC'), feature_group_count=CONV_C) + lp['b_dw']
    return jax.nn.silu(layernorm(u, lp['g_cln'], lp['b_cln']))

def branch_merge(a_o, zf, zc, zg, lp):
    b, t, _ = zg.shape
    g = jax.nn.sigmoid(zg.astype(jnp.float32)).astype(zg.dtype).reshape(b, t, N_BRANCH, D_MODEL)
    m = (g[:, :, 0] * (a_o @ lp['wb_attn'])
         + g[:, :, 1] * (fourier_mix(zf) @ lp['wb_fnet'])
         + g[:, :, 2] * (conformer_conv(zc, lp) @ lp['wb_conv']))
    return m @ lp['w_out']

def mixer_sublayer(x, ctx, mod_x, mod_c, lp, rope, update_ctx):
    sh, sc, gt = mod_x
    csh, csc, cgt = mod_c
    hx = modulate(rmsnorm(x, lp['g_norm1']), sh, sc)
    hc = modulate(rmsnorm(ctx, lp['g_norm1']), csh, csc)
    k_c, v_c = mla_kv(hc @ lp['w_in'][:, :KV_IN], lp, None)
    k_x, v_x = mla_kv(hx @ lp['w_in'][:, :KV_IN], lp, rope)
    cq_x, zf_x, zc_x, zg_x = jnp.split(hx @ lp['w_in'][:, KV_IN:], REST_SPLITS, axis=-1)
    q_x = mla_q(cq_x, lp, rope)
    a_x = latent_attention(q_x, jnp.concatenate([k_c, k_x], axis=1), jnp.concatenate([v_c, v_x], axis=1))
    x = x + gt[:, None, :] * branch_merge(a_x, zf_x, zc_x, zg_x, lp)
    if update_ctx:
        b, l, _ = ctx.shape
        cq_c, zf_c, zc_c, zg_c = jnp.split(hc @ lp['w_in'][:, KV_IN:], REST_SPLITS, axis=-1)
        a_c = softmax_attend(mla_q(cq_c, lp, None), k_c, v_c).reshape(b, l, MLA_HEADS * V_HEAD)
        ctx = ctx + cgt[:, None, :] * branch_merge(a_c, zf_c, zc_c, zg_c, lp)
    return x, ctx

def peer_ffn(h, w_query, sub_keys, u_tab, v_tab):
    b, t, d = h.shape
    chunks = h.reshape(-1, PEER_CHUNK, d)

    def chunk(hc):
        q = (hc @ w_query).reshape(PEER_CHUNK, PEER_HEADS, 2, D_KEY // 2)
        s = jnp.einsum('chpd,hpnd->chpn', q, sub_keys).astype(jnp.float32)
        s_top, i_top = lax.top_k(s, PEER_TOPK)
        cand = (s_top[:, :, 0, :, None] + s_top[:, :, 1, None, :]).reshape(PEER_CHUNK, PEER_HEADS, PEER_TOPK * PEER_TOPK)
        cand_id = (i_top[:, :, 0, :, None] * N_KEYS + i_top[:, :, 1, None, :]).reshape(PEER_CHUNK, PEER_HEADS, PEER_TOPK * PEER_TOPK)
        best, pos = lax.top_k(cand, PEER_TOPK)
        eid = jnp.take_along_axis(cand_id, pos, axis=-1)
        gate = jax.nn.softmax(best, axis=-1).astype(hc.dtype)
        u = jnp.take(u_tab, eid, axis=0)
        act = jax.nn.gelu(jnp.einsum('chkd,cd->chk', u, hc)) * gate
        v = jnp.take(v_tab, eid, axis=0)
        return jnp.einsum('chk,chkd->cd', act, v)

    return lax.map(chunk, chunks).reshape(b, t, d)

def first_inputs(seed: int = 0) -> dict:
    key = jax.random.key(seed)
    ks = jax.random.split(key, 28)
    f32 = jnp.float32

    def nrm(k, shape, scale):
        return jax.random.normal(k, shape, f32) * scale

    def gain(k, shape):
        return 1.0 + 0.02 * jax.random.normal(k, shape, f32)

    L = DEPTH
    return {
        'x': nrm(ks[0], (BATCH, SEQ, D_MODEL), 1.0),
        'c': nrm(ks[1], (BATCH, D_MODEL), 1.0),
        'ctx': nrm(ks[2], (BATCH, CTX_LEN, D_MODEL), 1.0),
        'c_ctx': nrm(ks[3], (D_MODEL,), 1.0),
        'w_mod': nrm(ks[4], (L, D_MODEL, 6 * D_MODEL), 0.5 * D_MODEL ** -0.5),
        'b_mod': nrm(ks[5], (L, 6 * D_MODEL), 0.02),
        'g_norm1': gain(ks[6], (L, D_MODEL)),
        'w_in': nrm(ks[7], (L, D_MODEL, IN_COLS), D_MODEL ** -0.5),
        'g_ckv': gain(ks[8], (L, KV_LORA)),
        'w_ukv': nrm(ks[9], (L, KV_LORA, MLA_HEADS * (QK_NOPE + V_HEAD)), KV_LORA ** -0.5),
        'g_cq': gain(ks[10], (L, Q_LORA)),
        'w_uq': nrm(ks[11], (L, Q_LORA, MLA_HEADS * QK_HEAD), Q_LORA ** -0.5),
        'g_qn': gain(ks[12], (L, QK_HEAD)),
        'g_kn': gain(ks[13], (L, QK_HEAD)),
        'w_dw': nrm(ks[14], (L, CONV_W, 1, CONV_C), CONV_W ** -0.5),
        'b_dw': nrm(ks[15], (L, CONV_C), 0.02),
        'g_cln': gain(ks[16], (L, CONV_C)),
        'b_cln': nrm(ks[17], (L, CONV_C), 0.02),
        'wb_attn': nrm(ks[18], (L, MLA_HEADS * V_HEAD, D_MODEL), (MLA_HEADS * V_HEAD) ** -0.5),
        'wb_fnet': nrm(ks[19], (L, FNET_C, D_MODEL), FNET_C ** -0.5),
        'wb_conv': nrm(ks[20], (L, CONV_C, D_MODEL), CONV_C ** -0.5),
        'w_out': nrm(ks[21], (L, D_MODEL, D_MODEL), D_MODEL ** -0.5),
        'g_norm2': gain(ks[22], (L, D_MODEL)),
        'w_query': nrm(ks[23], (L, D_MODEL, PEER_HEADS * D_KEY), D_MODEL ** -0.5),
        'sub_keys': nrm(ks[24], (L, PEER_HEADS, 2, N_KEYS, D_KEY // 2), (D_KEY // 2) ** -0.5),
        'u_tab': nrm(ks[25], (L, N_EXPERTS, D_MODEL), D_MODEL ** -0.5),
        'v_tab': nrm(ks[26], (L, N_EXPERTS, D_MODEL), PEER_HEADS ** -0.5),
    }

def first_block(x, c, ctx, c_ctx, w_mod, b_mod, g_norm1, w_in, g_ckv, w_ukv, g_cq, w_uq, g_qn, g_kn,
              w_dw, b_dw, g_cln, b_cln, wb_attn, wb_fnet, wb_conv, w_out, g_norm2, w_query, sub_keys,
              u_tab, v_tab):
    rope = axial_rope_tables(x.shape[1], x.dtype)
    for i in range(DEPTH):
        lp = {'g_norm1': g_norm1[i], 'w_in': w_in[i], 'g_ckv': g_ckv[i], 'w_ukv': w_ukv[i],
              'g_cq': g_cq[i], 'w_uq': w_uq[i], 'g_qn': g_qn[i], 'g_kn': g_kn[i],
              'w_dw': w_dw[i], 'b_dw': b_dw[i], 'g_cln': g_cln[i], 'b_cln': b_cln[i],
              'wb_attn': wb_attn[i], 'wb_fnet': wb_fnet[i], 'wb_conv': wb_conv[i], 'w_out': w_out[i]}
        sh1, sc1, gt1, sh2, sc2, gt2 = adaln(c, w_mod[i], b_mod[i])
        csh1, csc1, cgt1, csh2, csc2, cgt2 = adaln(c_ctx[None, :], w_mod[i], b_mod[i])
        update_ctx = i < DEPTH - 1
        x, ctx = mixer_sublayer(x, ctx, (sh1, sc1, gt1), (csh1, csc1, cgt1), lp, rope, update_ctx)
        x = x + gt2[:, None, :] * peer_ffn(modulate(rmsnorm(x, g_norm2[i]), sh2, sc2),
                                           w_query[i], sub_keys[i], u_tab[i], v_tab[i])
        if update_ctx:
            ctx = ctx + cgt2[:, None, :] * peer_ffn(modulate(rmsnorm(ctx, g_norm2[i]), csh2, csc2),
                                                    w_query[i], sub_keys[i], u_tab[i], v_tab[i])
    return x


N_A = DEPTH // 2
N_B = DEPTH - N_A

LRU_WIDTH = D_MODEL
LRU_HEADS = 8
LRU_BLOCK = LRU_WIDTH // LRU_HEADS
LRU_CONV = 4
LRU_C = 8.0

N_HEADS = 8
HEAD_DIM = D_MODEL // N_HEADS

D_FF = 3 * D_MODEL
FFN_CONV = 3

DN_ALPHA = (2 * DEPTH) ** 0.25
DN_BETA = (8 * DEPTH) ** -0.25
LN_EPS = 1e-5


def layer_norm(x, g, b):
    xf = x.astype(jnp.float32)
    mu = jnp.mean(xf, axis=-1, keepdims=True)
    xc = xf - mu
    var = jnp.mean(xc * xc, axis=-1, keepdims=True)
    y = xc * lax.rsqrt(var + LN_EPS) * g.astype(jnp.float32) + b.astype(jnp.float32)
    return y.astype(x.dtype)

def causal_depthwise_conv(x, w, b):
    K = w.shape[0]
    S = x.shape[1]
    xp = jnp.pad(x, ((0, 0), (K - 1, 0), (0, 0)))
    y = b + xp[:, 0:S] * w[0]
    for k in range(1, K):
        y = y + xp[:, k:k + S] * w[k]
    return y

def _lin_combine(left, right):
    a1, b1 = left
    a2, b2 = right
    return a1 * a2, a2 * b1 + b2

def rg_lru_block(x, w_in, b_in, conv_w, conv_b, w_gates, b_gates, a_param, w_out, b_out):
    B, S, _ = x.shape
    proj = x @ w_in + b_in
    y_br = jax.nn.gelu(proj[..., :LRU_WIDTH])
    x_br = causal_depthwise_conv(proj[..., LRU_WIDTH:], conv_w, conv_b)
    xb = x_br.reshape(B, S, LRU_HEADS, LRU_BLOCK)
    gates = jnp.einsum('bsnc,ncg->bsng', xb, w_gates) + b_gates
    gates = jax.nn.sigmoid(gates.astype(jnp.float32))
    gate_i = gates[..., :LRU_BLOCK].reshape(B, S, LRU_WIDTH)
    gate_r = gates[..., LRU_BLOCK:].reshape(B, S, LRU_WIDTH)
    log_a = -LRU_C * gate_r * jax.nn.softplus(-a_param.astype(jnp.float32))
    a = jnp.exp(log_a)
    mult = jnp.sqrt(jnp.maximum(1.0 - jnp.exp(2.0 * log_a), 0.0))
    is_start = (jnp.arange(S) == 0)[None, :, None]
    mult = jnp.where(is_start, 1.0, mult)
    u = mult * gate_i * x_br.astype(jnp.float32)
    _, h = lax.associative_scan(_lin_combine, (a, u), axis=1)
    return (h.astype(x.dtype) * y_br) @ w_out + b_out

def stick_breaking_attention(q, k, v):
    B, S, H, Dh = q.shape
    scale = Dh ** -0.5
    outs = []
    for i in range(S // Q_BLOCK):
        q0 = i * Q_BLOCK
        kv_len = q0 + Q_BLOCK
        q_blk = q[:, q0:kv_len]
        k_p = k[:, :kv_len]
        v_p = v[:, :kv_len]
        z = jnp.einsum('bqhd,bkhd->bhqk', q_blk, k_p).astype(jnp.float32) * scale
        q_pos = q0 + jnp.arange(Q_BLOCK)
        k_pos = jnp.arange(kv_len)
        mask = k_pos[None, :] < q_pos[:, None]
        log_beta = jax.nn.log_sigmoid(z)
        log_1m = jnp.where(mask, jax.nn.log_sigmoid(-z), 0.0)
        suffix = lax.cumsum(log_1m, axis=3, reverse=True) - log_1m
        w = jnp.where(mask, jnp.exp(log_beta + suffix), 0.0)
        o = jnp.einsum('bhqk,bkhd->bqhd', w, v_p.astype(jnp.float32))
        outs.append(o.astype(q.dtype))
    return jnp.concatenate(outs, axis=1)

def conv_ffn(x, w_up, conv_w, conv_b, w_down):
    h = causal_depthwise_conv(x @ w_up, conv_w, conv_b)
    return (jax.nn.gelu(h[..., :D_FF]) * h[..., D_FF:]) @ w_down

def second_inputs(seed: int = 0) -> dict:
    key = jax.random.key(seed)
    ks = jax.random.split(key, 24)
    f32 = jnp.float32

    def nrm(k, shape, fan_in, gain=1.0):
        return jax.random.normal(k, shape, f32) * (gain * fan_in ** -0.5)

    def small(k, shape):
        return 0.01 * jax.random.normal(k, shape, f32)

    W, HD = LRU_WIDTH, N_HEADS * HEAD_DIM
    u = jax.random.uniform(ks[8], (N_A, W), f32, minval=0.9, maxval=0.999)
    s = u ** (1.0 / LRU_C)
    lru_a_param = jnp.log(s) - jnp.log1p(-s)
    kv_w = jnp.concatenate([nrm(ks[11], (D_MODEL, HD), D_MODEL),
                            nrm(ks[12], (D_MODEL, HD), D_MODEL, DN_BETA)], axis=1)
    return {
        "x": jax.random.normal(ks[0], (BATCH, SEQ, D_MODEL), f32),
        "lru_w_in": nrm(ks[1], (N_A, D_MODEL, 2 * W), D_MODEL),
        "lru_b_in": small(ks[2], (N_A, 2 * W)),
        "lru_conv_w": nrm(ks[3], (N_A, LRU_CONV, W), LRU_CONV),
        "lru_conv_b": small(ks[4], (N_A, W)),
        "lru_w_gates": nrm(ks[5], (N_A, LRU_HEADS, LRU_BLOCK, 2 * LRU_BLOCK), LRU_BLOCK),
        "lru_b_gates": small(ks[6], (N_A, LRU_HEADS, 2 * LRU_BLOCK)),
        "lru_a_param": lru_a_param,
        "lru_w_out": nrm(ks[9], (N_A, W, D_MODEL), W, DN_BETA),
        "lru_b_out": small(ks[10], (N_A, D_MODEL)),
        "kv_w": kv_w,
        "attn_w_q": nrm(ks[13], (N_B, D_MODEL, HD), D_MODEL),
        "attn_w_out": nrm(ks[14], (N_B, HD, D_MODEL), HD, DN_BETA),
        "ffn_w_up": nrm(ks[15], (DEPTH, D_MODEL, 2 * D_FF), D_MODEL),
        "ffn_conv_w": nrm(ks[16], (DEPTH, FFN_CONV, 2 * D_FF), FFN_CONV),
        "ffn_conv_b": small(ks[17], (DEPTH, 2 * D_FF)),
        "ffn_w_down": nrm(ks[18], (DEPTH, D_FF, D_MODEL), D_FF, DN_BETA),
        "ln_g": 1.0 + small(ks[19], (DEPTH, 2, D_MODEL)),
        "ln_b": small(ks[20], (DEPTH, 2, D_MODEL)),
    }

def second_block(x, lru_w_in, lru_b_in, lru_conv_w, lru_conv_b, lru_w_gates, lru_b_gates,
              lru_a_param, lru_w_out, lru_b_out, kv_w, attn_w_q, attn_w_out,
              ffn_w_up, ffn_conv_w, ffn_conv_b, ffn_w_down, ln_g, ln_b):
    B, S, _ = x.shape
    HD = N_HEADS * HEAD_DIM
    k_sh = None
    v_sh = None
    for layer in range(DEPTH):
        if layer < N_A:
            mix = rg_lru_block(x, lru_w_in[layer], lru_b_in[layer], lru_conv_w[layer],
                               lru_conv_b[layer], lru_w_gates[layer], lru_b_gates[layer],
                               lru_a_param[layer], lru_w_out[layer], lru_b_out[layer])
        else:
            if layer == N_A:
                kv = x @ kv_w
                k_sh = kv[..., :HD].reshape(B, S, N_HEADS, HEAD_DIM)
                v_sh = kv[..., HD:].reshape(B, S, N_HEADS, HEAD_DIM)
            j = layer - N_A
            q = (x @ attn_w_q[j]).reshape(B, S, N_HEADS, HEAD_DIM)
            o = stick_breaking_attention(q, k_sh, v_sh).reshape(B, S, HD)
            mix = o @ attn_w_out[j]
        x = layer_norm(DN_ALPHA * x + mix, ln_g[layer, 0], ln_b[layer, 0])
        f = conv_ffn(x, ffn_w_up[layer], ffn_conv_w[layer], ffn_conv_b[layer], ffn_w_down[layer])
        x = layer_norm(DN_ALPHA * x + f, ln_g[layer, 1], ln_b[layer, 1])
    return x


def setup_inputs(seed=0):
    out = dict(first_inputs(seed))
    for name, value in second_inputs(seed + 1).items():
        if name != "x":
            out[name + "_2"] = value
    return out


def reference(
    x, c, ctx, c_ctx, w_mod, b_mod, g_norm1, w_in, g_ckv, w_ukv, g_cq, w_uq, g_qn, g_kn, w_dw,
    b_dw, g_cln, b_cln, wb_attn, wb_fnet, wb_conv, w_out, g_norm2, w_query, sub_keys, u_tab,
    v_tab, lru_w_in_2, lru_b_in_2, lru_conv_w_2, lru_conv_b_2, lru_w_gates_2, lru_b_gates_2,
    lru_a_param_2, lru_w_out_2, lru_b_out_2, kv_w_2, attn_w_q_2, attn_w_out_2, ffn_w_up_2,
    ffn_conv_w_2, ffn_conv_b_2, ffn_w_down_2, ln_g_2, ln_b_2,
):
    x = first_block(
        x, c, ctx, c_ctx, w_mod, b_mod, g_norm1, w_in, g_ckv, w_ukv, g_cq, w_uq, g_qn, g_kn,
        w_dw, b_dw, g_cln, b_cln, wb_attn, wb_fnet, wb_conv, w_out, g_norm2, w_query, sub_keys,
        u_tab, v_tab,
    )
    return second_block(
        x, lru_w_in_2, lru_b_in_2, lru_conv_w_2, lru_conv_b_2, lru_w_gates_2, lru_b_gates_2,
        lru_a_param_2, lru_w_out_2, lru_b_out_2, kv_w_2, attn_w_q_2, attn_w_out_2, ffn_w_up_2,
        ffn_conv_w_2, ffn_conv_b_2, ffn_w_down_2, ln_g_2, ln_b_2,
    )


_drawn_inputs = setup_inputs


def setup_inputs(seed=0):
    import zlib

    import numpy as np

    out = dict(_drawn_inputs(seed))
    spreads = {}
    factors = {'ctx': 3.54,
     'g_norm1': 6.526,
     'g_ckv': 8.0,
     'g_cq': 8.0,
     'g_qn': 8.0,
     'g_kn': 8.0,
     'b_dw': 5.878,
     'g_cln': 8.0,
     'b_cln': 8.0,
     'g_norm2': 4.196,
     'lru_b_in_2': 6.199,
     'lru_conv_b_2': 6.195,
     'lru_b_gates_2': 30.241,
     'lru_b_out_2': 25.41,
     'ffn_conv_b_2': 8.0,
     'ln_g_2': 2.704,
     'ln_b_2': 6.22}
    for name, (base, spread) in spreads.items():
        noise = np.random.default_rng([zlib.crc32(name.encode()), seed]).standard_normal(out[name].shape)
        drawn = base * np.exp(spread * noise) if base else spread * noise
        out[name] = __import__('jax').numpy.asarray(drawn.astype(out[name].dtype))
    for name, factor in factors.items():
        out[name] = (out[name] * factor).astype(out[name].dtype)
    return out
```

```python
from contextlib import ExitStack

import numpy as np

import concourse.bass as bass
from concourse import mybir

F32 = mybir.dt.float32
U32 = mybir.dt.uint32
ALU = mybir.AluOpType
ACT = mybir.ActivationFunctionType
AX_X = mybir.AxisListType.X

P = 128
D = 1024
DC = D // P
SEQ = 256
LAYERS = 2
EPS = 1e-6
HEADS, NOPE, ROPE, VH = 8, 64, 32, 64
QKH = NOPE + ROPE
QL, KVL = 256, 128
KVR = KVL + ROPE
FC, GROUP = 256, 64
CC, TAPS = 256, 31
PAD = TAPS // 2
BRANCH = 3
PH, NK, TOPK = 8, 128, 16
EXPERTS = NK * NK
ATT_SCALE = float(QKH) ** -0.5

W2 = 1024
LCONV = 4
LRU_C = 8.0
FF = 3 * D
FJ = FF // P
FCONV = 3
LN_EPS = 1e-5
ALPHA = (2 * LAYERS) ** 0.25
H2, HD2 = 8, 128
STICK_SCALE = float(HD2) ** -0.5

RING, WIDE = 4, 2
SLOT = 4096
SLOTS = 3
ARENA = 22760
UB, VB = 8, 8
NEG = -3.0e38

COLS = [("c", DC), ("c_ctx", DC), ("b_mod", LAYERS * 6 * DC), ("g_norm1", LAYERS * DC), ("g_norm2", LAYERS * DC),
        ("g_ckv", LAYERS), ("g_cq", LAYERS * 2), ("w_dw", LAYERS * 2 * TAPS), ("b_dw", LAYERS * 2),
        ("g_cln", LAYERS * 2), ("b_cln", LAYERS * 2), ("lru_b_in", 2 * DC), ("lru_conv_w", LCONV * DC),
        ("lru_conv_b", DC), ("lru_b_gates", 2 * DC), ("lru_a_param", DC), ("ffn_conv_w", LAYERS * FCONV * 2 * FJ),
        ("ffn_conv_b", LAYERS * 2 * FJ)]
COL_AT, _n = {}, 0
for _name, _k in COLS:
    COL_AT[_name] = _n
    _n += _k
NCOLS = _n

CONST = [("ident", P), ("ones", P), ("zeros", P), ("tri", P), ("iota", TOPK), ("cos", 2 * ROPE), ("sin", 2 * ROPE),
         ("dft_t", 2 * 2 * SEQ), ("dft_c", P), ("dft_s", P), ("eps", 1),
         ("ln_eps", 1)]
CONST_AT, _n = {}, 0
for _name, _k in CONST:
    CONST_AT[_name] = _n
    _n += _k
NCONST = _n


def shape_constants():
    out = np.zeros((P, NCONST), np.float32)

    def put(name, a):
        out[:, CONST_AT[name]:CONST_AT[name] + a.shape[1]] = a

    put("ident", np.eye(P))
    put("ones", np.ones((P, P)))
    put("tri", np.tril(np.ones((P, P)), -1))
    put("iota", np.tile(np.arange(TOPK), (P, 1)))
    tok = np.arange(SEQ)
    half = ROPE // 2
    inv = 10000.0 ** (-np.arange(0, half, 2) / half)
    ar, ac = (tok // 64)[:, None] * inv, (tok % 64)[:, None] * inv
    ang = np.concatenate([ar, ar, ac, ac], -1)
    sign = np.tile(np.repeat([-1.0, 1.0], half // 2), 2)
    put("cos", np.cos(ang).reshape(2, P, ROPE).transpose(1, 0, 2).reshape(P, -1))
    put("sin", (np.sin(ang) * sign).reshape(2, P, ROPE).transpose(1, 0, 2).reshape(P, -1))
    at = 2 * np.pi * (np.outer(tok, tok) % SEQ) / SEQ
    both = np.concatenate([np.cos(at), np.sin(at)], 1) / np.sqrt(SEQ * GROUP)
    put("dft_t", both.reshape(2, P, 2 * SEQ).transpose(1, 0, 2).reshape(P, -1))
    ch = np.arange(GROUP)
    ac = 2 * np.pi * (np.outer(ch, ch) % GROUP) / GROUP
    put("dft_c", np.kron(np.eye(2), np.cos(ac)))
    put("dft_s", -np.kron(np.eye(2), np.sin(ac)))
    put("eps", np.full((P, 1), EPS))
    put("ln_eps", np.full((P, 1), LN_EPS))
    return out


class Stage:
    pass


class Weights:

    def __init__(self, kind, l, i, size, n):
        self.kind, self.l, self.i, self.size, self.n = kind, l, i, size, n
        self.release = None


class Count:
    def __init__(self):
        self.n = 0

    def take(self, k=1):
        self.n += k
        return self.n - k


def make_plan():
    ring, wide, items = Count(), Count(), []
    pl = Stage()
    pl.layers = []

    def item(kind, l, i, size):
        items.append(Weights(kind, l, i, size, len(items)))
        return items[-1]

    def mod_items(l, a, b):
        out = []
        for i in range(a, b):
            it, g = item("w_mod", l, i, 8 * 512), ring.take()
            it.release = ("ring", g)
            out.append((it, g, l, i))
        return out

    def grow(sets):
        return [ring.take(2) for _ in range(sets)]

    for l in range(LAYERS):
        s = Stage()
        s.l, s.n, s.sets = l, (4, 2)[l], (2, 1)[l]
        s.mod_a = mod_items(l, 0, 4) if l == 0 else []
        s.norm1 = ring.take(DC)
        s.zc = item("w_zc", l, 0, 8 * 512)
        s.conv_in = ring.take(4)
        s.zc.release = ("ring", s.conv_in + 3)
        s.wa = [item("w_a", l, i, 4 * 672) for i in range(2)]
        s.kvq = wide.take(4)
        for it in s.wa:
            it.release = ("wide", s.kvq + 3)
        s.fn_y, s.fn_f = [], []
        for _ in range(2 * s.sets):
            s.fn_y.append(ring.take())
            s.fn_f.append(ring.take())
        s.lat_k = ring.take()
        s.lat_q = ring.take(2)
        s.uk = item("w_uk", l, 0, 2560)
        s.kv = wide.take(4)
        s.q = wide.take(s.n)
        s.uk.release = ("wide", s.q + s.n - 1)
        s.cv_t = ring.take(s.n)
        s.cv_b = ring.take(2)
        N = HEADS * s.n
        s.N = N
        s.gk, s.gq, s.gs, s.gp, s.att = {}, {}, {}, {}, []
        s.gk[0], s.gq[0] = ring.take(), ring.take()
        for i in range(N + 2):
            if i < N:
                s.gs[i] = ring.take()
                if i % s.n == 0 and i // s.n + 1 < HEADS:
                    s.gk[i // s.n + 1], s.gq[i // s.n + 1] = ring.take(), ring.take()
            if 1 <= i <= N:
                s.gp[i - 1] = ring.take()
        s.pairs = wide.take(HEADS // 2)
        rest = [(0, i) for i in range(4, 12)] + [(1, i) for i in range(12)] if l == 0 else []
        s.merge, s.mods = [], []
        for j in range(DC):
            it = item("w_m", l, j, 4096)
            g = ring.take(2 * BRANCH)
            it.release = ("ring", g + 2 * BRANCH - 1)
            s.merge.append((it, g))
            k = [rest.pop(0) for _ in range(min(len(rest), 3))]
            s.mods.append([m for ll, i in k for m in mod_items(ll, i, i + 1)])
        s.grow1 = grow(s.sets)
        s.wo = [item("w_out", l, i, 4096) for i in range(2)]
        s.out = wide.take(s.n)
        for it in s.wo:
            it.release = ("wide", s.out + s.n - 1)
        s.norm2 = ring.take(DC)
        s.back = ring.take(2 * s.n)
        s.grow2 = grow(s.sets)
        s.wq = [item("w_query", l, i, 4096) for i in range(2)]
        s.query = ring.take(PH)
        for i, it in enumerate(s.wq):
            it.release = ("ring", s.query + 4 * i + 3)
        s.sk = item("sub_keys", l, 0, (PH + 2) * NK)
        s.sk.release = ("selected", l)
        s.exp = wide.take(s.n)
        pl.layers.append(s)

    def transposes():
        return ring.take(DC // 2)

    def ffn(l):
        f = Stage()
        f.l, f.xt, f.up, f.items = l, transposes(), [], []
        for j in range(FJ):
            it = item("w_ffn", l, j, 3072)
            f.items.append(it)
            f.up.append(ring.take())
        f.down = wide.take(2)
        for j in range(FJ):
            f.items[j].release = ("ring", f.up[j + 2]) if j + 2 < FJ else ("wide", f.down + 1)
        return f

    r = Stage()
    r.xt = transposes()
    r.w = [item("lru_in", 0, i, 4096) for i in range(4)]
    r.proj = ring.take(8)
    for i, it in enumerate(r.w):
        it.release = ("ring", r.proj + 2 * i + 1)
    r.wg = item("lru_gates", 0, 0, 2048)
    r.gates = ring.take(8)
    r.wg.release = ("ring", r.gates + 7)
    r.wo = [item("lru_out", 0, i, 4096) for i in range(2)]
    r.out = wide.take(2)
    for it in r.wo:
        it.release = ("wide", r.out + 1)
    pl.lru = r
    pl.ffn = [ffn(0)]
    a = Stage()
    a.xt = transposes()
    a.wk = [item("kv_k", 0, i, 4096) for i in range(2)]
    a.k = ring.take(4)
    a.wq = [item("attn_q", 0, i, 4096) for i in range(2)]
    a.q = ring.take(4)
    for w, g in ((a.wk, a.k), (a.wq, a.q)):
        for i, it in enumerate(w):
            it.release = ("ring", g + 2 * i + 1)
    a.wv = [item("kv_v", 0, i, 4096) for i in range(2)]
    a.v = wide.take(2)
    for it in a.wv:
        it.release = ("wide", a.v + 1)
    a.gz, a.gw = {}, {}
    N = H2 * 2
    for i in range(N + 3):
        if i < N:
            a.gz[i] = ring.take()
        if 2 <= i < N + 2:
            a.gw[i - 2] = ring.take()
    a.o = wide.take(H2)
    a.wo = [item("attn_out", 0, i, 4096) for i in range(2)]
    a.out = wide.take(2)
    for it in a.wo:
        it.release = ("wide", a.out + 1)
    pl.stick = a
    pl.ffn.append(ffn(1))
    pl.items = items
    return pl


def build(nc, w, out):
    pl = make_plan()
    with ExitStack() as ctx:
        def sb(name, shape, dt=F32):
            return ctx.enter_context(nc.sbuf_tensor(name, shape, dt))

        def sem(name):
            return ctx.enter_context(nc.semaphore(name))

        const = sb("const", [P, NCONST])
        cols = sb("cols", [P, NCOLS])
        hrow = sb("hrow", [P, 2 * LAYERS * QKH])
        x = sb("x", [P, 4, D])
        hT_b = sb("hT_b", [P, DC * 512])
        xn = sb("xn", [P, 4, D])
        wbuf = sb("wbuf", [P, SLOTS, SLOT])
        grow = sb("grow", [P, 2, D])
        cond = sb("cond", [P, DC, 2])
        mod = sb("mod", [P, LAYERS, 6 * DC, 2])
        amod = sb("amod", [P, LAYERS, 2, DC, 2])
        small = sb("small", [P, 416])
        arena = sb("arena", [P, ARENA])

        hT = hT_b[:, :].rearrange("p (k t) -> p k t", k=DC)
        xT = hT_b[:, 0:DC * SEQ].rearrange("p (k t) -> p k t", k=DC)
        mT = xn[:, :, :].rearrange("p a (b t) -> p (a b) t", t=512)

        def K(name, a=0, b=None):
            n = dict(CONST)[name]
            return const[:, CONST_AT[name] + a:CONST_AT[name] + (n if b is None else b)]

        def C(name, i, n=1):
            return cols[:, COL_AT[name] + i:COL_AT[name] + i + n]

        class Carve:
            def __init__(self, at=0):
                self.at = at

            def __call__(self, n):
                self.at += n
                assert self.at <= ARENA, self.at
                return arena[:, self.at - n:self.at]

        sm = Count()

        def tiny(n):
            at = sm.take(n)
            assert sm.n <= 416
            return small[:, at:at + n]

        ss = tiny(8)
        rstd = tiny(8)
        lss, lr = tiny(8), tiny(8)
        hss, hr = tiny(64), tiny(64)
        cst, cmv, cr = tiny(24), tiny(8), tiny(4)
        nmax, nms, rsum, rinv = tiny(4), tiny(4), tiny(4), tiny(4)
        lst, lmv, lrs = tiny(24), tiny(4), tiny(2)
        sp = tiny(48)
        lmv3 = lmv.rearrange("p (t c) -> p t c", c=2)
        cmv3 = cmv.rearrange("p (t c) -> p t c", c=2)

        c = Carve()
        conv_at = c.at
        upad = c(2 * 2 * (SEQ + 2 * PAD)).rearrange("p (c s t) -> p c s t", c=2, s=2)
        cacc = c(2 * 512).rearrange("p (c s t) -> p c s t", c=2, s=2)
        cn = c(4 * CC).rearrange("p (t c) -> p t c", t=4)
        sgc = c(2 * 512).rearrange("p (c t) -> p c t", c=2)
        c2 = Carve(conv_at)
        kTb = c2(2 * 512).rearrange("p (b t) -> p b t", b=2)
        qTb = c2(2 * 512).rearrange("p (b t) -> p b t", b=2)
        prob = c2(2 * 512).rearrange("p (b t) -> p b t", b=2)
        pT = c2(2 * 512).rearrange("p (b t) -> p b t", b=2)
        assert c2.at <= c.at
        fy = c(2 * 512).rearrange("p (b t) -> p b t", b=2)
        zf = c(4 * FC).rearrange("p (t c) -> p t c", t=4)
        kvq = c(4 * 416).rearrange("p (t c) -> p t c", t=4)
        ckvT = c(512)
        cqT = c(2 * 512).rearrange("p (c t) -> p c t", c=2)
        vv = c(4 * HEADS * VH).rearrange("p (t h d) -> p t h d", t=4, h=HEADS)
        aT = c(4 * 512).rearrange("p (c t) -> p c t", c=4)
        fT = c(2 * 512).rearrange("p (c t) -> p c t", c=2)
        cvT = c(2 * 512).rearrange("p (c t) -> p c t", c=2)
        kq_at = c.at
        kq = c(8 * HEADS * QKH).rearrange("p (b h d) -> p b h d", b=8, h=HEADS)
        sqb = c(HEADS * QKH).rearrange("p (h d) -> p h d", h=HEADS)
        rtmp = sgc[:, 0, 0:256]
        c2 = Carve(kq_at)
        sgm = c2(2 * 512).rearrange("p (b t) -> p b t", b=2)
        mtmp = c2(2 * 512).rearrange("p (b t) -> p b t", b=2)
        xtmp = c2(2 * D).rearrange("p (b t) -> p b t", b=2)
        assert c2.at <= c.at

        c = Carve()
        qs = c(4 * PH * P).rearrange("p (t h c) -> p t h c", t=4, h=PH)
        dg = c(TOPK * P).rearrange("p (k c) -> p k c", k=TOPK)
        vbuf = c(VB * D).rearrange("p (k d) -> p k d", k=VB)
        ubuf4 = c(4 * D).rearrange("p (k d) -> p k d", k=4)
        ub = [ubuf4[:, k, :] for k in range(4)] + [hT_b[:, k * D:(k + 1) * D] for k in range(4)]
        eid = c(P + 2 * TOPK).bitcast(U32)
        gate = c(P + 2 * TOPK)
        qfix = c(2 * P).rearrange("p (b c) -> p b c", b=2)
        kfix = c(2 * P).rearrange("p (b c) -> p b c", b=2)
        sval = c(2 * TOPK).rearrange("p (b c) -> p b c", b=2)
        sidx = c(2 * TOPK).bitcast(U32).rearrange("p (b c) -> p b c", b=2)
        sidf = c(2 * TOPK).rearrange("p (b c) -> p b c", b=2)
        s2 = c(2 * NK).rearrange("p (b c) -> p b c", b=2)
        cand = c(256).rearrange("p (b c) -> p b c", b=TOPK)
        cand2 = c(256)
        best = c(TOPK)
        pos = c(TOPK).bitcast(U32)
        posu = c(2 * TOPK).bitcast(U32).rearrange("p (b c) -> p b c", b=2)
        posf = c(2 * TOPK).rearrange("p (b c) -> p b c", b=2)
        eq = c(2 * 256).rearrange("p (b i j) -> p b i j", b=2, i=TOPK)
        eqm = c(2 * 256).rearrange("p (b i j) -> p b i j", b=2, i=TOPK)
        rr = c(2 * TOPK).rearrange("p (b c) -> p b c", b=2)
        ebase = c(TOPK)
        nbest = c(1)
        gexp, gsum, ginv = c(TOPK), c(1), c(1)
        ixf = c(2 * TOPK).bitcast(U32).rearrange("p (b c) -> p b c", b=2)
        dots = c(2 * TOPK).rearrange("p (b c) -> p b c", b=2)
        gel = c(2 * TOPK).rearrange("p (b c) -> p b c", b=2)
        actv = c(2 * TOPK).rearrange("p (b c) -> p b c", b=2)
        ytmp = c(D)
        dgrow = dg[:, :, :].rearrange("p (s k) c -> p s k c", s=2)

        c = Carve()
        lnrow = c(4 * 2 * D).rearrange("p (i g d) -> p i g d", i=4, g=2)
        borow = c(D)
        sb_at = c.at
        lpad = c(DC * (SEQ + LCONV - 1)).rearrange("p (c t) -> p c t", c=DC)
        xb = c(DC * SEQ).rearrange("p (c t) -> p c t", c=DC)
        yb = c(DC * SEQ).rearrange("p (c t) -> p c t", c=DC)
        gi = c(DC * SEQ).rearrange("p (c t) -> p c t", c=DC)
        gr = c(DC * SEQ).rearrange("p (c t) -> p c t", c=DC)
        lm = c(DC * SEQ).rearrange("p (c t) -> p c t", c=DC)
        c = Carve(sb_at)
        hpad = c(2 * 2 * (SEQ + FCONV - 1)).rearrange("p (b g t) -> p b g t", b=2, g=2)
        facc = c(2 * 2 * SEQ).rearrange("p (b g t) -> p b g t", b=2, g=2)
        fgel = c(2 * SEQ).rearrange("p (b t) -> p b t", b=2)
        fgT = c(2 * SEQ).rearrange("p (b t) -> p b t", b=2)
        c = Carve(sb_at)
        k2T = c(H2 * SEQ).rearrange("p (h t) -> p h t", h=H2)
        q2T = c(H2 * SEQ).rearrange("p (h t) -> p h t", h=H2)
        v2 = c(2 * D).rearrange("p (t d) -> p t d", t=2)
        o2T = c(H2 * SEQ).rearrange("p (h t) -> p h t", h=H2)
        zs = c(2 * SEQ).rearrange("p (b t) -> p b t", b=2)
        za = c(2 * SEQ).rearrange("p (b t) -> p b t", b=2)
        ze = c(2 * SEQ).rearrange("p (b t) -> p b t", b=2)
        zl = c(2 * SEQ).rearrange("p (b t) -> p b t", b=2)
        zsp = c(2 * SEQ).rearrange("p (b t) -> p b t", b=2)
        zcum = c(2 * SEQ).rearrange("p (b t) -> p b t", b=2)
        zarg = c(2 * SEQ).rearrange("p (b t) -> p b t", b=2)
        zw = c(2 * SEQ).rearrange("p (b t) -> p b t", b=2)
        wT = c(2 * SEQ).rearrange("p (b t) -> p b t", b=2)
        one_row = c(SEQ)

        ring = [ctx.enter_context(nc.psum_tensor(f"ring{i}", [P, 512], F32)) for i in range(RING)]
        wide = [ctx.enter_context(nc.psum_tensor(f"wide{i}", [P, 1024], F32)) for i in range(WIDE)]

        ring_full = [sem(f"ring_full{i}") for i in range(RING)]
        ring_free = [sem(f"ring_free{i}") for i in range(RING)]
        wide_full = [sem(f"wide_full{i}") for i in range(WIDE)]
        wide_free = [sem(f"wide_free{i}") for i in range(WIDE)]
        weights_in = [sem(f"weights_in{i}") for i in range(SLOTS)]
        params_in = sem("params_in")
        x_in = sem("x_in")
        rows_in = sem("rows_in")
        x_out = sem("x_out")
        cond_ready = sem("cond_ready")
        act_order = sem("act_order")
        dve_order = sem("dve_order")
        std_ready = sem("std_ready")
        xn_ready = sem("xn_ready")
        x_new = sem("x_new")
        conv_done = sem("conv_done")
        lat_sq = sem("lat_sq")
        lat_ready = sem("lat_ready")
        stat_ready = sem("stat_ready")
        heads_ready = sem("heads_ready")
        max_ready = sem("max_ready")
        p_ready = sem("p_ready")
        pv_done = sem("pv_done")
        m_ready = sem("m_ready")
        gdiag_ready = sem("gdiag_ready")
        qk_copied = [sem(f"qk_copied{i}") for i in range(2)]
        sel_full = [sem(f"sel_full{i}") for i in range(2)]
        sel_free = [sem(f"sel_free{i}") for i in range(2)]
        sel_order = sem("sel_order")
        best_ready = sem("best_ready")
        gate_exp = sem("gate_exp")
        eid_ready = sem("eid_ready")
        eid_moved = sem("eid_moved")
        idx_ready = sem("idx_ready")
        u_in = [sem(f"u_in{i}") for i in range(UB)]
        v_in = [sem(f"v_in{i}") for i in range(VB)]
        u_free = sem("u_free")
        v_free = sem("v_free")
        gelu_done = sem("gelu_done")
        act_ready = sem("act_ready")
        diag_ready = sem("diag_ready")
        sp_ready = sem("sp_ready")
        lru_y = sem("lru_y")
        lru_xb = sem("lru_xb")
        lru_h = sem("lru_h")
        lru_act = sem("lru_act")
        lru_dve = sem("lru_dve")
        ffn_pad = sem("ffn_pad")
        ffn_acc = sem("ffn_acc")
        ffn_gel = sem("ffn_gel")
        ffn_g = sem("ffn_g")
        z_exp = sem("z_exp")
        z_arg = sem("z_arg")
        z_out = sem("z_out")
        z_w = sem("z_w")
        o_done = sem("o_done")

        def filled(e, g):
            e.wait_ge(ring_full[g % RING], g // RING + 1)

        def taken(e, g):
            e.wait_ge(ring_free[g % RING], g // RING + 1)

        def wfilled(e, g):
            e.wait_ge(wide_full[g % WIDE], g // WIDE + 1)

        def wtaken(e, g):
            e.wait_ge(wide_free[g % WIDE], g // WIDE + 1)

        def bank(g):
            return ring[g % RING]

        def wbank(g):
            return wide[g % WIDE]

        def W(it):
            return wbuf[:, it.n % SLOTS, 0:it.size]

        L = pl.layers
        TILES_DONE = [0, 4]
        STD = {}
        n_std = Count()
        for l in range(LAYERS):
            for k in ("norm1", "lat", "heads", "conv", "norm2"):
                STD[k, l] = n_std.take() + 1
        for i in range(4):
            STD["ln", i] = n_std.take() + 1
        XNEW, n_x = {}, Count()
        for l in range(LAYERS):
            for k in ("out", "exp"):
                n_x.take(L[l].n)
                XNEW[k, l] = n_x.n
        for i in range(4):
            n_x.take(2)
            XNEW["ln", i] = n_x.n
        XN, n_xn = {}, Count()
        for l in range(LAYERS):
            for k in ("norm1", "norm2"):
                XN[k, l] = n_xn.take(4 if k == "norm1" else L[l].n)
        STAT, n_stat = {}, Count()
        for l in range(LAYERS):
            for k in ("heads", "conv"):
                STAT[k, l] = n_stat.take() + 1
        for i in range(4):
            STAT["ln", i] = n_stat.take() + 1
        GD = {}
        n_gd = Count()
        for l in range(LAYERS):
            for k in (1, 2):
                GD[l, k] = n_gd.take(L[l].sets)
        SELQ = [0, 4]

        MOVES = [0, L[0].n - 1]

        def head_pairs(e, t, n, body):
            last = t + 1 == n
            with e.Fori(0, PH // 2 - last) as i:
                for par in range(2):
                    body(i, par, True)
            if last:
                for par in range(2):
                    body(PH // 2 - 1, par, False)

        def heads_base(l):
            return (4 + L[0].n) * l

        def pv_wait(e, s, j):
            if (j + 1) % (2 * s.n) == 0:
                wfilled(e, s.pairs + (j + 1) // (2 * s.n) - 1)
            else:
                before = sum(x_.N - HEADS // 2 for x_ in L[:s.l])
                e.wait_ge(pv_done, before + j + 1 - (j + 1) // (2 * s.n))

        def o_wait(e, a, j):
            if j % 2:
                wfilled(e, a.o + j // 2)
            else:
                e.wait_ge(o_done, j // 2 + 1)

        block = ctx.enter_context(nc.Block())

        @block.sync
        def _(sp_e):
            sp_e.dma_start(const[:], w["const"]).then_inc(params_in, 16)
            sp_e.dma_start(cols[:], w["cols"]).then_inc(params_in, 16)
            sp_e.dma_start(hrow[:], w["hrow"].partition_broadcast(P)).then_inc(params_in, 16)
            for t in range(4):
                src = w["x"] if t < 2 else w["ctx"]
                sp_e.dma_start(x[:, t, :], src[(t % 2) * P:(t % 2 + 1) * P, :]).then_inc(x_in, 16)

            def release(it):
                kind, g = it.release
                if kind == "ring":
                    filled(sp_e, g)
                elif kind == "wide":
                    wfilled(sp_e, g)
                else:
                    for par in range(2):
                        sp_e.wait_ge(sel_full[par], 4 * (SELQ[g] + L[g].n))

            for it in pl.items:
                if it.n >= SLOTS:
                    release(pl.items[it.n - SLOTS])
                if it.kind == "lru_in" and it.i == 0:
                    sp_e.wait_ge(x_new, XNEW["exp", 1])
                    sp_e.dma_start(lnrow[:, :, :, :].rearrange("p i g d -> p (i g d)"),
                                   w["lnrow"].partition_broadcast(P)).then_inc(rows_in, 16)
                    sp_e.dma_start(borow, w["lru_b_out"].partition_broadcast(P)).then_inc(rows_in, 16)
                sp_e.dma_start(W(it), w[it.kind][it.l, it.i]).then_inc(weights_in[it.n % SLOTS], 16)
            for t in range(2):
                sp_e.wait_ge(x_new, XNEW["ln", 3] - 1 + t)
                sp_e.dma_start(out[t * P:(t + 1) * P, :], x[:, t, :]).then_inc(x_out, 16)
            sp_e.wait_ge(x_out, 32)

        @block.tensor
        def _(pe):
            mm = nc.tensor.matmul

            def claim(g):
                if g >= RING:
                    taken(pe, g - RING)

            def wclaim(g):
                if g >= WIDE:
                    wtaken(pe, g - WIDE)

            def arrived(it):
                pe.wait_ge(weights_in[it.n % SLOTS], 16 * (it.n // SLOTS + 1))

            def transpose(o, i):
                n = i.shape[0]
                return nc.tensor.transpose(o, i, K("ident")[0:n, 0:n])

            def modulation(lot):
                for it, g, l, i in lot:
                    arrived(it)
                    claim(g)
                    wt = W(it).rearrange("p (k c) -> p k c", k=DC)
                    for m in range(4):
                        for k in range(DC):
                            last = mm(bank(g)[:, 2 * m:2 * m + 2], wt[:, k, m * P:(m + 1) * P], cond[:, k, :],
                                      start=(k == 0), stop=(k == DC - 1))
                    last.then_inc(ring_full[g % RING], 1)

            def norm_transposes(g0, base, n):
                pe.wait_ge(xn_ready, base + n)
                for j in range(DC):
                    claim(g0 + j)
                    for t in range(n):
                        last = transpose(bank(g0 + j)[:, t * P:(t + 1) * P], xn[:, t, j * P:(j + 1) * P])
                    last.then_inc(ring_full[(g0 + j) % RING], 1)

            def gate_rows(gs, base, l):
                for s, g0 in enumerate(gs):
                    pe.wait_ge(gdiag_ready, base + s + 1)
                    for h in range(2):
                        claim(g0 + h)
                        mm(bank(g0 + h)[:, :], K("ones"), dgrow[:, s, 4 * h:4 * h + 4, :],
                           start=True, stop=True).then_inc(ring_full[(g0 + h) % RING], 1)

            pe.wait_ge(params_in, 48)
            pe.wait_ge(cond_ready, 2)
            for s in L:
                l, n, T = s.l, s.n, s.n * P
                modulation(s.mod_a)
                norm_transposes(s.norm1, XN["norm1", l], 4)
                for j in range(DC):
                    taken(pe, s.norm1 + j)
                arrived(s.zc)
                wt = W(s.zc).rearrange("p (k c) -> p k c", k=DC)
                for i, m in enumerate((2, 0, 3, 1)):
                    g = s.conv_in + i
                    claim(g)
                    for k in range(DC):
                        last = mm(bank(g)[:, 0:T], wt[:, k, m * P:(m + 1) * P], hT[:, k, 0:T],
                                  start=(k == 0), stop=(k == DC - 1))
                    last.then_inc(ring_full[g % RING], 1)
                for it in s.wa:
                    arrived(it)
                for t in range(4):
                    g = s.kvq + t
                    wclaim(g)
                    parts = [(0, 416, 0), (416, 672, 512)] if t < n else [(0, KVR, 0)]
                    for a, b, o in parts:
                        for k in range(DC):
                            wt = W(s.wa[k // 4])[:, (k % 4) * 672 + a:(k % 4) * 672 + b]
                            last = mm(wbank(g)[:, o:o + b - a], hT[:, k, t * P:(t + 1) * P], wt,
                                      start=(k == 0), stop=(k == DC - 1))
                    last.then_inc(wide_full[g % WIDE], 1)
                for i in range(2 * s.sets):
                    st, cc = i // 2, i % 2
                    gy, gf = s.fn_y[i], s.fn_f[i]
                    wtaken(pe, s.kvq + 2 * st)
                    wtaken(pe, s.kvq + 2 * st + 1)
                    claim(gy)
                    for tt in range(2):
                        last = mm(bank(gy)[:, :], zf[:, 2 * st + tt, cc * P:(cc + 1) * P],
                                  K("dft_t", tt * 2 * SEQ, (tt + 1) * 2 * SEQ), start=(tt == 0), stop=(tt == 1))
                    last.then_inc(ring_full[gy % RING], 1)
                    claim(gf)
                    taken(pe, gy)
                    mm(bank(gf)[:, 0:SEQ], K("dft_c"), fy[:, i % 2, 0:SEQ], start=True, stop=False)
                    mm(bank(gf)[:, 0:SEQ], K("dft_s"), fy[:, i % 2, SEQ:2 * SEQ],
                       start=False, stop=True).then_inc(ring_full[gf % RING], 1)
                pe.wait_ge(lat_ready, 4 * l + 4)
                g = s.lat_k
                claim(g)
                for t in range(4):
                    last = transpose(bank(g)[:, t * P:(t + 1) * P], kvq[:, t, 0:KVL])
                last.then_inc(ring_full[g % RING], 1)
                for cc in range(2):
                    g = s.lat_q + cc
                    claim(g)
                    for t in range(n):
                        last = transpose(bank(g)[:, t * P:(t + 1) * P], kvq[:, t, KVR + cc * P:KVR + (cc + 1) * P])
                    last.then_inc(ring_full[g % RING], 1)
                arrived(s.uk)
                taken(pe, s.lat_k)
                for t in range(4):
                    g = s.kv + t
                    wclaim(g)
                    for h in range(2):
                        last = mm(wbank(g)[:, h * 512:(h + 1) * 512], ckvT[:, t * P:(t + 1) * P],
                                  W(s.uk)[:, h * 512:(h + 1) * 512], start=True, stop=True)
                    last.then_inc(wide_full[g % WIDE], 1)
                taken(pe, s.lat_q)
                taken(pe, s.lat_q + 1)
                for t in range(n):
                    g = s.q + t
                    wclaim(g)
                    for h in range(2):
                        for cc in range(2):
                            a = 1024 + cc * 768 + h * 384
                            last = mm(wbank(g)[:, h * 512:h * 512 + 384], cqT[:, cc, t * P:(t + 1) * P],
                                      W(s.uk)[:, a:a + 384], start=(cc == 0), stop=(cc == 1))
                    last.then_inc(wide_full[g % WIDE], 1)
                pe.wait_ge(conv_done, 2 * l + 2)
                for t in range(n):
                    g = s.cv_t + t
                    claim(g)
                    for cc in range(2):
                        last = transpose(bank(g)[:, cc * P:(cc + 1) * P],
                                         cacc[:, cc, t // 2, (t % 2) * P:(t % 2 + 1) * P])
                    last.then_inc(ring_full[g % RING], 1)
                for t in range(n):
                    taken(pe, s.cv_t + t)
                for cc in range(2):
                    g = s.cv_b + cc
                    claim(g)
                    for t in range(n):
                        last = transpose(bank(g)[:, t * P:(t + 1) * P], cn[:, t, cc * P:(cc + 1) * P])
                    last.then_inc(ring_full[g % RING], 1)

                pe.wait_ge(heads_ready, heads_base(l) + 4 + n)

                def head_columns(h):
                    for g, b0, k in ((s.gk[h], 0, 4), (s.gq[h], 4, n)):
                        claim(g)
                        for t in range(k):
                            last = transpose(bank(g)[0:QKH, t * P:(t + 1) * P], kq[:, b0 + t, h, :])
                        last.then_inc(ring_full[g % RING], 1)

                head_columns(0)
                for i in range(s.N + 2):
                    if i < s.N:
                        h, t = i // n, i % n
                        if t == 0:
                            taken(pe, s.gk[h])
                            taken(pe, s.gq[h])
                        g = s.gs[i]
                        claim(g)
                        a = 0 if t < 2 else 256
                        mm(bank(g)[:, 0:512 - a], qTb[0:QKH, h % 2, t * P:(t + 1) * P], kTb[0:QKH, h % 2, a:512],
                           start=True, stop=True).then_inc(ring_full[g % RING], 1)
                        if t == 0 and h + 1 < HEADS:
                            head_columns(h + 1)
                    if 1 <= i <= s.N:
                        j = i - 1
                        g = s.gp[j]
                        pe.wait_ge(p_ready, L[0].N * l + j + 1)
                        claim(g)
                        for kc in range(4 if j % n < 2 else 2):
                            last = transpose(bank(g)[:, kc * P:(kc + 1) * P], prob[:, j % 2, kc * P:(kc + 1) * P])
                        last.then_inc(ring_full[g % RING], 1)
                    if i >= 2:
                        j = i - 2
                        h, t = j // n, j % n
                        pair = s.pairs + h // 2
                        taken(pe, s.gp[j])
                        if h % 2 == 0 and t == 0:
                            wclaim(pair)
                        nk = 4 if t < 2 else 2
                        for kc in range(nk):
                            last = mm(wbank(pair)[(h % 2) * 64:(h % 2) * 64 + 64, t * P:(t + 1) * P],
                                      vv[:, 4 - nk + kc, h, :], pT[:, j % 2, kc * P:(kc + 1) * P],
                                      start=(kc == 0), stop=(kc == nk - 1))
                        if (j + 1) % (2 * n) == 0:
                            last.then_inc(wide_full[pair % WIDE], 1)
                        else:
                            last.then_inc(pv_done, 1)
                for i in range(4):
                    wtaken(pe, s.pairs + i)
                for g in s.fn_f + [s.cv_b, s.cv_b + 1]:
                    taken(pe, g)
                for j in range(DC):
                    it, g0 = s.merge[j]
                    arrived(it)
                    wt = W(it).rearrange("p (k c) -> p k c", c=P)
                    for b, (src, k0, nk) in enumerate(((aT, 24, 4), (fT, 28, 2), (cvT, 30, 2))):
                        g = g0 + 2 * b
                        claim(g)
                        for k in range(DC):
                            last = mm(bank(g)[:, 0:T], wt[:, b * DC + k, :], hT[:, k, 0:T],
                                      start=(k == 0), stop=(k == DC - 1))
                        last.then_inc(ring_full[g % RING], 1)
                        claim(g + 1)
                        for k in range(nk):
                            last = mm(bank(g + 1)[:, 0:T], wt[:, k0 + k, :], src[:, k, 0:T],
                                      start=(k == 0), stop=(k == nk - 1))
                        last.then_inc(ring_full[(g + 1) % RING], 1)
                    modulation(s.mods[j])
                gate_rows(s.grow1, GD[l, 1], l)
                pe.wait_ge(m_ready, DC * (l + 1))
                for it in s.wo:
                    arrived(it)

                def rows_out(its, g, src, t):
                    wclaim(g)
                    for h in range(2):
                        for k in range(DC):
                            a = (k % 4) * D + h * 512
                            last = mm(wbank(g)[:, h * 512:(h + 1) * 512], src[:, k, t * P:(t + 1) * P],
                                      W(its[k // 4])[:, a:a + 512], start=(k == 0), stop=(k == DC - 1))
                    last.then_inc(wide_full[g % WIDE], 1)

                for t in range(n):
                    rows_out(s.wo, s.out + t, mT, t)
                norm_transposes(s.norm2, XN["norm2", l], n)
                for j in range(DC):
                    taken(pe, s.norm2 + j)
                for t in range(n):
                    for h in range(2):
                        g = s.back + 2 * t + h
                        claim(g)
                        for j in range(4):
                            last = transpose(bank(g)[:, j * P:(j + 1) * P], hT[:, 4 * h + j, t * P:(t + 1) * P])
                        last.then_inc(ring_full[g % RING], 1)
                gate_rows(s.grow2, GD[l, 2], l)
                for h in range(PH):
                    g = s.query + h
                    if h % 4 == 0:
                        arrived(s.wq[h // 4])
                    wt = W(s.wq[h // 4]).rearrange("p (k c) -> p k c", k=DC)
                    claim(g)
                    for k in range(DC):
                        last = mm(bank(g)[:, 0:T], wt[:, k, (h % 4) * P:(h % 4 + 1) * P], hT[:, k, 0:T],
                                  start=(k == 0), stop=(k == DC - 1))
                    last.then_inc(ring_full[g % RING], 1)

                for b in range(RING):
                    taken(pe, s.query + PH - RING + b)

                def scores(par, it):
                    pe.wait_ge(qk_copied[par], it + 1)
                    pe.wait_ge(sel_free[par], it + 1)
                    mm(ring[2 * par][:, 0:NK], qfix[0:64, par, :], kfix[0:64, par, :], start=True, stop=True)
                    mm(ring[2 * par + 1][:, 0:NK], qfix[64:128, par, :], kfix[64:128, par, :],
                       start=True, stop=True).then_inc(sel_full[par], 1)

                q0 = SELQ[l]
                for par in range(2):
                    scores(par, 4 * q0)
                for t in range(n):
                    g = s.exp + t
                    wclaim(g)
                    for h in range(2):
                        mm(wbank(g)[:, h * 512:(h + 1) * 512], K("zeros"), const[:, 0:512],
                           start=True, stop=False)

                    def weigh(i, par, nxt):
                        if nxt:
                            scores(par, i + (4 * (q0 + t) + 1))
                        pick0 = 128 * (q0 + t) + 16 * par
                        for k in range(TOPK):
                            pe.wait_ge(diag_ready, i * 32 + (pick0 + k + 1))
                            pe.wait_ge(v_in[k % VB], i * (32 * 16 // VB) + 16 * ((pick0 + k) // VB + 1))
                            for h in range(2):
                                last = mm(wbank(g)[:, h * 512:(h + 1) * 512], dg[:, k, :],
                                          vbuf[:, k % VB, h * 512:(h + 1) * 512], start=False, stop=False,
                                          skip_group_check=True)
                            last.then_inc(v_free, 1)

                    head_pairs(pe, t, n, weigh)
                    for h in range(2):
                        last = mm(wbank(g)[:, h * 512:(h + 1) * 512], K("zeros"), const[:, 0:512],
                                  start=False, stop=True)
                    last.then_inc(wide_full[g % WIDE], 1)
                for par in range(2):
                    pe.wait_ge(sel_free[par], 4 * (q0 + n) + 1)

            def x_columns(g0, have):
                pe.wait_ge(x_new, have)
                for jj in range(DC // 2):
                    g = g0 + jj
                    claim(g)
                    for b in range(4):
                        last = transpose(bank(g)[:, b * P:(b + 1) * P],
                                         x[:, b % 2, (2 * jj + b // 2) * P:(2 * jj + b // 2 + 1) * P])
                    last.then_inc(ring_full[g % RING], 1)
                for jj in range(DC // 2):
                    taken(pe, g0 + jj)

            def columns(its, g0, per):
                for i, it in enumerate(its):
                    arrived(it)
                    wt = W(it).rearrange("p (k c) -> p k c", k=DC)
                    for gg in range(2):
                        g = g0 + 2 * i + gg
                        claim(g)
                        for m in range(2):
                            for k in range(DC):
                                last = mm(bank(g)[:, m * SEQ:(m + 1) * SEQ],
                                          wt[:, k, (2 * gg + m) * P:(2 * gg + m + 1) * P], xT[:, k, :],
                                          start=(k == 0), stop=(k == DC - 1))
                        last.then_inc(ring_full[g % RING], 1)

            def rows(its, g0, src):
                for it in its:
                    arrived(it)
                for t in range(2):
                    rows_out(its, g0 + t, src, t)

            r = pl.lru
            x_columns(r.xt, XNEW["exp", 1])
            columns(r.w, r.proj, 0)
            arrived(r.wg)
            for h in range(DC):
                g = r.gates + h
                claim(g)
                pe.wait_ge(lru_xb, h + 1)
                for m in range(2):
                    last = mm(bank(g)[:, m * SEQ:(m + 1) * SEQ], W(r.wg)[:, (2 * h + m) * P:(2 * h + m + 1) * P],
                              xb[:, h, :], start=True, stop=True)
                last.then_inc(ring_full[g % RING], 1)
            pe.wait_ge(lru_h, DC)
            rows(r.wo, r.out, xb)

            def ffn(f, have):
                x_columns(f.xt, have)
                for j in range(FJ + 1):
                    if j < FJ:
                        it, g = f.items[j], f.up[j]
                        arrived(it)
                        claim(g)
                        for m in range(2):
                            for k in range(DC):
                                last = mm(bank(g)[:, m * SEQ:(m + 1) * SEQ],
                                          W(it)[:, (m * DC + k) * P:(m * DC + k + 1) * P], xT[:, k, :],
                                          start=(k == 0), stop=(k == DC - 1))
                        last.then_inc(ring_full[g % RING], 1)
                    if j == 0:
                        for t in range(2):
                            wclaim(f.down + t)
                    if j >= 1:
                        i = j - 1
                        pe.wait_ge(ffn_g, FJ * f.l + i + 1)
                        for t in range(2):
                            for h in range(2):
                                last = mm(wbank(f.down + t)[:, h * 512:(h + 1) * 512],
                                          fgT[:, i % 2, t * P:(t + 1) * P],
                                          W(f.items[i])[:, 2048 + h * 512:2048 + (h + 1) * 512],
                                          start=(i == 0), stop=(i == FJ - 1), skip_group_check=True)
                            if i == FJ - 1:
                                last.then_inc(wide_full[(f.down + t) % WIDE], 1)

            ffn(pl.ffn[0], XNEW["ln", 0])
            a = pl.stick
            x_columns(a.xt, XNEW["ln", 1])
            columns(a.wk, a.k, 0)
            columns(a.wq, a.q, 0)
            rows(a.wv, a.v, xT)
            for g in range(4):
                taken(pe, a.k + g)
                taken(pe, a.q + g)
            wtaken(pe, a.v)
            wtaken(pe, a.v + 1)
            N = 2 * H2
            for i in range(N + 3):
                if i < N:
                    h, t = i // 2, i % 2
                    g = a.gz[i]
                    claim(g)
                    mm(bank(g)[:, 0:(t + 1) * P], q2T[:, h, t * P:(t + 1) * P], k2T[:, h, 0:(t + 1) * P],
                       start=True, stop=True).then_inc(ring_full[g % RING], 1)
                if 2 <= i < N + 2:
                    j = i - 2
                    g = a.gw[j]
                    pe.wait_ge(z_w, j + 1)
                    claim(g)
                    for kc in range(j % 2 + 1):
                        last = transpose(bank(g)[:, kc * P:(kc + 1) * P], zw[:, j % 2, kc * P:(kc + 1) * P])
                    last.then_inc(ring_full[g % RING], 1)
                if i >= 3:
                    j = i - 3
                    h, t = j // 2, j % 2
                    go = a.o + h
                    taken(pe, a.gw[j])
                    if t == 0:
                        wclaim(go)
                    for kc in range(t + 1):
                        last = mm(wbank(go)[:, t * P:(t + 1) * P], v2[:, kc, h * P:(h + 1) * P],
                                  wT[:, j % 2, kc * P:(kc + 1) * P], start=(kc == 0), stop=(kc == t))
                    last.then_inc(*((wide_full[go % WIDE], 1) if t else (o_done, 1)))
            for h in range(H2):
                wtaken(pe, a.o + h)
            rows(a.wo, a.out, o2T)
            ffn(pl.ffn[1], XNEW["ln", 2])

        @block.scalar
        def _(act):
            A = nc.scalar.activation
            order = Count()

            def did(ins):
                ins.then_inc(act_order, 1)
                return order.take() + 1

            def need(v):
                act.wait_ge(act_order, v)

            act.wait_ge(params_in, 48)
            for s_ in range(2):
                A(cond[:, :, s_], C("c", s_ * DC, DC), ACT.Silu).then_inc(cond_ready, 1)
            v = did(A(sp[:, 0:8], C("lru_a_param", 0, 8), ACT.Abs))
            need(v)
            A(sp[:, 8:16], sp[:, 0:8], ACT.Exp, scale=-1.0).then_inc(sp_ready, 1)
            act.wait_ge(sp_ready, 2)
            A(sp[:, 24:32], sp[:, 16:24], ACT.Ln).then_inc(sp_ready, 1)

            def norm(tiles, l, which):
                last = 0
                for t in range(tiles):
                    last = did(A(xn[:, t, :], x[:, t, :], ACT.Square, accum_out=ss[:, t:t + 1]))
                need(last)
                A(ss[:, 4:4 + tiles], ss[:, 0:tiles], ACT.Sqrt, scale=1.0 / D, bias=K("eps")).then_inc(std_ready, 1)

            def gate_rows(gs):
                for s_, g0 in enumerate(gs):
                    for h in range(2):
                        filled(act, g0 + h)
                        A(grow[:, s_, h * 512:(h + 1) * 512], bank(g0 + h)[:, :], ACT.Copy)\
                            .then_inc(ring_free[(g0 + h) % RING], 1)

            act.wait_ge(x_in, 64)
            for s in L:
                l, n, T = s.l, s.n, s.n * P
                if l == 1:
                    act.wait_ge(x_new, XNEW["exp", 0])
                norm(4, l, "norm1")
                for i in (0, 2):
                    g = s.conv_in + i
                    filled(act, g)
                    A(sgc[:, i // 2, 0:T], bank(g)[:, 0:T], ACT.Sigmoid).then_inc(ring_free[g % RING], 1)
                last = 0
                for t in range(4):
                    g = s.kvq + t
                    wfilled(act, g)
                    if t < n:
                        A(kvq[:, t, :], wbank(g)[:, 0:416], ACT.Copy)
                        A(zf[:, t, :], wbank(g)[:, 512:768], ACT.Copy).then_inc(wide_free[g % WIDE], 1)
                    else:
                        A(kvq[:, t, 0:KVR], wbank(g)[:, 0:KVR], ACT.Copy).then_inc(wide_free[g % WIDE], 1)
                    wtaken(act, g)
                    need(last) if last else None
                    last = did(A(fy[:, 0, 0:KVL], kvq[:, t, 0:KVL], ACT.Square, accum_out=lss[:, t:t + 1]))
                    if t < n:
                        need(last)
                        last = did(A(fy[:, 0, 0:QL], kvq[:, t, KVR:416], ACT.Square, accum_out=lss[:, 4 + t:5 + t]))
                need(last)
                A(lr[:, 0:4], lss[:, 0:4], ACT.Sqrt, scale=1.0 / KVL, bias=K("eps"))
                A(lr[:, 4:4 + n], lss[:, 4:4 + n], ACT.Sqrt, scale=1.0 / QL, bias=K("eps")).then_inc(std_ready, 1)
                for i in range(2 * s.sets):
                    g = s.fn_y[i]
                    filled(act, g)
                    if i >= 2:
                        filled(act, s.fn_f[i - 2])
                    A(fy[:, i % 2, :], bank(g)[:, :], ACT.Copy).then_inc(ring_free[g % RING], 1)
                for t in range(4):
                    g = s.kv + t
                    wfilled(act, g)
                    src = wbank(g)[:, :].rearrange("p (h d) -> p h d", h=HEADS)
                    A(vv[:, t, :, :], src[:, :, NOPE:P], ACT.Copy)
                    A(kq[:, t, :, 0:NOPE], src[:, :, 0:NOPE], ACT.Copy).then_inc(wide_free[g % WIDE], 1)
                for t in range(n):
                    g = s.q + t
                    wfilled(act, g)
                    A(kq[:, 4 + t, :, :].rearrange("p (a h) d -> p a (h d)", a=2),
                      wbank(g)[:, :].rearrange("p (a c) -> p a c", a=2)[:, :, 0:384], ACT.Copy)\
                        .then_inc(wide_free[g % WIDE], 1)
                act.wait_ge(stat_ready, STAT["heads", l])
                A(hss[:, 0:32 + 8 * n], hss[:, 0:32 + 8 * n], ACT.Sqrt, scale=1.0 / QKH, bias=K("eps"))\
                    .then_inc(std_ready, 1)
                act.wait_ge(stat_ready, STAT["conv", l])
                A(cr[:, 0:n], cmv3[:, 0:n, 1], ACT.Sqrt, bias=K("eps")).then_inc(std_ready, 1)
                for cc in range(2):
                    g = s.cv_b + cc
                    filled(act, g)
                    A(cvT[:, cc, 0:T], bank(g)[:, 0:T], ACT.Silu, scale=C("g_cln", 2 * l + cc),
                      bias=C("b_cln", 2 * l + cc)).then_inc(ring_free[g % RING], 1)
                for i in range(s.N + 3):
                    if i < s.N:
                        t = i % n
                        g = s.gs[i]
                        kk = 512 if t < 2 else 256
                        filled(act, g)
                        act.wait_ge(max_ready, L[0].N * l + i + 1)
                        if i >= 2:
                            filled(act, s.gp[i - 2])
                        A(prob[:, i % 2, 0:kk], bank(g)[:, 0:kk], ACT.Exp, scale=ATT_SCALE,
                          bias=nms[:, i % 4:i % 4 + 1], accum_out=rsum[:, i % 4:i % 4 + 1])\
                            .then_inc(ring_free[g % RING], 1)
                    if 1 <= i <= s.N:
                        j = i - 1
                        g = s.gp[j]
                        kk = 512 if j % n < 2 else 256
                        filled(act, g)
                        if j >= 2:
                            pv_wait(act, s, j - 2)
                        A(pT[:, j % 2, 0:kk], bank(g)[:, 0:kk], ACT.Copy).then_inc(ring_free[g % RING], 1)
                    if i >= 3 and (i - 2) % (2 * n) == 0:
                        p_ = (i - 2) // (2 * n) - 1
                        g = s.pairs + p_
                        wfilled(act, g)
                        A(aT[:, p_, 0:T], wbank(g)[:, 0:T], ACT.Copy).then_inc(wide_free[g % WIDE], 1)
                for j in range(DC):
                    for b in range(BRANCH):
                        g = s.merge[j][1] + 2 * b
                        k = BRANCH * j + b
                        filled(act, g)
                        if k >= 2:
                            kk = k - 2
                            taken(act, s.merge[kk // BRANCH][1] + 2 * (kk % BRANCH) + 1)
                        A(sgm[:, k % 2, 0:T], bank(g)[:, 0:T], ACT.Sigmoid).then_inc(ring_free[g % RING], 1)
                gate_rows(s.grow1)
                act.wait_ge(x_new, XNEW["out", l])
                norm(n, l, "norm2")
                for t in range(n):
                    for h in range(2):
                        g = s.back + 2 * t + h
                        filled(act, g)
                        A(xn[:, t, h * 512:(h + 1) * 512], bank(g)[:, :], ACT.Copy).then_inc(ring_free[g % RING], 1)
                gate_rows(s.grow2)
                for h in range(PH):
                    g = s.query + h
                    filled(act, g)
                    A(qs[:, 0:n, h, :], bank(g)[:, 0:T].rearrange("p (t c) -> p t c", t=n), ACT.Copy)\
                        .then_inc(ring_free[g % RING], 1)

                taken(act, s.query + PH - 1)
                act.wait_ge(weights_in[s.sk.n % SLOTS], 16 * (s.sk.n // SLOTS + 1))
                qflat = qs[:, :, :, :].rearrange("p t h c -> p (t h c)")
                keys = W(s.sk)

                def select_in(par, i, t, skip, it):
                    act.wait_ge(sel_free[par], it + 1)
                    A(qfix[:, par, :], qflat[:, bass.ds(i * (2 * P) + (t * PH + skip + par) * P, P)], ACT.Copy)
                    A(kfix[:, par, :], keys[:, bass.ds(i * (2 * P) + (skip + par) * P, P)], ACT.Copy)\
                        .then_inc(qk_copied[par], 1)

                def select_gate(i, head):
                    act.wait_ge(best_ready, i * 2 + (head + 1))
                    A(gexp, best, ACT.Exp, bias=nbest, accum_out=gsum).then_inc(gate_exp, 1)

                q0 = SELQ[l]
                for par in range(2):
                    select_in(par, 0, 0, 0, 4 * q0)
                    select_gate(0, 8 * q0 + par)
                for t in range(n):
                    def weights(i, par, nxt):
                        head = 8 * (q0 + t) + par
                        if nxt:
                            select_in(par, i, t, 2, i + (4 * (q0 + t) + 1))
                        act.wait_ge(u_free, i * 32 + (UB + 16 * (head + 1)))
                        A(gel[:, par, :], dots[:, par, :], ACT.Gelu_apprx_tanh).then_inc(gelu_done, 1)
                        act.wait_ge(act_ready, i * 2 + (head + 1))
                        act.wait_ge(v_free, i * 32 + (VB + 16 * head))
                        for k in range(TOPK):
                            A(dg[:, k, :], K("ident"), ACT.Copy, scale=actv[:, par, k:k + 1])\
                                .then_inc(diag_ready, 1)
                        if nxt:
                            select_gate(i, head + 2)

                    head_pairs(act, t, n, weights)

            def x_columns(g0):
                for jj in range(DC // 2):
                    g = g0 + jj
                    filled(act, g)
                    A(hT_b[:, jj * 512:(jj + 1) * 512], bank(g)[:, :], ACT.Copy).then_inc(ring_free[g % RING], 1)

            r = pl.lru
            x_columns(r.xt)
            act.wait_ge(x_new, XNEW["exp", 1])
            for i in range(8):
                g = r.proj + i
                filled(act, g)
                for m in range(2):
                    cidx = 2 * i + m
                    src = bank(g)[:, m * SEQ:(m + 1) * SEQ]
                    if cidx < DC:
                        ins = A(lpad[:, cidx, LCONV - 1:LCONV - 1 + SEQ], src, ACT.Identity,
                                bias=C("lru_b_in", DC + cidx))
                    else:
                        ins = A(yb[:, cidx - DC, :], src, ACT.Gelu_apprx_tanh, bias=C("lru_b_in", cidx - DC))
                ins.then_inc(ring_free[g % RING], 1)
            for h in range(DC):
                g = r.gates + h
                filled(act, g)
                A(gi[:, h, :], bank(g)[:, 0:SEQ], ACT.Sigmoid, bias=C("lru_b_gates", 2 * h))
                A(gr[:, h, :], bank(g)[:, SEQ:2 * SEQ], ACT.Sigmoid, bias=C("lru_b_gates", 2 * h + 1))\
                    .then_inc(ring_free[g % RING], 1)
            taken(act, r.gates + DC - 1)
            act.wait_ge(sp_ready, 4)
            for h in range(DC):
                v = did(A(lm[:, h, :], gr[:, h, :], ACT.Exp, scale=sp[:, 40 + h:41 + h]))
                need(v)
                A(gr[:, h, :], gr[:, h, :], ACT.Exp, scale=sp[:, 32 + h:33 + h]).then_inc(lru_act, 1)
            act.wait_ge(lru_dve, 1)
            A(lm[:, :, :], lm[:, :, :], ACT.Sqrt).then_inc(lru_act, 1)

            def layer_norm(i):
                act.wait_ge(stat_ready, STAT["ln", i])
                A(lrs[:, :], lmv3[:, :, 1], ACT.Sqrt, bias=K("ln_eps")).then_inc(std_ready, 1)

            def ffn(f):
                x_columns(f.xt)
                for j in range(FJ):
                    g = f.up[j]
                    filled(act, g)
                    if j == 0:
                        act.wait_ge(ffn_pad, f.l + 1)
                    if j >= 2:
                        act.wait_ge(ffn_acc, 2 * (FJ * f.l + j - 1))
                    A(hpad[:, j % 2, :, FCONV - 1:FCONV - 1 + SEQ],
                      bank(g)[:, :].rearrange("p (g t) -> p g t", g=2), ACT.Copy).then_inc(ring_free[g % RING], 1)
                    if j >= 1:
                        gelu_step(f, j - 1)
                gelu_step(f, FJ - 1)

            def gelu_step(f, j):
                act.wait_ge(ffn_acc, 2 * (FJ * f.l + j) + 1)
                if j >= 2:
                    act.wait_ge(ffn_g, FJ * f.l + j - 1)
                A(fgel[:, j % 2, :], facc[:, j % 2, 0, :], ACT.Gelu_apprx_tanh).then_inc(ffn_gel, 1)

            layer_norm(0)
            ffn(pl.ffn[0])
            layer_norm(1)
            a = pl.stick
            x_columns(a.xt)
            for dst, g0 in ((k2T, a.k), (q2T, a.q)):
                for i in range(4):
                    g = g0 + i
                    filled(act, g)
                    A(dst[:, 2 * i:2 * i + 2, :], bank(g)[:, :].rearrange("p (h t) -> p h t", h=2), ACT.Copy)\
                        .then_inc(ring_free[g % RING], 1)
            for t in range(2):
                g = a.v + t
                wfilled(act, g)
                A(v2[:, t, :], wbank(g)[:, :], ACT.Copy).then_inc(wide_free[g % WIDE], 1)
            N = 2 * H2
            for i in range(N + 4):
                if i < N:
                    b, kk = i % 2, (i % 2 + 1) * P
                    g = a.gz[i]
                    filled(act, g)
                    if i >= 2:
                        act.wait_ge(z_arg, i - 1)
                    A(zs[:, b, 0:kk], bank(g)[:, 0:kk], ACT.Copy, scale=STICK_SCALE)
                    v = did(A(za[:, b, 0:kk], bank(g)[:, 0:kk], ACT.Abs, scale=STICK_SCALE))
                    need(v)
                    v = did(A(ze[:, b, 0:kk], za[:, b, 0:kk], ACT.Exp, scale=-1.0))
                    need(v)
                    A(zl[:, b, 0:kk], ze[:, b, 0:kk], ACT.Ln, bias=1.0).then_inc(ring_free[g % RING], 1)
                if 1 <= i <= N:
                    j = i - 1
                    b, kk = j % 2, (j % 2 + 1) * P
                    act.wait_ge(z_arg, j + 1)
                    if j >= 2:
                        filled(act, a.gw[j - 2])
                    A(zw[:, b, 0:kk], zarg[:, b, 0:kk], ACT.Exp).then_inc(z_out, 1)
                if 3 <= i <= N + 2:
                    j = i - 3
                    g = a.gw[j]
                    b, kk = j % 2, (j % 2 + 1) * P
                    filled(act, g)
                    if j >= 2:
                        o_wait(act, a, j - 2)
                    A(wT[:, b, 0:kk], bank(g)[:, 0:kk], ACT.Copy).then_inc(ring_free[g % RING], 1)
                if i >= 4 and i % 2 == 1:
                    h = (i - 4) // 2
                    g = a.o + h
                    wfilled(act, g)
                    A(o2T[:, h, :], wbank(g)[:, 0:SEQ], ACT.Copy).then_inc(wide_free[g % WIDE], 1)
            layer_norm(2)
            ffn(pl.ffn[1])
            layer_norm(3)

        @block.gpsimd
        def _(pool):
            pool.sem_inc(u_free, UB)
            pool.sem_inc(v_free, VB)
            for par in range(2):
                pool.sem_inc(sel_free[par], 1)
            for s in L:
                for t in range(s.n):
                    q = SELQ[s.l] + t
                    if t >= 1:
                        pool.wait_ge(eid_moved, MOVES[s.l] + t)
                    with pool.Fori(0, 4) as i:
                        for par in range(2):
                            pool.wait_ge(eid_ready, i * 2 + (8 * q + par + 1))
                            pool.nop(nofuse=True)
                            nc.gpsimd.tensor_copy(ixf[:, par, :], eid[:, bass.ds(i * 32 + par * 16, TOPK)])\
                                .then_inc(idx_ready, 1)
                            pool.wait_ge(idx_ready, i * 2 + (8 * q + par + 1))
                            pool.nop(nofuse=True)
                            pick0 = 128 * q + 16 * par
                            for buf, tab, free, arrive, nb in ((ub, w["u_tab"], u_free, u_in, UB),
                                                               (None, w["v_tab"], v_free, v_in, VB)):
                                for k in range(TOPK):
                                    pool.wait_ge(free, i * 32 + (pick0 + k + 1))
                                    pool.nop(nofuse=True)
                                    dst = buf[k % nb] if buf is not None else vbuf[:, k % nb, :]
                                    nc.gpsimd.indirect_dma_start(
                                        dst, None, tab, bass.IndirectOffsetOnAxis(ap=ixf[:, par, k:k + 1], axis=0))\
                                        .then_inc(arrive[k % nb], 16)

        @block.vector
        def _(dve):
            V = nc.vector
            order = Count()

            def did(ins):
                ins.then_inc(dve_order, 1)
                return order.take() + 1

            def need(v):
                dve.wait_ge(dve_order, v)

            def bc(ap, axis, shape):
                return ap.unsqueeze(axis).to_broadcast(shape)

            dve.wait_ge(params_in, 48)
            dve.wait_ge(sp_ready, 1)
            V.tensor_scalar(sp[:, 16:24], sp[:, 8:16], 1.0, None, ALU.add).then_inc(sp_ready, 1)
            dve.wait_ge(sp_ready, 3)
            v = did(V.tensor_scalar(sp[:, 32:40], sp[:, 16:24], 1.0, None, ALU.subtract))
            need(v)
            v = did(V.tensor_tensor(sp[:, 32:40], sp[:, 8:16], sp[:, 32:40], ALU.subtract))
            need(v)
            v = did(V.reciprocal(sp[:, 40:48], sp[:, 16:24]))
            need(v)
            v = did(V.tensor_tensor(sp[:, 32:40], sp[:, 32:40], sp[:, 40:48], ALU.mult))
            need(v)
            v = did(V.tensor_tensor(sp[:, 24:32], sp[:, 24:32], sp[:, 32:40], ALU.add))
            need(v)
            v = did(V.tensor_scalar(sp[:, 0:8], C("lru_a_param", 0, 8), -1.0, 0.0, ALU.mult, ALU.max))
            need(v)
            v = did(V.tensor_tensor(sp[:, 24:32], sp[:, 24:32], sp[:, 0:8], ALU.add))
            need(v)
            V.tensor_scalar(sp[:, 32:40], sp[:, 24:32], -LRU_C, None, ALU.mult)
            V.tensor_scalar(sp[:, 40:48], sp[:, 24:32], -2.0 * LRU_C, None, ALU.mult).then_inc(sp_ready, 1)

            def modulation(lot):
                for it, g, l, i in lot:
                    filled(dve, g)
                    b = C("b_mod", (l * 12 + i) * 4, 4)
                    V.tensor_tensor(mod[:, l, 4 * i:4 * i + 4, :], bank(g)[:, 0:8].rearrange("p (m s) -> p m s", m=4),
                                    bc(b, 2, [P, 4, 2]), ALU.add).then_inc(ring_free[g % RING], 1)
                    taken(dve, g)

            def scales(l, which):
                gname = ("g_norm1", "g_norm2")[which]
                sc = 3 * which + 1
                return did(V.scalar_tensor_tensor(
                    amod[:, l, which, :, :], mod[:, l, sc * DC:(sc + 1) * DC, :], 1.0,
                    bc(C(gname, l * DC, DC), 2, [P, DC, 2]), ALU.add, ALU.mult))

            def norm(g0, tiles, l, which):
                dve.wait_ge(std_ready, STD[("norm1", "norm2")[which], l])
                v = did(V.reciprocal(rstd[:, 0:tiles], ss[:, 4:4 + tiles]))
                need(v)
                for t in range(tiles):
                    V.tensor_scalar(xn[:, t, :], x[:, t, :], rstd[:, t:t + 1], None, ALU.mult)\
                        .then_inc(xn_ready, 1)
                for j in range(DC):
                    g = g0 + j
                    filled(dve, g)
                    for st in range(tiles // 2):
                        ins = V.tensor_scalar(
                            hT[:, j, st * SEQ:(st + 1) * SEQ], bank(g)[:, st * SEQ:(st + 1) * SEQ],
                            amod[:, l, which, j, st:st + 1],
                            mod[:, l, 3 * which * DC + j, st:st + 1], ALU.mult, ALU.add)
                    ins.then_inc(ring_free[g % RING], 1)

            def gate_rows(vec, l, sets, gs):
                for st in range(sets):
                    V.tensor_tensor(dgrow[:, st, :, :], bc(K("ident"), 1, [P, DC, P]),
                                    bc(mod[:, l, vec * DC:(vec + 1) * DC, st], 2, [P, DC, P]), ALU.mult)\
                        .then_inc(gdiag_ready, 1)

            def add_to_x(g, t, buf):
                wfilled(dve, g)
                V.tensor_tensor(buf, wbank(g)[:, :], grow[:, t // 2, :], ALU.mult)\
                    .then_inc(wide_free[g % WIDE], 1)
                wtaken(dve, g)
                V.tensor_tensor(x[:, t, :], x[:, t, :], buf, ALU.add).then_inc(x_new, 1)

            sel_n = [0]

            for s in L:
                l, n, T = s.l, s.n, s.n * P
                v = did(V.memset(upad[:, :, :, :].rearrange("p c s t -> p (c s t)"), 0.0))
                modulation(s.mod_a)
                v = scales(l, 0)
                need(v)
                norm(s.norm1, 4, l, 0)
                for cc in range(2):
                    taken(dve, s.conv_in + 2 * cc)
                    g = s.conv_in + 2 * cc + 1
                    filled(dve, g)
                    V.tensor_tensor(upad[:, cc, 0:s.sets, PAD:PAD + SEQ],
                                    bank(g)[:, 0:T].rearrange("p (s t) -> p s t", t=SEQ),
                                    sgc[:, cc, 0:T].rearrange("p (s t) -> p s t", t=SEQ), ALU.mult)\
                        .then_inc(ring_free[g % RING], 1)
                v = [0, 0]
                for k in range(TAPS):
                    for cc in range(2):
                        wc = C("w_dw", (l * 2 + cc) * TAPS + k)
                        src, dst = upad[:, cc, 0:s.sets, k:k + SEQ], cacc[:, cc, 0:s.sets, :]
                        if k == 0:
                            taken(dve, s.conv_in + 2 * cc + 1)
                            v[cc] = did(V.tensor_scalar(dst, src, wc, C("b_dw", 2 * l + cc), ALU.mult, ALU.add))
                        else:
                            need(v[cc])
                            ins = V.scalar_tensor_tensor(dst, src, wc, dst, ALU.mult, ALU.add)
                            if k == TAPS - 1:
                                ins.then_inc(conv_done, 1)
                            else:
                                v[cc] = did(ins)
                dve.wait_ge(std_ready, STD["lat", l])
                v = did(V.reciprocal(lr[:, 0:4 + n], lr[:, 0:4 + n]))
                need(v)
                for t in range(4):
                    ins = V.tensor_scalar(kvq[:, t, 0:KVL], kvq[:, t, 0:KVL], lr[:, t:t + 1], None, ALU.mult)
                    if t < n:
                        ins = V.tensor_scalar(kvq[:, t, KVR:416], kvq[:, t, KVR:416], lr[:, 4 + t:5 + t], None,
                                              ALU.mult)
                    ins.then_inc(lat_ready, 1)
                for i in range(2 * s.sets):
                    g = s.fn_f[i]
                    filled(dve, g)
                    V.tensor_copy(fT[:, i % 2, (i // 2) * SEQ:(i // 2 + 1) * SEQ], bank(g)[:, 0:SEQ])\
                        .then_inc(ring_free[g % RING], 1)
                g = s.lat_k
                filled(dve, g)
                V.tensor_scalar(ckvT, bank(g)[:, :], C("g_ckv", l), None, ALU.mult).then_inc(ring_free[g % RING], 1)
                for cc in range(2):
                    g = s.lat_q + cc
                    filled(dve, g)
                    V.tensor_scalar(cqT[:, cc, 0:T], bank(g)[:, 0:T], C("g_cq", 2 * l + cc), None, ALU.mult)\
                        .then_inc(ring_free[g % RING], 1)
                bufs = list(range(4)) + list(range(4, 4 + n))
                v = 0
                for b in bufs:
                    wtaken(dve, s.kv + b if b < 4 else s.q + b - 4)
                    if b < 4:
                        u = did(V.tensor_copy(kq[:, b, :, NOPE:QKH],
                                              bc(kvq[:, b, KVL:KVR], 1, [P, HEADS, ROPE])))
                        need(u)
                    elif v:
                        need(v)
                    u = did(V.tensor_tensor(sqb, kq[:, b, :, :], kq[:, b, :, :], ALU.mult))
                    need(u)
                    v = did(V.tensor_reduce(hss[:, 8 * b:8 * b + 8], sqb, AX_X, ALU.add))
                need(v)
                dve.nop().then_inc(stat_ready, 1)
                for t in range(n):
                    filled(dve, s.cv_t + t)
                    v = did(V.bn_stats(cst[:, 6 * t:6 * t + 6], bank(s.cv_t + t)[:, 0:CC]))
                need(v)
                for t in range(n):
                    ins = V.bn_aggr(cmv3[:, t, :], cst[:, 6 * t:6 * t + 6])
                ins.then_inc(stat_ready, 1)
                dve.wait_ge(std_ready, STD["heads", l])
                v = did(V.reciprocal(hr[:, 0:32 + 8 * n], hss[:, 0:32 + 8 * n]))
                dve.wait_ge(std_ready, STD["conv", l])
                u = did(V.reciprocal(cr[:, 0:n], cr[:, 0:n]))
                need(u)
                for t in range(n):
                    g = s.cv_t + t
                    V.tensor_scalar(cn[:, t, :], bank(g)[:, 0:CC], cmv3[:, t, 0:1], cr[:, t:t + 1],
                                    ALU.subtract, ALU.mult).then_inc(ring_free[g % RING], 1)
                for b in bufs:
                    buf = kq[:, b, :, :]
                    v = did(V.tensor_tensor(buf, buf, bc(hr[:, 8 * b:8 * b + 8], 2, [P, HEADS, QKH]), ALU.mult))
                    need(v)
                    gi0 = (2 * l + (0 if b >= 4 else 1)) * QKH
                    ins = V.tensor_tensor(buf, buf, bc(hrow[:, gi0:gi0 + QKH], 1, [P, HEADS, QKH]), ALU.mult)
                    tt = b % 4
                    if tt >= 2:
                        ins.then_inc(heads_ready, 1)
                        continue
                    v = did(ins)
                    need(v)
                    z = buf[:, :, NOPE:QKH].rearrange("p h (a b c) -> p h a b c", a=2, b=2)
                    sn = K("sin", tt * ROPE, (tt + 1) * ROPE).rearrange("p (a b c) -> p a b c", a=2, b=2)
                    tv = rtmp.rearrange("p (h a b c) -> p h a b c", h=HEADS, a=2, b=2)
                    for o in range(2):
                        v = did(V.tensor_tensor(tv[:, :, :, o, :], z[:, :, :, 1 - o, :],
                                                bc(sn[:, :, o, :], 1, [P, HEADS, 2, 8]), ALU.mult))
                    need(v)
                    v = did(V.tensor_tensor(buf[:, :, NOPE:QKH], buf[:, :, NOPE:QKH],
                                            bc(K("cos", tt * ROPE, (tt + 1) * ROPE), 1, [P, HEADS, ROPE]), ALU.mult))
                    need(v)
                    V.tensor_tensor(buf[:, :, NOPE:QKH], buf[:, :, NOPE:QKH],
                                    rtmp.rearrange("p (h c) -> p h c", h=HEADS), ALU.add).then_inc(heads_ready, 1)
                    dve.wait_ge(heads_ready, heads_base(l) + b + 1 if b < 4 else heads_base(l) + b + 1)
                def head_columns(h):
                    for g, dst, k in ((s.gk[h], kTb, 4), (s.gq[h], qTb, n)):
                        filled(dve, g)
                        V.tensor_copy(dst[0:QKH, h % 2, 0:k * P], bank(g)[0:QKH, 0:k * P])\
                            .then_inc(ring_free[g % RING], 1)

                head_columns(0)
                for i in range(s.N + 1):
                    if i < s.N:
                        t = i % n
                        g = s.gs[i]
                        kk = 512 if t < 2 else 256
                        filled(dve, g)
                        if i >= 4:
                            taken(dve, s.gs[i - 4])
                        v = did(V.tensor_reduce(nmax[:, i % 4:i % 4 + 1], bank(g)[:, 0:kk], AX_X, ALU.max,
                                                negate=True))
                        need(v)
                        V.tensor_scalar(nms[:, i % 4:i % 4 + 1], nmax[:, i % 4:i % 4 + 1], ATT_SCALE, None,
                                        ALU.mult).then_inc(max_ready, 1)
                        if t == 0 and i // n + 1 < HEADS:
                            head_columns(i // n + 1)
                    if i >= 1:
                        j = i - 1
                        kk = 512 if j % n < 2 else 256
                        taken(dve, s.gs[j])
                        v = did(V.reciprocal(rinv[:, j % 4:j % 4 + 1], rsum[:, j % 4:j % 4 + 1]))
                        need(v)
                        V.tensor_scalar(prob[:, j % 2, 0:kk], prob[:, j % 2, 0:kk], rinv[:, j % 4:j % 4 + 1],
                                        None, ALU.mult).then_inc(p_ready, 1)
                vs = {}
                for j in range(DC):
                    for b in range(BRANCH):
                        g = s.merge[j][1] + 2 * b
                        k = BRANCH * j + b
                        taken(dve, g)
                        filled(dve, g + 1)
                        if b and (b - 1, j - 1) in vs:
                            need(vs[b - 1, j - 1])
                        V.tensor_tensor(mT[:, j, 0:T] if b == 0 else mtmp[:, b - 1, 0:T], bank(g + 1)[:, 0:T],
                                        sgm[:, k % 2, 0:T], ALU.mult).then_inc(ring_free[(g + 1) % RING], 1)
                        if b:
                            taken(dve, g + 1)
                            if b == 2:
                                need(vs[0, j])
                            ins = V.tensor_tensor(mT[:, j, 0:T], mT[:, j, 0:T], mtmp[:, b - 1, 0:T], ALU.add)
                            if b == 2:
                                ins.then_inc(m_ready, 1)
                                dve.wait_ge(m_ready, DC * l + j + 1)
                            else:
                                vs[0, j] = did(ins)
                    modulation(s.mods[j])
                if l == 0:
                    v = scales(0, 1)
                    v = scales(1, 0)
                    v = scales(1, 1)
                    need(v)
                gate_rows(2, l, s.sets, s.grow1)
                for g0 in s.grow1:
                    taken(dve, g0)
                    taken(dve, g0 + 1)
                for t in range(n):
                    add_to_x(s.out + t, t, xtmp[:, t % 2, :])
                norm(s.norm2, n, l, 1)
                gate_rows(5, l, s.sets, s.grow2)
                for g0 in s.grow2:
                    taken(dve, g0)
                    taken(dve, g0 + 1)

                q0 = SELQ[l]

                def hold():
                    dve.nop(nofuse=True)

                class Steps:

                    def __init__(self, i, base, par):
                        self.i, self.at = i, base + par * SEL_STEPS
                        self.end = self.at + SEL_STEPS

                    def did(self, ins):
                        ins.then_inc(sel_order, 1)
                        self.at += 1

                    def need(self):
                        dve.wait_ge(sel_order, self.i * (2 * SEL_STEPS) + self.at)
                        hold()

                def best_halves(st, par, it):
                    dve.wait_ge(sel_full[par], it + 1)
                    hold()
                    sc = [ring[2 * par + p_][:, 0:NK] for p_ in range(2)]
                    for p_ in range(2):
                        st.did(V.max(sval[:, p_, 0:8], sc[p_]))
                    st.need()
                    for p_ in range(2):
                        st.did(V.max_index(sidx[:, p_, 0:8], sval[:, p_, 0:8], sc[p_]))
                        ins = V.match_replace(s2[:, p_, :], sval[:, p_, 0:8], sc[p_], NEG)
                        if p_ == 0:
                            st.did(ins)
                        else:
                            ins.then_inc(sel_free[par], 1)
                    dve.wait_ge(sel_free[par], it + 2)
                    hold()

                def rest_halves(st):
                    for p_ in range(2):
                        st.did(V.max(sval[:, p_, 8:16], s2[:, p_, :]))
                    st.need()
                    for p_ in range(2):
                        st.did(V.max_index(sidx[:, p_, 8:16], sval[:, p_, 8:16], s2[:, p_, :]))
                    st.did(V.tensor_tensor(cand, bc(sval[:, 0, :], 2, [P, TOPK, TOPK]),
                                           bc(sval[:, 1, :], 1, [P, TOPK, TOPK]), ALU.add))
                    st.need()

                def best_pairs(st, i, head):
                    cf = cand.rearrange("p a b -> p (a b)")
                    st.did(V.max(best[:, 0:8], cf))
                    st.need()
                    st.did(V.max_index(pos[:, 0:8], best[:, 0:8], cf))
                    st.did(V.match_replace(cand2, best[:, 0:8], cf, NEG))
                    st.did(V.tensor_scalar(nbest, best[:, 0:1], -1.0, None, ALU.mult))
                    st.need()
                    V.max(best[:, 8:16], cand2).then_inc(best_ready, 1)
                    dve.wait_ge(best_ready, i * 2 + (head + 1))
                    hold()
                    st.did(V.max_index(pos[:, 8:16], best[:, 8:16], cand2))
                    st.did(V.tensor_copy(sidf, sidx))
                    st.need()

                def pair_keys(st):
                    st.did(V.tensor_scalar(posu[:, 0, :], pos, 4, None, ALU.logical_shift_right))
                    st.did(V.tensor_scalar(posu[:, 1, :], pos, 15, None, ALU.bitwise_and))
                    st.need()
                    st.did(V.tensor_copy(posf, posu))
                    st.need()
                    pf = posf.rearrange("p b c -> p (b c)")
                    st.did(V.tensor_tensor(eq.rearrange("p b i j -> p (b i) j"), bc(pf, 2, [P, 2 * TOPK, TOPK]),
                                           bc(K("iota"), 1, [P, 2 * TOPK, TOPK]), ALU.is_equal))
                    st.need()
                    st.did(V.tensor_tensor(eqm, eq, bc(sidf, 2, [P, 2, TOPK, TOPK]), ALU.mult))
                    st.need()
                    st.did(V.tensor_reduce(rr, eqm, AX_X, ALU.add))
                    st.need()
                    st.did(V.tensor_scalar(ebase, rr[:, 0, :], float(NK), float(l * EXPERTS), ALU.mult, ALU.add))
                    st.need()

                def selected(st, i, head, at):
                    V.tensor_tensor(eid[:, bass.ds(i * 32 + at, TOPK)], ebase, rr[:, 1, :],
                                    ALU.add).then_inc(eid_ready, 1)
                    dve.wait_ge(gate_exp, i * 2 + (head + 1))
                    st.did(V.reciprocal(ginv, gsum))
                    st.need()
                    st.did(V.tensor_scalar(gate[:, bass.ds(i * 32 + at, TOPK)], gexp, ginv, None,
                                           ALU.mult))
                    assert st.at == st.end, (st.at, st.end)
                    st.need()

                def select(i, pair, par, it, at):
                    st = Steps(i, 2 * SEL_STEPS * pair, par)
                    best_halves(st, par, it)
                    rest_halves(st)
                    best_pairs(st, i, 2 * pair + par)
                    pair_keys(st)
                    selected(st, i, 2 * pair + par, at)

                for par in range(2):
                    select(0, 4 * q0, par, 4 * q0, TOPK * par)
                for t in range(n):
                    q = q0 + t

                    def weights(i, par, nxt):
                        head = 8 * q + par
                        for k in range(TOPK):
                            dve.wait_ge(u_in[k % UB], i * (32 * 16 // UB) + 16 * ((16 * head + k) // UB + 1))
                            V.tensor_tensor_reduce(ub[k % UB], ub[k % UB], xn[:, t, :], 1.0, 0.0,
                                                   ALU.mult, ALU.add, dots[:, par, k:k + 1]).then_inc(u_free, 1)
                        dve.wait_ge(gelu_done, i * 2 + (head + 1))
                        V.tensor_tensor(actv[:, par, :], gel[:, par, :], gate[:, bass.ds(i * 32 + par * 16, TOPK)],
                                        ALU.mult).then_inc(act_ready, 1)
                        if nxt:
                            select(i, 4 * q + 1, par, i + (4 * q + 1), 2 * TOPK + TOPK * par)

                    head_pairs(dve, t, n, weights)
                    if t + 1 < n:
                        dve.wait_ge(act_ready, 8 * (q + 1))
                        dve.wait_ge(eid_ready, 8 * (q + 1) + 2)
                        V.tensor_copy(eid[:, 0:2 * TOPK], eid[:, P:P + 2 * TOPK]).then_inc(eid_moved, 1)
                        v = did(V.tensor_copy(gate[:, 0:2 * TOPK], gate[:, P:P + 2 * TOPK]))
                        need(v)
                        dve.wait_ge(eid_moved, MOVES[l] + t + 1)
                    if t >= 1:
                        add_to_x(s.exp + t - 1, t - 1, ytmp)
                        dve.wait_ge(x_new, XNEW["out", l] + t)
                add_to_x(s.exp + n - 1, n - 1, ytmp)

            r = pl.lru
            dve.wait_ge(x_new, XNEW["exp", 1])
            v = did(V.memset(lpad[:, :, 0:LCONV - 1], 0.0))
            dve.wait_ge(rows_in, 32)
            for cidx in range(DC):
                taken(dve, r.proj + cidx // 2)
                for k in range(LCONV):
                    src = lpad[:, cidx, k:k + SEQ]
                    wc = C("lru_conv_w", k * DC + cidx)
                    need(v)
                    if k == 0:
                        v = did(V.tensor_scalar(xb[:, cidx, :], src, wc, C("lru_conv_b", cidx), ALU.mult, ALU.add))
                    else:
                        ins = V.scalar_tensor_tensor(xb[:, cidx, :], src, wc, xb[:, cidx, :], ALU.mult, ALU.add)
                        if k == LCONV - 1:
                            ins.then_inc(lru_xb, 1)
                        else:
                            v = did(ins)
            dve.wait_ge(lru_act, DC)
            v = did(V.tensor_scalar(lm[:, :, :], lm[:, :, :], -1.0, 1.0, ALU.mult, ALU.add))
            need(v)
            V.tensor_scalar(lm[:, :, :], lm[:, :, :], 0.0, None, ALU.max).then_inc(lru_dve, 1)
            dve.wait_ge(lru_xb, DC)
            v = did(V.tensor_tensor(gi[:, :, :], gi[:, :, :], xb[:, :, :], ALU.mult))
            need(v)
            dve.wait_ge(lru_act, DC + 1)
            v = did(V.memset(lm[:, :, 0:1], 1.0))
            need(v)
            v = did(V.tensor_tensor(gi[:, :, :], gi[:, :, :], lm[:, :, :], ALU.mult))
            need(v)
            taken(dve, r.proj + 7)
            for h in range(DC):
                v = did(V.tensor_tensor_scan(lm[:, h, :], gr[:, h, :], gi[:, h, :], 0.0, ALU.mult, ALU.add))
                need(v)
                V.tensor_tensor(xb[:, h, :], lm[:, h, :], yb[:, h, :], ALU.mult).then_inc(lru_h, 1)

            def layer_norm(i, g0, bias):
                for t in range(2):
                    g = g0 + t
                    wfilled(dve, g)
                    V.scalar_tensor_tensor(x[:, t, :], x[:, t, :], ALPHA, wbank(g)[:, :], ALU.mult, ALU.add)\
                        .then_inc(wide_free[g % WIDE], 1)
                    wtaken(dve, g)
                    if bias:
                        need(did(V.tensor_tensor(x[:, t, :], x[:, t, :], borow, ALU.add)))
                    for h in range(2):
                        v = did(V.bn_stats(lst[:, 12 * t + 6 * h:12 * t + 6 * h + 6],
                                           x[:, t, h * 512:(h + 1) * 512]))
                need(v)
                for t in range(2):
                    ins = V.bn_aggr(lmv3[:, t, :], lst[:, 12 * t:12 * t + 12])
                ins.then_inc(stat_ready, 1)
                dve.wait_ge(std_ready, STD["ln", i])
                v = did(V.reciprocal(lrs, lrs))
                need(v)
                for t in range(2):
                    need(did(V.tensor_scalar(x[:, t, :], x[:, t, :], lmv3[:, t, 0:1], lrs[:, t:t + 1],
                                             ALU.subtract, ALU.mult)))
                    need(did(V.tensor_tensor(x[:, t, :], x[:, t, :], lnrow[:, i, 0, :], ALU.mult)))
                    V.tensor_tensor(x[:, t, :], x[:, t, :], lnrow[:, i, 1, :], ALU.add).then_inc(x_new, 1)

            def ffn(f):
                V.memset(hpad[:, :, :, :].rearrange("p b g t -> p (b g t)"), 0.0).then_inc(ffn_pad, 1)
                for j in range(FJ + 1):
                    if j < FJ:
                        g = f.up[j]
                        taken(dve, g)
                        if j >= 2:
                            dve.wait_ge(ffn_gel, FJ * f.l + j - 1)
                        v = [0, 0]
                        for k in range(FCONV):
                            for m in range(2):
                                cidx = m * FJ + j
                                src = hpad[:, j % 2, m, k:k + SEQ]
                                dst = facc[:, j % 2, m, :]
                                wc = C("ffn_conv_w", (f.l * FCONV + k) * 2 * FJ + cidx)
                                if k == 0:
                                    v[m] = did(V.tensor_scalar(dst, src, wc, C("ffn_conv_b", f.l * 2 * FJ + cidx),
                                                               ALU.mult, ALU.add))
                                else:
                                    need(v[m])
                                    ins = V.scalar_tensor_tensor(dst, src, wc, dst, ALU.mult, ALU.add)
                                    if k == FCONV - 1:
                                        ins.then_inc(ffn_acc, 1)
                                    else:
                                        v[m] = did(ins)
                    if j >= 1:
                        i = j - 1
                        dve.wait_ge(ffn_gel, FJ * f.l + i + 1)
                        dve.wait_ge(ffn_acc, 2 * (FJ * f.l + i + 1))
                        if i >= 2:
                            filled(dve, f.up[i])
                        V.tensor_tensor(fgT[:, i % 2, :], fgel[:, i % 2, :], facc[:, i % 2, 1, :], ALU.mult)\
                            .then_inc(ffn_g, 1)

            layer_norm(0, r.out, True)
            ffn(pl.ffn[0])
            layer_norm(1, pl.ffn[0].down, False)
            a = pl.stick
            v1 = did(V.memset(one_row, 1.0))
            N = 2 * H2
            need(v1)
            for i in range(N + 2):
                if i < N:
                    b, kk = i % 2, (i % 2 + 1) * P
                    taken(dve, a.gz[i])
                    v = did(V.scalar_tensor_tensor(zsp[:, b, 0:kk], zs[:, b, 0:kk], 0.0, zl[:, b, 0:kk],
                                                   ALU.max, ALU.add))
                    need(v)
                    v = did(V.tensor_tensor(zsp[:, b, kk - P:kk], zsp[:, b, kk - P:kk], K("tri"), ALU.mult))
                    need(v)
                    v = did(V.tensor_tensor_scan(zcum[:, b, 0:kk][:, ::-1], one_row[:, 0:kk],
                                                 zsp[:, b, 0:kk][:, ::-1], 0.0, ALU.mult, ALU.add))
                    need(v)
                    if i >= 2:
                        dve.wait_ge(z_out, i - 1)
                    v = did(V.tensor_tensor(zarg[:, b, 0:kk], zs[:, b, 0:kk], zcum[:, b, 0:kk], ALU.subtract))
                    need(v)
                    V.tensor_scalar(zarg[:, b, 0:kk], zarg[:, b, 0:kk], 0.0, None, ALU.min).then_inc(z_arg, 1)
                if 1 <= i <= N:
                    j = i - 1
                    b, kk = j % 2, (j % 2 + 1) * P
                    dve.wait_ge(z_out, j + 1)
                    V.tensor_tensor(zw[:, b, kk - P:kk], zw[:, b, kk - P:kk], K("tri"), ALU.mult).then_inc(z_w, 1)
            layer_norm(2, a.out, False)
            ffn(pl.ffn[1])
            layer_norm(3, pl.ffn[1].down, False)


SEL_STEPS = 25


def arrange(inputs):
    f = {k: np.asarray(v) for k, v in inputs.items()}
    o = {}

    def columns(a):
        a = a.reshape(-1, a.shape[-1] // P, P)
        return a.transpose(2, 0, 1).reshape(P, -1)

    parts = {
        "c": columns(f["c"]), "c_ctx": columns(f["c_ctx"]), "b_mod": columns(f["b_mod"]),
        "g_norm1": columns(f["g_norm1"]), "g_norm2": columns(f["g_norm2"]), "g_ckv": columns(f["g_ckv"]),
        "g_cq": columns(f["g_cq"]),
        "w_dw": f["w_dw"].reshape(LAYERS, TAPS, 2, P).transpose(3, 0, 2, 1).reshape(P, -1),
        "b_dw": columns(f["b_dw"]), "g_cln": columns(f["g_cln"]), "b_cln": columns(f["b_cln"]),
        "lru_b_in": columns(f["lru_b_in_2"]), "lru_conv_w": columns(f["lru_conv_w_2"]),
        "lru_conv_b": columns(f["lru_conv_b_2"]), "lru_b_gates": columns(f["lru_b_gates_2"]),
        "lru_a_param": columns(f["lru_a_param_2"]), "ffn_conv_w": columns(f["ffn_conv_w_2"]),
        "ffn_conv_b": columns(f["ffn_conv_b_2"]),
    }
    o["cols"] = np.concatenate([parts[n] for n, _ in COLS], 1)
    o["hrow"] = np.stack([f["g_qn"], f["g_kn"]], 1).reshape(-1)
    o["lnrow"] = np.stack([f["ln_g_2"], f["ln_b_2"]], 2).reshape(-1)
    o["lru_b_out"] = f["lru_b_out_2"].reshape(-1)
    o["x"], o["ctx"] = f["x"][0], f["ctx"][0]

    def by_columns(a, width):
        L_, k, n = a.shape
        return a.reshape(L_, k // P, P, n // width, width).transpose(0, 3, 2, 1, 4).reshape(L_, n // width, P, -1)

    def by_rows(a, items):
        L_, k, n = a.shape
        return a.reshape(L_, items, k // P // items, P, n).transpose(0, 1, 3, 2, 4).reshape(L_, items, P, -1)

    w_in = f["w_in"]
    o["w_mod"] = by_columns(f["w_mod"], 512)
    o["w_a"] = by_rows(w_in[:, :, 0:672], 2)
    o["w_zc"] = by_columns(w_in[:, :, 672:1184], 512)
    zg = w_in[:, :, 1184:].reshape(LAYERS, DC, P, BRANCH, DC, P).transpose(0, 4, 2, 3, 1, 5)
    zg = zg.reshape(LAYERS, DC, P, BRANCH * DC * P)
    br = [by_columns(f[k], P) for k in ("wb_attn", "wb_fnet", "wb_conv")]
    o["w_m"] = np.concatenate([zg] + br, 3)
    o["w_uk"] = np.concatenate([by_rows(f["w_ukv"], 1), by_rows(f["w_uq"], 1)], 3)
    o["w_out"] = by_rows(f["w_out"], 2)
    o["w_query"] = by_columns(f["w_query"], 512)
    sk = f["sub_keys"].transpose(0, 2, 4, 1, 3)
    o["sub_keys"] = np.concatenate([sk, sk[:, :, :, 0:2]], 3).reshape(LAYERS, 1, P, (PH + 2) * NK)
    w = f["lru_w_in_2"]
    o["lru_in"] = by_columns(np.concatenate([w[:, :, W2:], w[:, :, :W2]], 2), 512)
    o["lru_gates"] = f["lru_w_gates_2"].transpose(0, 2, 1, 3).reshape(1, 1, P, -1)
    o["lru_out"] = by_rows(f["lru_w_out_2"], 2)
    o["kv_k"] = by_columns(f["kv_w_2"][None, :, :D], 512)
    o["kv_v"] = by_rows(f["kv_w_2"][None, :, D:], 2)
    o["attn_q"] = by_columns(f["attn_w_q_2"], 512)
    o["attn_out"] = by_rows(f["attn_w_out_2"], 2)
    up = f["ffn_w_up_2"]
    o["w_ffn"] = np.concatenate([by_columns(up[:, :, :FF], P), by_columns(up[:, :, FF:], P),
                                 by_rows(f["ffn_w_down_2"], FJ)], 3)
    o["u_tab"] = f["u_tab"].reshape(LAYERS * EXPERTS, D)
    o["v_tab"] = f["v_tab"].reshape(LAYERS * EXPERTS, D)
    o["const"] = shape_constants()
    return {k: np.ascontiguousarray(v) for k, v in o.items()}


def kernel(**inputs):
    import concourse.bacc as bacc
    from concourse.bass_utils import run_bass_kernel_spmd as run

    arrays = arrange(inputs)
    nc = bacc.Bacc("TRN2", target_bir_lowering=False, num_devices=1)
    args = {k: nc.dram_tensor(f"in_{k}", a.shape, mybir.dt.from_np(a.dtype), kind="ExternalInput").ap()
            for k, a in arrays.items()}
    out = nc.dram_tensor("out_x", (SEQ, D), F32, kind="ExternalOutput").ap()
    build(nc, args, out)
    r = run(nc, [{f"in_{k}": a for k, a in arrays.items()}], core_ids=[0])
    return r.results[0]["out_x"].reshape(1, SEQ, D)
```

```python
from contextlib import ExitStack

import numpy as np

import concourse.bass as bass
from concourse import mybir

F32 = mybir.dt.float32
U32 = mybir.dt.uint32
ALU = mybir.AluOpType
ACT = mybir.ActivationFunctionType
AX_X = mybir.AxisListType.X

P = 128
D = 1024
DC = D // P
SEQ = 256
LAYERS = 2
EPS = 1e-6
HEADS, NOPE, ROPE, VH = 8, 64, 32, 64
QKH = NOPE + ROPE
QL, KVL = 256, 128
KVR = KVL + ROPE
FC, GROUP = 256, 64
CC, TAPS = 256, 31
PAD = TAPS // 2
BRANCH = 3
PH, NK, TOPK = 8, 128, 16
EXPERTS = NK * NK
ATT_SCALE = float(QKH) ** -0.5

W2 = 1024
LCONV = 4
LRU_C = 8.0
FF = 3 * D
FJ = FF // P
FCONV = 3
LN_EPS = 1e-5
ALPHA = (2 * LAYERS) ** 0.25
H2, HD2 = 8, 128
STICK_SCALE = float(HD2) ** -0.5

RING, WIDE = 4, 2
BATCH = 4
WBUF = 3 * 4096
CUTS = {"third": (3, 4096, 0), "sixth": (6, 2048, 0), "quarter": (4, 3072, 0), "middle": (2, 3072, 4096)}
ARENA = 22760
UB, VB = 8, 8
NEG = -3.0e38

COLS = [("c", DC), ("c_ctx", DC), ("b_mod", LAYERS * 6 * DC), ("g_norm1", LAYERS * DC), ("g_norm2", LAYERS * DC),
        ("g_ckv", LAYERS), ("g_cq", LAYERS * 2), ("w_dw", LAYERS * 2 * TAPS), ("b_dw", LAYERS * 2),
        ("g_cln", LAYERS * 2), ("b_cln", LAYERS * 2), ("lru_b_in", 2 * DC), ("lru_conv_w", LCONV * DC),
        ("lru_conv_b", DC), ("lru_b_gates", 2 * DC), ("lru_a_param", DC), ("ffn_conv_w", LAYERS * FCONV * 2 * FJ),
        ("ffn_conv_b", LAYERS * 2 * FJ)]
COL_AT, _n = {}, 0
for _name, _k in COLS:
    COL_AT[_name] = _n
    _n += _k
NCOLS = _n

CONST = [("ident", P), ("ones", P), ("zeros", P), ("tri", P), ("iota", TOPK), ("cos", 2 * ROPE), ("sin", 2 * ROPE),
         ("dft_t", 2 * 2 * SEQ), ("dft_c", P), ("dft_s", P), ("eps", 1),
         ("ln_eps", 1)]
CONST_AT, _n = {}, 0
for _name, _k in CONST:
    CONST_AT[_name] = _n
    _n += _k
NCONST = _n


def shape_constants():
    out = np.zeros((P, NCONST), np.float32)

    def put(name, a):
        out[:, CONST_AT[name]:CONST_AT[name] + a.shape[1]] = a

    put("ident", np.eye(P))
    put("ones", np.ones((P, P)))
    put("tri", np.tril(np.ones((P, P)), -1))
    put("iota", np.tile(np.arange(TOPK), (P, 1)))
    tok = np.arange(SEQ)
    half = ROPE // 2
    inv = 10000.0 ** (-np.arange(0, half, 2) / half)
    ar, ac = (tok // 64)[:, None] * inv, (tok % 64)[:, None] * inv
    ang = np.concatenate([ar, ar, ac, ac], -1)
    sign = np.tile(np.repeat([-1.0, 1.0], half // 2), 2)
    put("cos", np.cos(ang).reshape(2, P, ROPE).transpose(1, 0, 2).reshape(P, -1))
    put("sin", (np.sin(ang) * sign).reshape(2, P, ROPE).transpose(1, 0, 2).reshape(P, -1))
    at = 2 * np.pi * (np.outer(tok, tok) % SEQ) / SEQ
    both = np.concatenate([np.cos(at), np.sin(at)], 1) / np.sqrt(SEQ * GROUP)
    put("dft_t", both.reshape(2, P, 2 * SEQ).transpose(1, 0, 2).reshape(P, -1))
    ch = np.arange(GROUP)
    ac = 2 * np.pi * (np.outer(ch, ch) % GROUP) / GROUP
    put("dft_c", np.kron(np.eye(2), np.cos(ac)))
    put("dft_s", -np.kron(np.eye(2), np.sin(ac)))
    put("eps", np.full((P, 1), EPS))
    put("ln_eps", np.full((P, 1), LN_EPS))
    return out


class Stage:
    pass


class Weights:

    def __init__(self, kind, l, i, size, cut, at):
        self.kind, self.l, self.i, self.size, self.cut, self.at = kind, l, i, size, cut, at
        self.release = None
        _, piece, first = CUTS[cut]
        self.start, self.end = first + at * piece, first + (at + 1) * piece
        assert size <= CUTS[cut][1]


class Count:
    def __init__(self):
        self.n = 0

    def take(self, k=1):
        self.n += k
        return self.n - k


def make_plan():
    ring, wide, items = Count(), Count(), []
    pl = Stage()
    pl.layers = []
    turn, uses = Count(), {}

    def item(kind, l, i, size, cut="third", at=None):
        it = Weights(kind, l, i, size, cut, turn.take() % CUTS["third"][0] if at is None else at)
        it.before = {}
        for old in items:
            if old.start < it.end and it.start < old.end:
                it.before[old.cut, old.at] = old
        it.use = uses.get((it.cut, it.at), 0) + 1
        uses[it.cut, it.at] = it.use
        items.append(it)
        return it

    mod_rows = Count()

    def mod_items(lot, places):
        out = []
        for k, (l, i) in enumerate(lot):
            it = item("w_mod_rows", l, i, 2 * D, "sixth", places[k % len(places)])
            it.release = ("mod", mod_rows.take() + 1)
            it.count = mod_rows.n
            out.append(it)
        return out

    def grow(sets):
        return [ring.take(2) for _ in range(sets)]

    for l in range(LAYERS):
        s = Stage()
        s.l, s.n, s.sets = l, (4, 2)[l], (2, 1)[l]
        s.mod_pe, s.mod_a, rest = [], [], []
        if l == 0:
            for i in range(2):
                s.mod_pe.append((item("w_mod", 0, i, 4096, "third", i), ring.take(), i))
                s.mod_pe[i][0].release = ("ring", s.mod_pe[i][1])
                s.mod_a += mod_items([(0, 4 + 2 * i), (0, 5 + 2 * i)], (4, 5))
            rest = [(0, i) for i in range(8, 24)] + [(1, i) for i in range(24)]
        s.norm1 = ring.take(DC)
        s.zc = item("w_zc", l, 0, 8 * 512, "third", 0)
        s.conv_in = ring.take(4)
        s.zc.release = ("ring", s.conv_in + 3)
        s.wa = [item("w_a", l, i, 4 * 672, "middle", i) for i in range(2)]
        s.mod_early = mod_items(rest[0:4], (5,))
        rest = rest[4:]
        s.kvq = wide.take(4)
        for it in s.wa:
            it.release = ("wide", s.kvq + 3)
        s.fn_y, s.fn_f = [], []
        for _ in range(2 * s.sets):
            s.fn_y.append(ring.take())
            s.fn_f.append(ring.take())
        s.lat_k = ring.take()
        s.lat_q = ring.take(2)
        s.uk = item("w_uk", l, 0, 2560, "third", 0)
        s.kv = wide.take(4)
        s.q = wide.take(s.n)
        s.uk.release = ("wide", s.q + s.n - 1)
        s.cv_t = ring.take(s.n)
        s.cv_b = ring.take(2)
        s.mod_b = mod_items(rest[0:2], (4, 5))

        def merge_item(j):
            return item("w_m", l, j, 4096, "third", j % 2)

        s.merge = [merge_item(0), merge_item(1)]
        s.mod_b += mod_items(rest[2:8], (4, 5))
        N = HEADS * s.n
        s.N = N
        s.gk, s.gq, s.gs, s.gp, s.att = {}, {}, {}, {}, []
        s.gk[0], s.gq[0] = ring.take(), ring.take()
        for i in range(N + 3):
            if i < N:
                s.gs[i] = ring.take()
                if i % s.n == 0 and i // s.n + 1 < HEADS:
                    s.gk[i // s.n + 1], s.gq[i // s.n + 1] = ring.take(), ring.take()
            if 2 <= i < N + 2:
                s.gp[i - 2] = ring.take()
        s.pairs = wide.take(HEADS // 2)
        s.mods = []
        for j in range(DC):
            g = ring.take(2 * BRANCH)
            s.merge[j].release = ("ring", g + 2 * BRANCH - 1)
            s.merge[j] = s.merge[j], g
            s.mods.append(mod_items(rest[8 + 4 * j:12 + 4 * j], (4, 5)))
            if j + 2 < DC:
                s.merge.append(merge_item(j + 2))
        s.grow1 = grow(s.sets)
        s.wo = [item("w_out", l, i, 4096, "third", 2 * i) for i in range(2)]
        s.out = wide.take(s.n)
        for it in s.wo:
            it.release = ("wide", s.out + s.n - 1)
        s.norm2 = ring.take(DC)
        s.back = ring.take(2 * s.n)
        s.grow2 = grow(s.sets)
        s.wq = [item("w_query", l, i, 4096, "third", 1 - i) for i in range(2)]
        s.query = ring.take(PH)
        for i, it in enumerate(s.wq):
            it.release = ("ring", s.query + 4 * i + 3)
        s.sk = item("sub_keys", l, 0, (PH + 2) * NK, "sixth", 5)
        s.sk.release = ("selected", l)
        s.exp = wide.take(s.n)
        pl.layers.append(s)

    def transposes():
        return ring.take(DC // 2)

    def ffn(l):
        f = Stage()
        f.l, f.xt, f.up, f.items = l, transposes(), [], []
        for j in range(FJ):
            it = item("w_ffn", l, j, 3072, "quarter", j % 4)
            f.items.append(it)
            f.up.append(ring.take())
        f.down = wide.take(2)
        for j in range(FJ):
            f.items[j].release = ("down", (FJ - 1) * l + j + 1) if j < FJ - 1 else ("wide", f.down + 1)
        return f

    r = Stage()
    r.xt = transposes()
    r.w = [item("lru_in", 0, i, 4096) for i in range(3)]
    r.wg = item("lru_gates", 0, 0, 2048)
    r.w.append(item("lru_in", 0, 3, 4096))
    first, r.gates, second = ring.take(5), ring.take(8), ring.take(3)
    r.proj = [first + i for i in range(5)] + [second + i for i in range(3)]
    for i, it in enumerate(r.w):
        it.release = ("ring", r.proj[2 * i + 1])
    r.wg.release = ("ring", r.gates + 7)
    r.wo = [item("lru_out", 0, i, 4096) for i in range(2)]
    r.out = wide.take(2)
    for it in r.wo:
        it.release = ("wide", r.out + 1)
    pl.lru = r
    pl.ffn = [ffn(0)]
    a = Stage()
    a.xt = transposes()
    a.wk = [item("kv_k", 0, i, 4096) for i in range(2)]
    a.k = ring.take(4)
    a.wq = [item("attn_q", 0, i, 4096) for i in range(2)]
    a.q = ring.take(4)
    for w, g in ((a.wk, a.k), (a.wq, a.q)):
        for i, it in enumerate(w):
            it.release = ("ring", g + 2 * i + 1)
    a.wv = [item("kv_v", 0, i, 4096) for i in range(2)]
    a.v = wide.take(2)
    for it in a.wv:
        it.release = ("wide", a.v + 1)
    a.gz, a.gw = {}, {}
    for b in range(2 * H2 // BATCH + 1):
        for k in range(BATCH):
            if b * BATCH < 2 * H2:
                a.gz[b * BATCH + k] = ring.take()
        for k in range(BATCH):
            if b:
                a.gw[(b - 1) * BATCH + k] = ring.take()
    a.o = wide.take(H2)
    a.wo = [item("attn_out", 0, i, 4096) for i in range(2)]
    a.out = wide.take(2)
    for it in a.wo:
        it.release = ("wide", a.out + 1)
    pl.stick = a
    pl.ffn.append(ffn(1))
    pl.items = items
    return pl


def build(nc, w, out):
    pl = make_plan()
    with ExitStack() as ctx:
        def sb(name, shape, dt=F32):
            return ctx.enter_context(nc.sbuf_tensor(name, shape, dt))

        def sem(name):
            return ctx.enter_context(nc.semaphore(name))

        const = sb("const", [P, NCONST])
        cols = sb("cols", [P, NCOLS])
        hrow = sb("hrow", [P, 2 * LAYERS * QKH])
        x = sb("x", [P, 4, D])
        hT_b = sb("hT_b", [P, DC * 512])
        xn = sb("xn", [P, 4, D])
        wbuf = sb("wbuf", [P, WBUF])
        grow = sb("grow", [P, 2, D])
        cond = sb("cond", [P, DC, 2])
        mod = sb("mod", [P, LAYERS, 6 * DC, 2])
        amod = sb("amod", [P, LAYERS, 2, DC, 2])
        small = sb("small", [P, 416])
        arena = sb("arena", [P, ARENA])

        hT = hT_b[:, :].rearrange("p (k t) -> p k t", k=DC)
        xT = hT_b[:, 0:DC * SEQ].rearrange("p (k t) -> p k t", k=DC)
        mT = xn[:, :, :].rearrange("p a (b t) -> p (a b) t", t=512)

        def K(name, a=0, b=None):
            n = dict(CONST)[name]
            return const[:, CONST_AT[name] + a:CONST_AT[name] + (n if b is None else b)]

        def C(name, i, n=1):
            return cols[:, COL_AT[name] + i:COL_AT[name] + i + n]

        class Carve:
            def __init__(self, at=0):
                self.at = at

            def __call__(self, n):
                self.at += n
                assert self.at <= ARENA, self.at
                return arena[:, self.at - n:self.at]

        sm = Count()

        def tiny(n):
            at = sm.take(n)
            assert sm.n <= 416
            return small[:, at:at + n]

        ss = tiny(8)
        rstd = tiny(8)
        lss, lr = tiny(8), tiny(8)
        hss, hr = tiny(64), tiny(64)
        cst, cmv, cr = tiny(24), tiny(8), tiny(4)
        nmax, nms, rsum, rinv = tiny(4), tiny(4), tiny(4), tiny(4)
        lst, lmv, lrs, lnb = tiny(24), tiny(4), tiny(2), tiny(2)
        sp = tiny(48)
        lmv3 = lmv.rearrange("p (t c) -> p t c", c=2)
        cmv3 = cmv.rearrange("p (t c) -> p t c", c=2)

        c = Carve()
        conv_at = c.at
        upad = c(2 * 2 * (SEQ + 2 * PAD)).rearrange("p (c s t) -> p c s t", c=2, s=2)
        cacc = c(2 * 512).rearrange("p (c s t) -> p c s t", c=2, s=2)
        cn = c(4 * CC).rearrange("p (t c) -> p t c", t=4)
        sgc = c(2 * 512).rearrange("p (c t) -> p c t", c=2)
        c2 = Carve(conv_at)
        kTb = c2(2 * 512).rearrange("p (b t) -> p b t", b=2)
        qTb = c2(2 * 512).rearrange("p (b t) -> p b t", b=2)
        prob = c2(3 * 512).rearrange("p (b t) -> p b t", b=3)
        pT = c2(2 * 512).rearrange("p (b t) -> p b t", b=2)
        fy = c(2 * 512).rearrange("p (b t) -> p b t", b=2)
        assert c2.at <= c.at
        zf = c(4 * FC).rearrange("p (t c) -> p t c", t=4)
        kvq = c(4 * 416).rearrange("p (t c) -> p t c", t=4)
        ckvT = c(512)
        cqT = c(2 * 512).rearrange("p (c t) -> p c t", c=2)
        vv = c(4 * HEADS * VH).rearrange("p (t h d) -> p t h d", t=4, h=HEADS)
        aT = c(4 * 512).rearrange("p (c t) -> p c t", c=4)
        fT = c(2 * 512).rearrange("p (c t) -> p c t", c=2)
        cvT = c(2 * 512).rearrange("p (c t) -> p c t", c=2)
        kq_at = c.at
        kq = c(8 * HEADS * QKH).rearrange("p (b h d) -> p b h d", b=8, h=HEADS)
        sqb = c(HEADS * QKH).rearrange("p (h d) -> p h d", h=HEADS)
        rtmp = sgc[:, 0, 0:256]
        c2 = Carve(kq_at)
        sgm = c2(2 * 512).rearrange("p (b t) -> p b t", b=2)
        mtmp = c2(2 * 512).rearrange("p (b t) -> p b t", b=2)
        xtmp = c2(2 * D).rearrange("p (b t) -> p b t", b=2)
        assert c2.at <= c.at

        c = Carve()
        qs = c(4 * PH * P).rearrange("p (t h c) -> p t h c", t=4, h=PH)
        dg = c(TOPK * P).rearrange("p (k c) -> p k c", k=TOPK)
        vbuf = c(VB * D).rearrange("p (k d) -> p k d", k=VB)
        ubuf4 = c(4 * D).rearrange("p (k d) -> p k d", k=4)
        ub = [ubuf4[:, k, :] for k in range(4)] + [hT_b[:, k * D:(k + 1) * D] for k in range(4)]
        eid = c(P + 2 * TOPK).bitcast(U32)
        gate = c(P + 2 * TOPK)
        qfix = c(2 * P).rearrange("p (b c) -> p b c", b=2)
        kfix = c(2 * P).rearrange("p (b c) -> p b c", b=2)
        sval = c(2 * TOPK).rearrange("p (b c) -> p b c", b=2)
        sidx = c(2 * TOPK).bitcast(U32).rearrange("p (b c) -> p b c", b=2)
        sidf = c(2 * TOPK).rearrange("p (b c) -> p b c", b=2)
        s2 = c(2 * NK).rearrange("p (b c) -> p b c", b=2)
        cand = c(256).rearrange("p (b c) -> p b c", b=TOPK)
        cand2 = c(256)
        best = c(TOPK)
        pos = c(TOPK).bitcast(U32)
        posu = c(2 * TOPK).bitcast(U32).rearrange("p (b c) -> p b c", b=2)
        posf = c(2 * TOPK).rearrange("p (b c) -> p b c", b=2)
        eq = c(2 * 256).rearrange("p (b i j) -> p b i j", b=2, i=TOPK)
        eqm = c(2 * 256).rearrange("p (b i j) -> p b i j", b=2, i=TOPK)
        rr = c(2 * TOPK).rearrange("p (b c) -> p b c", b=2)
        ebase = c(TOPK)
        nbest = c(1)
        gexp, gsum, ginv = c(TOPK), c(1), c(1)
        ixf = c(2 * TOPK).bitcast(U32).rearrange("p (b c) -> p b c", b=2)
        dots = c(2 * TOPK).rearrange("p (b c) -> p b c", b=2)
        gel = c(2 * TOPK).rearrange("p (b c) -> p b c", b=2)
        actv = c(2 * TOPK).rearrange("p (b c) -> p b c", b=2)
        ytmp = c(D)
        dgrow = dg[:, :, :].rearrange("p (s k) c -> p s k c", s=2)

        c = Carve()
        lnrow = c(4 * 2 * D).rearrange("p (i g d) -> p i g d", i=4, g=2)
        borow = c(D)
        sb_at = c.at
        lpad = c(DC * (SEQ + LCONV - 1)).rearrange("p (c t) -> p c t", c=DC)
        xb = c(DC * SEQ).rearrange("p (c t) -> p c t", c=DC)
        yb = c(DC * SEQ).rearrange("p (c t) -> p c t", c=DC)
        gi = c(DC * SEQ).rearrange("p (c t) -> p c t", c=DC)
        gr = c(DC * SEQ).rearrange("p (c t) -> p c t", c=DC)
        lm = c(DC * SEQ).rearrange("p (c t) -> p c t", c=DC)
        c = Carve(sb_at)
        hpad = c(2 * 2 * (SEQ + FCONV - 1)).rearrange("p (b g t) -> p b g t", b=2, g=2)
        facc = c(2 * 2 * SEQ).rearrange("p (b g t) -> p b g t", b=2, g=2)
        fgel = c(2 * SEQ).rearrange("p (b t) -> p b t", b=2)
        fgT = c(3 * SEQ).rearrange("p (b t) -> p b t", b=3)
        c = Carve(sb_at)
        k2T = c(H2 * SEQ).rearrange("p (h t) -> p h t", h=H2)
        q2T = c(H2 * SEQ).rearrange("p (h t) -> p h t", h=H2)
        v2 = c(2 * D).rearrange("p (t d) -> p t d", t=2)
        o2T = c(H2 * SEQ).rearrange("p (h t) -> p h t", h=H2)
        zs = xn[:, :, :].rearrange("p a (b t) -> p (a b) t", t=SEQ)[:, 0:3 * BATCH, :]
        zl = c(2 * BATCH * SEQ).rearrange("p (b t) -> p b t", b=2 * BATCH)
        zcum = c(2 * SEQ).rearrange("p (b t) -> p b t", b=2)
        wT = c(BATCH * SEQ).rearrange("p (b t) -> p b t", b=BATCH)
        one_row = c(SEQ)

        ring = [ctx.enter_context(nc.psum_tensor(f"ring{i}", [P, 512], F32)) for i in range(RING)]
        wide = [ctx.enter_context(nc.psum_tensor(f"wide{i}", [P, 1024], F32)) for i in range(WIDE)]

        ring_full = [sem(f"ring_full{i}") for i in range(RING)]
        ring_free = [sem(f"ring_free{i}") for i in range(RING)]
        wide_full = [sem(f"wide_full{i}") for i in range(WIDE)]
        wide_free = [sem(f"wide_free{i}") for i in range(WIDE)]
        weights_in = {(cut, i): sem(f"weights_in_{cut}{i}") for cut in CUTS for i in range(CUTS[cut][0])}
        crow_in = sem("crow_in")
        crow_ready = sem("crow_ready")
        mod_read = sem("mod_read")
        params_in = sem("params_in")
        x_in = sem("x_in")
        rows_in = sem("rows_in")
        x_out = sem("x_out")
        cond_ready = sem("cond_ready")
        act_order = sem("act_order")
        dve_order = sem("dve_order")
        std_ready = sem("std_ready")
        xn_ready = sem("xn_ready")
        lnb_ready = sem("lnb_ready")
        ln_scaled = sem("ln_scaled")
        x_new = sem("x_new")
        conv_done = sem("conv_done")
        lat_ready = sem("lat_ready")
        stat_ready = sem("stat_ready")
        hr_ready = sem("hr_ready")
        kn_ready = sem("kn_ready")
        qn_ready = sem("qn_ready")
        pool_order = sem("pool_order")
        max_ready = sem("max_ready")
        p_ready = sem("p_ready")
        pv_done = sem("pv_done")
        m_ready = sem("m_ready")
        gdiag_ready = sem("gdiag_ready")
        qk_copied = [sem(f"qk_copied{i}") for i in range(2)]
        sel_full = [sem(f"sel_full{i}") for i in range(2)]
        sel_free = [sem(f"sel_free{i}") for i in range(2)]
        sel_order = sem("sel_order")
        best_ready = sem("best_ready")
        gate_exp = sem("gate_exp")
        eid_ready = sem("eid_ready")
        eid_moved = sem("eid_moved")
        idx_ready = sem("idx_ready")
        u_in = [sem(f"u_in{i}") for i in range(UB)]
        v_in = [sem(f"v_in{i}") for i in range(VB)]
        u_free = sem("u_free")
        v_free = sem("v_free")
        gelu_done = sem("gelu_done")
        act_ready = sem("act_ready")
        diag_ready = sem("diag_ready")
        sp_ready = sem("sp_ready")
        lru_xb = sem("lru_xb")
        lru_h = sem("lru_h")
        lru_act = sem("lru_act")
        lru_dve = sem("lru_dve")
        ffn_pad = sem("ffn_pad")
        ffn_acc = sem("ffn_acc")
        ffn_gel = sem("ffn_gel")
        ffn_g = sem("ffn_g")
        down_done = sem("down_done")
        z_ln = sem("z_ln")
        z_arg = sem("z_arg")
        z_out = sem("z_out")
        z_w = sem("z_w")
        o_done = sem("o_done")

        def filled(e, g):
            e.wait_ge(ring_full[g % RING], g // RING + 1)

        def taken(e, g):
            e.wait_ge(ring_free[g % RING], g // RING + 1)

        def wfilled(e, g):
            e.wait_ge(wide_full[g % WIDE], g // WIDE + 1)

        def wtaken(e, g):
            e.wait_ge(wide_free[g % WIDE], g // WIDE + 1)

        def bank(g):
            return ring[g % RING]

        def wbank(g):
            return wide[g % WIDE]

        def W(it):
            return wbuf[:, it.start:it.start + it.size]

        def here(e, it):
            e.wait_ge(weights_in[it.cut, it.at], 16 * it.use)

        L = pl.layers
        STD = {}
        n_std = Count()
        for l in range(LAYERS):
            for k in ("norm1", "lat", "heads", "conv", "norm2"):
                STD[k, l] = n_std.take() + 1
        for i in range(4):
            STD["ln", i] = n_std.take() + 1
        XNEW, n_x = {}, Count()
        for l in range(LAYERS):
            for k in ("out", "exp"):
                n_x.take(L[l].n)
                XNEW[k, l] = n_x.n
        for i in range(4):
            n_x.take(2)
            XNEW["ln", i] = n_x.n
        XN, n_xn = {}, Count()
        for l in range(LAYERS):
            for k in ("norm1", "norm2"):
                XN[k, l] = n_xn.take(4 if k == "norm1" else L[l].n)
        STAT, n_stat = {}, Count()
        for l in range(LAYERS):
            for k in ("heads", "conv"):
                STAT[k, l] = n_stat.take() + 1
        for i in range(4):
            STAT["ln", i] = n_stat.take() + 1
        GD = {}
        n_gd = Count()
        for l in range(LAYERS):
            for k in (1, 2):
                GD[l, k] = n_gd.take(L[l].sets)
        SELQ = [0, 4]

        MOVES = [0, L[0].n - 1]

        def head_pairs(e, t, n, body):
            last = t + 1 == n
            with e.Fori(0, PH // 2 - last) as i:
                for par in range(2):
                    body(i, par, True)
            if last:
                for par in range(2):
                    body(PH // 2 - 1, par, False)

        def first_scores(s, par, half):
            at = half * 512 + par * NK
            return wbank(s.exp + 1)[:, at:at + NK]

        def pv_wait(e, s, j):
            if (j + 1) % (2 * s.n) == 0:
                wfilled(e, s.pairs + (j + 1) // (2 * s.n) - 1)
            else:
                before = sum(x_.N - HEADS // 2 for x_ in L[:s.l])
                e.wait_ge(pv_done, before + j + 1 - (j + 1) // (2 * s.n))

        def o_wait(e, a, j):
            if j % 2:
                wfilled(e, a.o + j // 2)
            else:
                e.wait_ge(o_done, j // 2 + 1)

        def head_norms(e, E, l, bufs, tmp, chain, order, ready):
            def step(ins):
                ins.then_inc(chain, 1)
                return order.take() + 1

            for b in bufs:
                buf = kq[:, b, :, :]
                v = step(E.tensor_tensor(buf, buf, hr[:, 8 * b:8 * b + 8].unsqueeze(2).to_broadcast(
                    [P, HEADS, QKH]), ALU.mult))
                e.wait_ge(chain, v)
                gain = (2 * l + (0 if b >= 4 else 1)) * QKH
                ins = E.tensor_tensor(buf, buf, hrow[:, gain:gain + QKH].unsqueeze(1).to_broadcast(
                    [P, HEADS, QKH]), ALU.mult)
                tt = b % 4
                if tt >= 2:
                    ins.then_inc(ready, 1)
                    continue
                e.wait_ge(chain, step(ins))
                z = buf[:, :, NOPE:QKH].rearrange("p h (a b c) -> p h a b c", a=2, b=2)
                sn = K("sin", tt * ROPE, (tt + 1) * ROPE).rearrange("p (a b c) -> p a b c", a=2, b=2)
                tv = tmp.rearrange("p (h a b c) -> p h a b c", h=HEADS, a=2, b=2)
                for o in range(2):
                    v = step(E.tensor_tensor(tv[:, :, :, o, :], z[:, :, :, 1 - o, :],
                                             sn[:, :, o, :].unsqueeze(1).to_broadcast([P, HEADS, 2, 8]), ALU.mult))
                e.wait_ge(chain, v)
                e.wait_ge(chain, step(E.tensor_tensor(
                    buf[:, :, NOPE:QKH], buf[:, :, NOPE:QKH],
                    K("cos", tt * ROPE, (tt + 1) * ROPE).unsqueeze(1).to_broadcast([P, HEADS, ROPE]), ALU.mult)))
                v = step(E.tensor_tensor(buf[:, :, NOPE:QKH], buf[:, :, NOPE:QKH],
                                         tmp.rearrange("p (h c) -> p h c", h=HEADS), ALU.add))
                e.wait_ge(chain, v)
                e.nop().then_inc(ready, 1)

        block = ctx.enter_context(nc.Block())

        @block.sync
        def _(sp_e):
            sp_e.dma_start(const[:], w["const"]).then_inc(params_in, 16)
            sp_e.dma_start(cols[:], w["cols"]).then_inc(params_in, 16)
            sp_e.dma_start(hrow[:], w["hrow"].partition_broadcast(P)).then_inc(params_in, 16)
            crow = grow[:, :, :].rearrange("p s d -> p (s d)")
            sp_e.dma_start(crow, w["crow"].partition_broadcast(P)).then_inc(crow_in, 16)
            def release(it):
                kind, g = it.release
                if kind == "ring":
                    filled(sp_e, g)
                elif kind == "wide":
                    wfilled(sp_e, g)
                elif kind == "down":
                    sp_e.wait_ge(down_done, g)
                elif kind == "mod":
                    sp_e.wait_ge(mod_read, g)
                else:
                    for par in range(2):
                        sp_e.wait_ge(sel_full[par], 4 * (SELQ[g] + L[g].n))

            for it in pl.items:
                for old in it.before.values():
                    release(old)
                if it is pl.items[4]:
                    for t in range(4):
                        src = w["x"] if t < 2 else w["ctx"]
                        sp_e.dma_start(x[:, t, :], src[(t % 2) * P:(t % 2 + 1) * P, :]).then_inc(x_in, 16)
                if it.kind == "lru_out" and it.i == 0:
                    sp_e.wait_ge(x_new, XNEW["exp", 1])
                    sp_e.dma_start(lnrow[:, :, :, :].rearrange("p i g d -> p (i g d)"),
                                   w["lnrow"].partition_broadcast(P)).then_inc(rows_in, 16)
                    sp_e.dma_start(borow, w["lru_b_out"].partition_broadcast(P)).then_inc(rows_in, 16)
                sp_e.dma_start(W(it), w[it.kind][it.l, it.i]).then_inc(weights_in[it.cut, it.at], 16)
            for t in range(2):
                sp_e.wait_ge(x_new, XNEW["ln", 3] - 1 + t)
                sp_e.dma_start(out[t * P:(t + 1) * P, :], x[:, t, :]).then_inc(x_out, 16)
            sp_e.wait_ge(x_out, 32)

        @block.tensor
        def _(pe):
            mm = nc.tensor.matmul

            def claim(g):
                if g >= RING:
                    taken(pe, g - RING)

            def wclaim(g):
                if g >= WIDE:
                    wtaken(pe, g - WIDE)

            def arrived(it):
                here(pe, it)

            def transpose(o, i):
                n = i.shape[0]
                return nc.tensor.transpose(o, i, K("ident")[0:n, 0:n])

            def modulation(it, g):
                arrived(it)
                claim(g)
                wt = W(it).rearrange("p (k c) -> p k c", k=DC)
                for m in range(4):
                    for k in range(DC):
                        last = mm(bank(g)[:, 2 * m:2 * m + 2], wt[:, k, m * P:(m + 1) * P], cond[:, k, :],
                                  start=(k == 0), stop=(k == DC - 1))
                last.then_inc(ring_full[g % RING], 1)

            def norm_transposes(g0, base, n):
                pe.wait_ge(xn_ready, base + n)
                for j in range(DC):
                    claim(g0 + j)
                    for t in range(n):
                        last = transpose(bank(g0 + j)[:, t * P:(t + 1) * P], xn[:, t, j * P:(j + 1) * P])
                    last.then_inc(ring_full[(g0 + j) % RING], 1)

            def gate_rows(gs, base, l):
                for s, g0 in enumerate(gs):
                    pe.wait_ge(gdiag_ready, base + s + 1)
                    for h in range(2):
                        claim(g0 + h)
                        mm(bank(g0 + h)[:, :], K("ones"), dgrow[:, s, 4 * h:4 * h + 4, :],
                           start=True, stop=True).then_inc(ring_full[(g0 + h) % RING], 1)

            pe.wait_ge(params_in, 48)
            pe.wait_ge(cond_ready, 2)
            for s in L:
                l, n, T = s.l, s.n, s.n * P
                for it, g, _ in s.mod_pe:
                    modulation(it, g)
                norm_transposes(s.norm1, XN["norm1", l], 4)
                for j in range(DC):
                    taken(pe, s.norm1 + j)
                arrived(s.zc)
                wt = W(s.zc).rearrange("p (k c) -> p k c", k=DC)
                for i, m in enumerate((2, 0, 3, 1)):
                    g = s.conv_in + i
                    claim(g)
                    for k in range(DC):
                        last = mm(bank(g)[:, 0:T], wt[:, k, m * P:(m + 1) * P], hT[:, k, 0:T],
                                  start=(k == 0), stop=(k == DC - 1))
                    last.then_inc(ring_full[g % RING], 1)
                for it in s.wa:
                    arrived(it)
                for t in range(4):
                    g = s.kvq + t
                    wclaim(g)
                    parts = [(0, 416, 0), (416, 672, 512)] if t < n else [(0, KVR, 0)]
                    for a, b, o in parts:
                        for k in range(DC):
                            wt = W(s.wa[k // 4])[:, (k % 4) * 672 + a:(k % 4) * 672 + b]
                            last = mm(wbank(g)[:, o:o + b - a], hT[:, k, t * P:(t + 1) * P], wt,
                                      start=(k == 0), stop=(k == DC - 1))
                    last.then_inc(wide_full[g % WIDE], 1)
                for i in range(2 * s.sets):
                    st, cc = i // 2, i % 2
                    gy, gf = s.fn_y[i], s.fn_f[i]
                    wtaken(pe, s.kvq + 2 * st)
                    wtaken(pe, s.kvq + 2 * st + 1)
                    claim(gy)
                    for tt in range(2):
                        last = mm(bank(gy)[:, :], zf[:, 2 * st + tt, cc * P:(cc + 1) * P],
                                  K("dft_t", tt * 2 * SEQ, (tt + 1) * 2 * SEQ), start=(tt == 0), stop=(tt == 1))
                    last.then_inc(ring_full[gy % RING], 1)
                    claim(gf)
                    taken(pe, gy)
                    mm(bank(gf)[:, 0:SEQ], K("dft_c"), fy[:, i % 2, 0:SEQ], start=True, stop=False)
                    mm(bank(gf)[:, 0:SEQ], K("dft_s"), fy[:, i % 2, SEQ:2 * SEQ],
                       start=False, stop=True).then_inc(ring_full[gf % RING], 1)
                pe.wait_ge(lat_ready, 4 * l + 4)
                g = s.lat_k
                claim(g)
                for t in range(4):
                    last = transpose(bank(g)[:, t * P:(t + 1) * P], kvq[:, t, 0:KVL])
                last.then_inc(ring_full[g % RING], 1)
                for cc in range(2):
                    g = s.lat_q + cc
                    claim(g)
                    for t in range(n):
                        last = transpose(bank(g)[:, t * P:(t + 1) * P], kvq[:, t, KVR + cc * P:KVR + (cc + 1) * P])
                    last.then_inc(ring_full[g % RING], 1)
                arrived(s.uk)
                taken(pe, s.lat_k)
                for t in range(4):
                    g = s.kv + t
                    wclaim(g)
                    for h in range(2):
                        last = mm(wbank(g)[:, h * 512:(h + 1) * 512], ckvT[:, t * P:(t + 1) * P],
                                  W(s.uk)[:, h * 512:(h + 1) * 512], start=True, stop=True)
                    last.then_inc(wide_full[g % WIDE], 1)
                taken(pe, s.lat_q)
                taken(pe, s.lat_q + 1)
                for t in range(n):
                    g = s.q + t
                    wclaim(g)
                    for h in range(2):
                        for cc in range(2):
                            a = 1024 + cc * 768 + h * 384
                            last = mm(wbank(g)[:, h * 512:h * 512 + 384], cqT[:, cc, t * P:(t + 1) * P],
                                      W(s.uk)[:, a:a + 384], start=(cc == 0), stop=(cc == 1))
                    last.then_inc(wide_full[g % WIDE], 1)
                pe.wait_ge(conv_done, 2 * l + 2)
                for t in range(n):
                    g = s.cv_t + t
                    claim(g)
                    for cc in range(2):
                        last = transpose(bank(g)[:, cc * P:(cc + 1) * P],
                                         cacc[:, cc, t // 2, (t % 2) * P:(t % 2 + 1) * P])
                    last.then_inc(ring_full[g % RING], 1)
                for t in range(n):
                    taken(pe, s.cv_t + t)
                for cc in range(2):
                    g = s.cv_b + cc
                    claim(g)
                    for t in range(n):
                        last = transpose(bank(g)[:, t * P:(t + 1) * P], cn[:, t, cc * P:(cc + 1) * P])
                    last.then_inc(ring_full[g % RING], 1)

                pe.wait_ge(kn_ready, 4 * (l + 1))
                pe.wait_ge(qn_ready, (l and L[0].n) + n)

                def head_columns(h):
                    for g, b0, k in ((s.gk[h], 0, 4), (s.gq[h], 4, n)):
                        claim(g)
                        for t in range(k):
                            last = transpose(bank(g)[0:QKH, t * P:(t + 1) * P], kq[:, b0 + t, h, :])
                        last.then_inc(ring_full[g % RING], 1)

                head_columns(0)
                for i in range(s.N + 3):
                    if i < s.N:
                        h, t = i // n, i % n
                        if t == 0:
                            taken(pe, s.gk[h])
                            taken(pe, s.gq[h])
                        g = s.gs[i]
                        claim(g)
                        a = 0 if t < 2 else 256
                        mm(bank(g)[:, 0:512 - a], qTb[0:QKH, h % 2, t * P:(t + 1) * P], kTb[0:QKH, h % 2, a:512],
                           start=True, stop=True).then_inc(ring_full[g % RING], 1)
                        if t == 0 and h + 1 < HEADS:
                            head_columns(h + 1)
                    if 2 <= i < s.N + 2:
                        j = i - 2
                        g = s.gp[j]
                        pe.wait_ge(p_ready, L[0].N * l + j + 1)
                        claim(g)
                        for kc in range(4 if j % n < 2 else 2):
                            last = transpose(bank(g)[:, kc * P:(kc + 1) * P], prob[:, j % 3, kc * P:(kc + 1) * P])
                        last.then_inc(ring_full[g % RING], 1)
                    if i >= 3:
                        j = i - 3
                        h, t = j // n, j % n
                        pair = s.pairs + h // 2
                        taken(pe, s.gp[j])
                        if h % 2 == 0 and t == 0:
                            wclaim(pair)
                        nk = 4 if t < 2 else 2
                        for kc in range(nk):
                            last = mm(wbank(pair)[(h % 2) * 64:(h % 2) * 64 + 64, t * P:(t + 1) * P],
                                      vv[:, 4 - nk + kc, h, :], pT[:, j % 2, kc * P:(kc + 1) * P],
                                      start=(kc == 0), stop=(kc == nk - 1))
                        if (j + 1) % (2 * n) == 0:
                            last.then_inc(wide_full[pair % WIDE], 1)
                        else:
                            last.then_inc(pv_done, 1)
                for i in range(4):
                    wtaken(pe, s.pairs + i)
                for g in s.fn_f + [s.cv_b, s.cv_b + 1]:
                    taken(pe, g)
                for j in range(DC):
                    it, g0 = s.merge[j]
                    arrived(it)
                    wt = W(it).rearrange("p (k c) -> p k c", c=P)
                    for b, (src, k0, nk) in enumerate(((aT, 24, 4), (fT, 28, 2), (cvT, 30, 2))):
                        g = g0 + 2 * b
                        claim(g)
                        for k in range(DC):
                            last = mm(bank(g)[:, 0:T], wt[:, b * DC + k, :], hT[:, k, 0:T],
                                      start=(k == 0), stop=(k == DC - 1))
                        last.then_inc(ring_full[g % RING], 1)
                        claim(g + 1)
                        for k in range(nk):
                            last = mm(bank(g + 1)[:, 0:T], wt[:, k0 + k, :], src[:, k, 0:T],
                                      start=(k == 0), stop=(k == nk - 1))
                        last.then_inc(ring_full[(g + 1) % RING], 1)
                pe.wait_ge(m_ready, DC * (l + 1))
                for it in s.wo:
                    arrived(it)

                def rows_out(its, g, src, t):
                    wclaim(g)
                    for h in range(2):
                        for k in range(DC):
                            a = (k % 4) * D + h * 512
                            last = mm(wbank(g)[:, h * 512:(h + 1) * 512], src[:, k, t * P:(t + 1) * P],
                                      W(its[k // 4])[:, a:a + 512], start=(k == 0), stop=(k == DC - 1))
                    last.then_inc(wide_full[g % WIDE], 1)

                for t in range(n):
                    rows_out(s.wo, s.out + t, mT, t)
                    if t == 0:
                        gate_rows(s.grow1, GD[l, 1], l)
                norm_transposes(s.norm2, XN["norm2", l], n)
                for j in range(DC):
                    taken(pe, s.norm2 + j)
                for t in range(n):
                    for h in range(2):
                        g = s.back + 2 * t + h
                        claim(g)
                        for j in range(4):
                            last = transpose(bank(g)[:, j * P:(j + 1) * P], hT[:, 4 * h + j, t * P:(t + 1) * P])
                        last.then_inc(ring_full[g % RING], 1)
                gate_rows(s.grow2, GD[l, 2], l)
                for h in range(PH):
                    g = s.query + h
                    if h % 4 == 0:
                        arrived(s.wq[h // 4])
                    wt = W(s.wq[h // 4]).rearrange("p (k c) -> p k c", k=DC)
                    claim(g)
                    for k in range(DC):
                        last = mm(bank(g)[:, 0:T], wt[:, k, (h % 4) * P:(h % 4 + 1) * P], hT[:, k, 0:T],
                                  start=(k == 0), stop=(k == DC - 1))
                    last.then_inc(ring_full[g % RING], 1)
                    if h == 2:
                        arrived(s.sk)
                        for g in range(2):
                            wtaken(pe, s.exp - 1 - g)
                            taken(pe, s.query + g)
                        for par in range(2):
                            for p_ in range(2):
                                last = mm(first_scores(s, par, p_), qs[64 * p_:64 * p_ + 64, 0, par, :],
                                          W(s.sk)[64 * p_:64 * p_ + 64, par * P:(par + 1) * P], start=True, stop=True)
                            last.then_inc(sel_full[par], 1)

                for b in range(RING):
                    taken(pe, s.query + PH - RING + b)

                def scores(par, i, pair):
                    pe.wait_ge(qk_copied[par], i + (pair - l))
                    pe.wait_ge(sel_free[par], i + (pair + 1))
                    mm(ring[2 * par][:, 0:NK], qfix[0:64, par, :], kfix[0:64, par, :], start=True, stop=True)
                    mm(ring[2 * par + 1][:, 0:NK], qfix[64:128, par, :], kfix[64:128, par, :],
                       start=True, stop=True).then_inc(sel_full[par], 1)

                q0 = SELQ[l]
                for t in range(n):
                    g = s.exp + t
                    wclaim(g)
                    for h in range(2):
                        mm(wbank(g)[:, h * 512:(h + 1) * 512], K("zeros"), const[:, 0:512],
                           start=True, stop=False)

                    def weigh(i, par, nxt):
                        if nxt:
                            scores(par, i, 4 * (q0 + t) + 1)
                        pick0 = 128 * (q0 + t) + 16 * par
                        for k in range(TOPK):
                            pe.wait_ge(diag_ready, i * 32 + (pick0 + k + 1))
                            pe.wait_ge(v_in[k % VB], i * (32 * 16 // VB) + 16 * ((pick0 + k) // VB + 1))
                            for h in range(2):
                                last = mm(wbank(g)[:, h * 512:(h + 1) * 512], dg[:, k, :],
                                          vbuf[:, k % VB, h * 512:(h + 1) * 512], start=False, stop=False,
                                          skip_group_check=True)
                            last.then_inc(v_free, 1)

                    head_pairs(pe, t, n, weigh)
                    for h in range(2):
                        last = mm(wbank(g)[:, h * 512:(h + 1) * 512], K("zeros"), const[:, 0:512],
                                  start=False, stop=True)
                    last.then_inc(wide_full[g % WIDE], 1)
                for par in range(2):
                    pe.wait_ge(sel_free[par], 4 * (q0 + n) + 1)

            def x_columns(g0, have):
                for t in range(2):
                    pe.wait_ge(x_new, have - 1 + t)
                    for jj in range(DC // 2):
                        g = g0 + jj
                        if t == 0:
                            claim(g)
                        for b in range(2):
                            last = transpose(bank(g)[:, (2 * b + t) * P:(2 * b + t + 1) * P],
                                             x[:, t, (2 * jj + b) * P:(2 * jj + b + 1) * P])
                        if t == 1:
                            last.then_inc(ring_full[g % RING], 1)
                for jj in range(DC // 2):
                    taken(pe, g0 + jj)

            def column_group(it, half, g):
                arrived(it)
                wt = W(it).rearrange("p (k c) -> p k c", k=DC)
                claim(g)
                for m in range(2):
                    for k in range(DC):
                        last = mm(bank(g)[:, m * SEQ:(m + 1) * SEQ],
                                  wt[:, k, (2 * half + m) * P:(2 * half + m + 1) * P], xT[:, k, :],
                                  start=(k == 0), stop=(k == DC - 1))
                last.then_inc(ring_full[g % RING], 1)

            def columns(its, g0):
                for i, it in enumerate(its):
                    for half in range(2):
                        column_group(it, half, g0 + 2 * i + half)

            def rows(its, g0, src):
                for it in its:
                    arrived(it)
                for t in range(2):
                    rows_out(its, g0 + t, src, t)

            r = pl.lru
            x_columns(r.xt, XNEW["exp", 1])

            for i in range(5):
                column_group(r.w[i // 2], i % 2, r.proj[i])
            arrived(r.wg)
            for h in range(DC):
                g = r.gates + h
                claim(g)
                pe.wait_ge(lru_xb, h + 1)
                for m in range(2):
                    last = mm(bank(g)[:, m * SEQ:(m + 1) * SEQ], W(r.wg)[:, (2 * h + m) * P:(2 * h + m + 1) * P],
                              xb[:, h, :], start=True, stop=True)
                last.then_inc(ring_full[g % RING], 1)
            for i in range(5, 8):
                column_group(r.w[i // 2], i % 2, r.proj[i])
            pe.wait_ge(lru_h, DC)
            rows(r.wo, r.out, xb)

            def ffn(f, have):
                x_columns(f.xt, have)
                for j in range(FJ + 2):
                    if j < FJ:
                        it, g = f.items[j], f.up[j]
                        arrived(it)
                        claim(g)
                        for m in range(2):
                            for k in range(DC):
                                last = mm(bank(g)[:, m * SEQ:(m + 1) * SEQ],
                                          W(it)[:, (m * DC + k) * P:(m * DC + k + 1) * P], xT[:, k, :],
                                          start=(k == 0), stop=(k == DC - 1))
                        last.then_inc(ring_full[g % RING], 1)
                    if j == 0:
                        for t in range(2):
                            wclaim(f.down + t)
                    if j >= 2:
                        i = j - 2
                        pe.wait_ge(ffn_g, FJ * f.l + i + 1)
                        for t in range(2):
                            for h in range(2):
                                last = mm(wbank(f.down + t)[:, h * 512:(h + 1) * 512],
                                          fgT[:, i % 3, t * P:(t + 1) * P],
                                          W(f.items[i])[:, 2048 + h * 512:2048 + (h + 1) * 512],
                                          start=(i == 0), stop=(i == FJ - 1), skip_group_check=True)
                            if i == FJ - 1:
                                last.then_inc(wide_full[(f.down + t) % WIDE], 1)
                        if i < FJ - 1:
                            last.then_inc(down_done, 1)

            ffn(pl.ffn[0], XNEW["ln", 0])
            a = pl.stick
            x_columns(a.xt, XNEW["ln", 1])
            columns(a.wk, a.k)
            columns(a.wq, a.q)
            NB = 2 * H2 // BATCH

            def stick_scores(b):
                for i in range(b * BATCH, min(b + 1, NB) * BATCH):
                    h, t = i // 2, i % 2
                    g = a.gz[i]
                    claim(g)
                    mm(bank(g)[:, 0:(t + 1) * P], q2T[:, h, t * P:(t + 1) * P], k2T[:, h, 0:(t + 1) * P],
                       start=True, stop=True).then_inc(ring_full[g % RING], 1)

            for g in range(4):
                taken(pe, a.k + g)
                taken(pe, a.q + g)
            stick_scores(0)
            rows(a.wv, a.v, xT)
            wtaken(pe, a.v)
            wtaken(pe, a.v + 1)
            for b in range(NB + 1):
                if b:
                    stick_scores(b)
                before = range(max(b - 1, 0) * BATCH, b * BATCH)
                for j in before:
                    g = a.gw[j]
                    pe.wait_ge(z_w, j + 1)
                    claim(g)
                    for kc in range(j % 2 + 1):
                        last = transpose(bank(g)[:, kc * P:(kc + 1) * P],
                                         zs[:, j % (3 * BATCH), kc * P:(kc + 1) * P])
                    last.then_inc(ring_full[g % RING], 1)
                for j in before:
                    h, t = j // 2, j % 2
                    go = a.o + h
                    taken(pe, a.gw[j])
                    if t == 0:
                        wclaim(go)
                    for kc in range(t + 1):
                        last = mm(wbank(go)[:, t * P:(t + 1) * P], v2[:, kc, h * P:(h + 1) * P],
                                  wT[:, j % BATCH, kc * P:(kc + 1) * P], start=(kc == 0), stop=(kc == t))
                    last.then_inc(*((wide_full[go % WIDE], 1) if t else (o_done, 1)))
            for h in range(H2):
                wtaken(pe, a.o + h)
            rows(a.wo, a.out, o2T)
            ffn(pl.ffn[1], XNEW["ln", 2])

        @block.scalar
        def _(act):
            A = nc.scalar.activation
            order = Count()

            def did(ins):
                ins.then_inc(act_order, 1)
                return order.take() + 1

            def need(v):
                act.wait_ge(act_order, v)

            act.wait_ge(params_in, 48)
            for s_ in range(2):
                A(cond[:, :, s_], C("c", s_ * DC, DC), ACT.Silu).then_inc(cond_ready, 1)
            act.wait_ge(crow_in, 16)
            A(grow[:, :, :], grow[:, :, :], ACT.Silu).then_inc(crow_ready, 1)
            v = did(A(sp[:, 0:8], C("lru_a_param", 0, 8), ACT.Abs))
            need(v)
            A(sp[:, 8:16], sp[:, 0:8], ACT.Exp, scale=-1.0).then_inc(sp_ready, 1)
            act.wait_ge(sp_ready, 2)
            A(sp[:, 24:32], sp[:, 16:24], ACT.Ln).then_inc(sp_ready, 1)

            def norm(tiles, before, buf):
                last = 0
                for t in range(tiles):
                    if before is not None:
                        act.wait_ge(x_new, before + t + 1)
                    if last and buf is not None:
                        need(last)
                    last = did(A(xn[:, t, :] if buf is None else buf, x[:, t, :], ACT.Square,
                                 accum_out=ss[:, t:t + 1]))
                need(last)
                A(ss[:, 4:4 + tiles], ss[:, 0:tiles], ACT.Sqrt, scale=1.0 / D, bias=K("eps")).then_inc(std_ready, 1)

            def gate_rows(gs):
                for s_, g0 in enumerate(gs):
                    for h in range(2):
                        filled(act, g0 + h)
                        A(grow[:, s_, h * 512:(h + 1) * 512], bank(g0 + h)[:, :], ACT.Copy)\
                            .then_inc(ring_free[(g0 + h) % RING], 1)

            act.wait_ge(x_in, 64)
            for s in L:
                l, n, T = s.l, s.n, s.n * P
                norm(4, XNEW["exp", 0] - 4 if l else None, None)
                for i in (0, 2):
                    g = s.conv_in + i
                    filled(act, g)
                    A(sgc[:, i // 2, 0:T], bank(g)[:, 0:T], ACT.Sigmoid).then_inc(ring_free[g % RING], 1)
                last = 0
                for t in range(4):
                    g = s.kvq + t
                    wfilled(act, g)
                    if t < n:
                        A(kvq[:, t, :], wbank(g)[:, 0:416], ACT.Copy)
                        A(zf[:, t, :], wbank(g)[:, 512:768], ACT.Copy).then_inc(wide_free[g % WIDE], 1)
                    else:
                        A(kvq[:, t, 0:KVR], wbank(g)[:, 0:KVR], ACT.Copy).then_inc(wide_free[g % WIDE], 1)
                    wtaken(act, g)
                    need(last) if last else None
                    last = did(A(fy[:, 0, 0:KVL], kvq[:, t, 0:KVL], ACT.Square, accum_out=lss[:, t:t + 1]))
                    if t < n:
                        need(last)
                        last = did(A(fy[:, 0, 0:QL], kvq[:, t, KVR:416], ACT.Square, accum_out=lss[:, 4 + t:5 + t]))
                need(last)
                A(lr[:, 0:4], lss[:, 0:4], ACT.Sqrt, scale=1.0 / KVL, bias=K("eps"))
                A(lr[:, 4:4 + n], lss[:, 4:4 + n], ACT.Sqrt, scale=1.0 / QL, bias=K("eps")).then_inc(std_ready, 1)
                for i in range(2 * s.sets):
                    g = s.fn_y[i]
                    filled(act, g)
                    if i >= 2:
                        filled(act, s.fn_f[i - 2])
                    A(fy[:, i % 2, :], bank(g)[:, :], ACT.Copy).then_inc(ring_free[g % RING], 1)
                for t in range(4):
                    g = s.kv + t
                    wfilled(act, g)
                    src = wbank(g)[:, :].rearrange("p (h d) -> p h d", h=HEADS)
                    A(vv[:, t, :, :], src[:, :, NOPE:P], ACT.Copy)
                    A(kq[:, t, :, 0:NOPE], src[:, :, 0:NOPE], ACT.Copy).then_inc(wide_free[g % WIDE], 1)
                for t in range(n):
                    g = s.q + t
                    wfilled(act, g)
                    A(kq[:, 4 + t, :, :].rearrange("p (a h) d -> p a (h d)", a=2),
                      wbank(g)[:, :].rearrange("p (a c) -> p a c", a=2)[:, :, 0:384], ACT.Copy)\
                        .then_inc(wide_free[g % WIDE], 1)
                act.wait_ge(stat_ready, STAT["heads", l])
                A(hss[:, 0:32 + 8 * n], hss[:, 0:32 + 8 * n], ACT.Sqrt, scale=1.0 / QKH, bias=K("eps"))\
                    .then_inc(std_ready, 1)
                act.wait_ge(stat_ready, STAT["conv", l])
                A(cr[:, 0:n], cmv3[:, 0:n, 1], ACT.Sqrt, bias=K("eps")).then_inc(std_ready, 1)
                for cc in range(2):
                    g = s.cv_b + cc
                    filled(act, g)
                    A(cvT[:, cc, 0:T], bank(g)[:, 0:T], ACT.Silu, scale=C("g_cln", 2 * l + cc),
                      bias=C("b_cln", 2 * l + cc)).then_inc(ring_free[g % RING], 1)
                for i in range(s.N + 4):
                    if i < s.N:
                        t = i % n
                        g = s.gs[i]
                        kk = 512 if t < 2 else 256
                        filled(act, g)
                        act.wait_ge(max_ready, L[0].N * l + i + 1)
                        if i >= 3:
                            filled(act, s.gp[i - 3])
                        A(prob[:, i % 3, 0:kk], bank(g)[:, 0:kk], ACT.Exp, scale=ATT_SCALE,
                          bias=nms[:, i % 4:i % 4 + 1], accum_out=rsum[:, i % 4:i % 4 + 1])\
                            .then_inc(ring_free[g % RING], 1)
                    if 2 <= i < s.N + 2:
                        j = i - 2
                        g = s.gp[j]
                        kk = 512 if j % n < 2 else 256
                        filled(act, g)
                        if j >= 2:
                            pv_wait(act, s, j - 2)
                        A(pT[:, j % 2, 0:kk], bank(g)[:, 0:kk], ACT.Copy).then_inc(ring_free[g % RING], 1)
                    if i >= 4 and (i - 3) % (2 * n) == 0:
                        p_ = (i - 3) // (2 * n) - 1
                        g = s.pairs + p_
                        wfilled(act, g)
                        A(aT[:, p_, 0:T], wbank(g)[:, 0:T], ACT.Copy).then_inc(wide_free[g % WIDE], 1)
                for j in range(DC):
                    for b in range(BRANCH):
                        g = s.merge[j][1] + 2 * b
                        k = BRANCH * j + b
                        filled(act, g)
                        if k >= 2:
                            kk = k - 2
                            taken(act, s.merge[kk // BRANCH][1] + 2 * (kk % BRANCH) + 1)
                        A(sgm[:, k % 2, 0:T], bank(g)[:, 0:T], ACT.Sigmoid).then_inc(ring_free[g % RING], 1)
                gate_rows(s.grow1)
                norm(n, XNEW["out", l] - n, mtmp[:, :, :].rearrange("p b t -> p (b t)"))
                for t in range(n):
                    for h in range(2):
                        g = s.back + 2 * t + h
                        filled(act, g)
                        A(xn[:, t, h * 512:(h + 1) * 512], bank(g)[:, :], ACT.Copy).then_inc(ring_free[g % RING], 1)
                gate_rows(s.grow2)
                q0 = SELQ[l]

                def select_gate(i, head):
                    act.wait_ge(best_ready, i * 2 + (head + 1))
                    A(gexp, best, ACT.Exp, bias=nbest, accum_out=gsum).then_inc(gate_exp, 1)

                for h in range(PH):
                    g = s.query + h
                    filled(act, g)
                    A(qs[:, 0:n, h, :], bank(g)[:, 0:T].rearrange("p (t c) -> p t c", t=n), ACT.Copy)\
                        .then_inc(ring_free[g % RING], 1)
                    if h in (3, 5):
                        select_gate(0, 8 * q0 + (h - 3) // 2)

                taken(act, s.query + PH - 1)
                here(act, s.sk)
                qflat = qs[:, :, :, :].rearrange("p t h c -> p (t h c)")
                keys = W(s.sk)

                def select_in(par, i, t, it):
                    act.wait_ge(sel_free[par], it + 1)
                    A(qfix[:, par, :], qflat[:, bass.ds(i * (2 * P) + (t * PH + 2 + par) * P, P)], ACT.Copy)
                    A(kfix[:, par, :], keys[:, bass.ds(i * (2 * P) + (2 + par) * P, P)], ACT.Copy)\
                        .then_inc(qk_copied[par], 1)

                for t in range(n):
                    def weights(i, par, nxt):
                        head = 8 * (q0 + t) + par
                        if nxt:
                            select_in(par, i, t, i + (4 * (q0 + t) + 1))
                        act.wait_ge(u_free, i * 32 + (UB + 16 * (head + 1)))
                        A(gel[:, par, :], dots[:, par, :], ACT.Gelu_apprx_tanh).then_inc(gelu_done, 1)
                        act.wait_ge(act_ready, i * 2 + (head + 1))
                        act.wait_ge(v_free, i * 32 + (VB + 16 * head))
                        for k in range(TOPK):
                            A(dg[:, k, :], K("ident"), ACT.Copy, scale=actv[:, par, k:k + 1])\
                                .then_inc(diag_ready, 1)
                        if nxt:
                            select_gate(i, head + 2)

                    head_pairs(act, t, n, weights)

            def x_columns(g0):
                for jj in range(DC // 2):
                    g = g0 + jj
                    filled(act, g)
                    A(hT_b[:, jj * 512:(jj + 1) * 512], bank(g)[:, :], ACT.Copy).then_inc(ring_free[g % RING], 1)

            r = pl.lru
            x_columns(r.xt)
            act.wait_ge(x_new, XNEW["exp", 1])

            def lru_projection(i):
                g = r.proj[i]
                filled(act, g)
                for m in range(2):
                    cidx = 2 * i + m
                    src = bank(g)[:, m * SEQ:(m + 1) * SEQ]
                    if cidx < DC:
                        ins = A(lpad[:, cidx, LCONV - 1:LCONV - 1 + SEQ], src, ACT.Identity,
                                bias=C("lru_b_in", DC + cidx))
                    else:
                        ins = A(yb[:, cidx - DC, :], src, ACT.Gelu_apprx_tanh, bias=C("lru_b_in", cidx - DC))
                ins.then_inc(ring_free[g % RING], 1)

            for i in range(5):
                lru_projection(i)
            for h in range(DC):
                g = r.gates + h
                filled(act, g)
                A(gi[:, h, :], bank(g)[:, 0:SEQ], ACT.Sigmoid, bias=C("lru_b_gates", 2 * h))
                A(gr[:, h, :], bank(g)[:, SEQ:2 * SEQ], ACT.Sigmoid, bias=C("lru_b_gates", 2 * h + 1))\
                    .then_inc(ring_free[g % RING], 1)
            taken(act, r.gates + DC - 1)
            act.wait_ge(sp_ready, 4)
            for h in range(DC):
                v = did(A(lm[:, h, :], gr[:, h, :], ACT.Exp, scale=sp[:, 40 + h:41 + h]))
                need(v)
                A(gr[:, h, :], gr[:, h, :], ACT.Exp, scale=sp[:, 32 + h:33 + h]).then_inc(lru_act, 1)
            act.wait_ge(lru_dve, 1)
            A(lm[:, :, :], lm[:, :, :], ACT.Sqrt).then_inc(lru_act, 1)
            for i in range(5, 8):
                lru_projection(i)

            def layer_norm(i):
                act.wait_ge(stat_ready, STAT["ln", i])
                A(lrs[:, :], lmv3[:, :, 1], ACT.Sqrt, bias=K("ln_eps")).then_inc(std_ready, 1)
                act.wait_ge(lnb_ready, i + 1)
                for t in range(2):
                    A(x[:, t, :], x[:, t, :], ACT.Identity, scale=lrs[:, t:t + 1], bias=lnb[:, t:t + 1])\
                        .then_inc(ln_scaled, 1)

            def ffn(f):
                x_columns(f.xt)
                for j in range(FJ):
                    g = f.up[j]
                    filled(act, g)
                    if j == 0:
                        act.wait_ge(ffn_pad, f.l + 1)
                    if j >= 2:
                        act.wait_ge(ffn_acc, 2 * (FJ * f.l + j - 1))
                    A(hpad[:, j % 2, :, FCONV - 1:FCONV - 1 + SEQ],
                      bank(g)[:, :].rearrange("p (g t) -> p g t", g=2), ACT.Copy).then_inc(ring_free[g % RING], 1)
                    if j >= 1:
                        gelu_step(f, j - 1)
                gelu_step(f, FJ - 1)

            def gelu_step(f, j):
                act.wait_ge(ffn_acc, 2 * (FJ * f.l + j) + 1)
                if j >= 2:
                    act.wait_ge(ffn_g, FJ * f.l + j - 1)
                A(fgel[:, j % 2, :], facc[:, j % 2, 0, :], ACT.Gelu_apprx_tanh).then_inc(ffn_gel, 1)

            layer_norm(0)
            ffn(pl.ffn[0])
            layer_norm(1)
            a = pl.stick
            x_columns(a.xt)
            for dst, g0 in ((k2T, a.k), (q2T, a.q)):
                for i in range(4):
                    g = g0 + i
                    filled(act, g)
                    A(dst[:, 2 * i:2 * i + 2, :], bank(g)[:, :].rearrange("p (h t) -> p h t", h=2), ACT.Copy)\
                        .then_inc(ring_free[g % RING], 1)
            NB = 2 * H2 // BATCH

            def step(i):
                return i % (3 * BATCH), i % (2 * BATCH), (i % 2 + 1) * P

            for b in range(NB + 2):
                these = range(b * BATCH, min(b + 1, NB) * BATCH)
                before = range(max(b - 1, 0) * BATCH, min(b, NB) * BATCH)
                v = {}
                for i in these:
                    s3, s2_, kk = step(i)
                    g = a.gz[i]
                    filled(act, g)
                    if i >= 3 * BATCH:
                        filled(act, a.gw[i - 3 * BATCH])
                    if i >= 2 * BATCH:
                        act.wait_ge(z_arg, i - 2 * BATCH + 1)
                    A(zs[:, s3, 0:kk], bank(g)[:, 0:kk], ACT.Copy, scale=STICK_SCALE)
                    A(zl[:, s2_, 0:kk], bank(g)[:, 0:kk], ACT.Abs, scale=STICK_SCALE)\
                        .then_inc(ring_free[g % RING], 1)
                for i in these:
                    _, s2_, kk = step(i)
                    taken(act, a.gz[i])
                    v[i] = did(A(zl[:, s2_, 0:kk], zl[:, s2_, 0:kk], ACT.Exp, scale=-1.0))
                if b >= 2:
                    for h in range((b - 2) * BATCH // 2, (b - 1) * BATCH // 2):
                        g = a.o + h
                        wfilled(act, g)
                        A(o2T[:, h, :], wbank(g)[:, 0:SEQ], ACT.Copy).then_inc(wide_free[g % WIDE], 1)
                for j in before:
                    s3, _, kk = step(j)
                    act.wait_ge(z_arg, j + 1)
                    A(zs[:, s3, 0:kk], zs[:, s3, 0:kk], ACT.Exp).then_inc(z_out, 1)
                for i in these:
                    _, s2_, kk = step(i)
                    need(v[i])
                    A(zl[:, s2_, 0:kk], zl[:, s2_, 0:kk], ACT.Ln, bias=1.0).then_inc(z_ln, 1)
                if b == 0:
                    for t in range(2):
                        g = a.v + t
                        wfilled(act, g)
                        A(v2[:, t, :], wbank(g)[:, :], ACT.Copy).then_inc(wide_free[g % WIDE], 1)
                for j in before:
                    g, kk = a.gw[j], (j % 2 + 1) * P
                    filled(act, g)
                    if j >= BATCH:
                        o_wait(act, a, j - BATCH)
                    A(wT[:, j % BATCH, 0:kk], bank(g)[:, 0:kk], ACT.Copy).then_inc(ring_free[g % RING], 1)
            layer_norm(2)
            ffn(pl.ffn[1])
            layer_norm(3)

        @block.gpsimd
        def _(pool):
            pool.sem_inc(u_free, UB)
            pool.sem_inc(v_free, VB)
            for par in range(2):
                pool.sem_inc(sel_free[par], 1)
            order = Count()
            for s in L:
                pool.wait_ge(hr_ready, s.l + 1)
                head_norms(pool, nc.gpsimd, s.l, range(4, 4 + s.n), sgc[:, 1, 0:256], pool_order, order, qn_ready)
                for t in range(s.n):
                    q = SELQ[s.l] + t
                    if t >= 1:
                        pool.wait_ge(eid_moved, MOVES[s.l] + t)

                    def numbers(i, par):
                        pool.wait_ge(eid_ready, i * 2 + (8 * q + par + 1))
                        pool.nop(nofuse=True)
                        nc.gpsimd.tensor_copy(ixf[:, par, :], eid[:, bass.ds(i * 32 + par * 16, TOPK)])\
                            .then_inc(idx_ready, 1)
                        pool.wait_ge(idx_ready, i * 2 + (8 * q + par + 1))
                        pool.nop(nofuse=True)

                    def fetch(i, par, bufs, tab, free, arrive, a, b):
                        for k in range(a, b):
                            pool.wait_ge(free, i * 32 + (128 * q + 16 * par + k + 1))
                            pool.nop(nofuse=True)
                            nc.gpsimd.indirect_dma_start(
                                bufs[k % len(bufs)], None, tab,
                                bass.IndirectOffsetOnAxis(ap=ixf[:, par, k:k + 1], axis=0))\
                                .then_inc(arrive[k % len(bufs)], 16)

                    u = ub, w["u_tab"], u_free, u_in
                    vv_ = [vbuf[:, k, :] for k in range(VB)], w["v_tab"], v_free, v_in
                    if t == 0:
                        numbers(0, 0)
                        fetch(0, 0, *u, 0, 4)
                        fetch(0, 0, *vv_, 0, VB)
                        filled(pool, s.query + PH - 1)
                        fetch(0, 0, *u, 4, TOPK)
                        numbers(0, 1)
                        fetch(0, 1, *u, 0, UB)
                        fetch(0, 0, *vv_, VB, TOPK)
                        fetch(0, 1, *u, UB, TOPK)
                        fetch(0, 1, *vv_, 0, TOPK)
                    with pool.Fori(1 if t == 0 else 0, PH // 2) as i:
                        for par in range(2):
                            numbers(i, par)
                            fetch(i, par, *u, 0, TOPK)
                            fetch(i, par, *vv_, 0, TOPK)

        @block.vector
        def _(dve):
            V = nc.vector
            order = Count()

            def did(ins):
                ins.then_inc(dve_order, 1)
                return order.take() + 1

            def need(v):
                dve.wait_ge(dve_order, v)

            def bc(ap, axis, shape):
                return ap.unsqueeze(axis).to_broadcast(shape)

            dve.wait_ge(params_in, 48)
            dve.wait_ge(sp_ready, 1)
            V.tensor_scalar(sp[:, 16:24], sp[:, 8:16], 1.0, None, ALU.add).then_inc(sp_ready, 1)
            dve.wait_ge(sp_ready, 3)
            v = did(V.tensor_scalar(sp[:, 32:40], sp[:, 16:24], 1.0, None, ALU.subtract))
            need(v)
            v = did(V.tensor_tensor(sp[:, 32:40], sp[:, 8:16], sp[:, 32:40], ALU.subtract))
            need(v)
            v = did(V.reciprocal(sp[:, 40:48], sp[:, 16:24]))
            need(v)
            v = did(V.tensor_tensor(sp[:, 32:40], sp[:, 32:40], sp[:, 40:48], ALU.mult))
            need(v)
            v = did(V.tensor_tensor(sp[:, 24:32], sp[:, 24:32], sp[:, 32:40], ALU.add))
            need(v)
            v = did(V.tensor_scalar(sp[:, 0:8], C("lru_a_param", 0, 8), -1.0, 0.0, ALU.mult, ALU.max))
            need(v)
            v = did(V.tensor_tensor(sp[:, 24:32], sp[:, 24:32], sp[:, 0:8], ALU.add))
            need(v)
            V.tensor_scalar(sp[:, 32:40], sp[:, 24:32], -LRU_C, None, ALU.mult)
            V.tensor_scalar(sp[:, 40:48], sp[:, 24:32], -2.0 * LRU_C, None, ALU.mult).then_inc(sp_ready, 1)

            def modulation(it, g, i):
                filled(dve, g)
                V.tensor_tensor(mod[:, 0, 4 * i:4 * i + 4, :], bank(g)[:, 0:8].rearrange("p (m s) -> p m s", m=4),
                                bc(C("b_mod", 4 * i, 4), 2, [P, 4, 2]), ALU.add).then_inc(ring_free[g % RING], 1)
                taken(dve, g)

            junk = [zf[:, :, :].rearrange("p t c -> p (t c)"), kvq[:, :, :].rearrange("p t c -> p (t c)")[:, 0:D]]
            junk_written = [0, 0]

            early_junk = kq[:, :, :, :].rearrange("p b h d -> p (b h d)")
            early_junk = [early_junk[:, 0:D], early_junk[:, D:2 * D]]

            def mod_products(lot, a, b, junk=junk):
                for k in range(a, min(b, 4 * len(lot))):
                    it, m, st = lot[k // 4], k % 4 // 2, k % 2
                    if k % 4 == 0:
                        here(dve, it)
                    if junk_written[st]:
                        need(junk_written[st])
                    ins = V.tensor_tensor_reduce(junk[st], W(it)[:, m * D:(m + 1) * D], grow[:, st, :], 1.0, 0.0,
                                                 ALU.mult, ALU.add, mod[:, it.l, 2 * it.i + m, st:st + 1])
                    if k % 4 < 3:
                        junk_written[st] = did(ins)
                    else:
                        ins.then_inc(mod_read, 1)
                        dve.wait_ge(mod_read, it.count)
                        need(junk_written[0])
                        bias = C("b_mod", it.l * 6 * DC + 2 * it.i, 2)
                        mods = mod[:, it.l, 2 * it.i:2 * it.i + 2, :]
                        junk_written[st] = did(V.tensor_tensor(mods, mods, bc(bias, 2, [P, 2, 2]), ALU.add))


            def scales(l, which):
                gname = ("g_norm1", "g_norm2")[which]
                sc = 3 * which + 1
                return did(V.scalar_tensor_tensor(
                    amod[:, l, which, :, :], mod[:, l, sc * DC:(sc + 1) * DC, :], 1.0,
                    bc(C(gname, l * DC, DC), 2, [P, DC, 2]), ALU.add, ALU.mult))

            def norm(g0, tiles, l, which):
                dve.wait_ge(std_ready, STD[("norm1", "norm2")[which], l])
                v = did(V.reciprocal(rstd[:, 0:tiles], ss[:, 4:4 + tiles]))
                need(v)
                for t in range(tiles):
                    V.tensor_scalar(xn[:, t, :], x[:, t, :], rstd[:, t:t + 1], None, ALU.mult)\
                        .then_inc(xn_ready, 1)
                for j in range(DC):
                    g = g0 + j
                    filled(dve, g)
                    for st in range(tiles // 2):
                        ins = V.tensor_scalar(
                            hT[:, j, st * SEQ:(st + 1) * SEQ], bank(g)[:, st * SEQ:(st + 1) * SEQ],
                            amod[:, l, which, j, st:st + 1],
                            mod[:, l, 3 * which * DC + j, st:st + 1], ALU.mult, ALU.add)
                    ins.then_inc(ring_free[g % RING], 1)

            def gate_rows(vec, l, sets, gs):
                for st in range(sets):
                    V.tensor_tensor(dgrow[:, st, :, :], bc(K("ident"), 1, [P, DC, P]),
                                    bc(mod[:, l, vec * DC:(vec + 1) * DC, st], 2, [P, DC, P]), ALU.mult)\
                        .then_inc(gdiag_ready, 1)

            def add_to_x(g, t, buf):
                wfilled(dve, g)
                V.tensor_tensor(buf, wbank(g)[:, :], grow[:, t // 2, :], ALU.mult)\
                    .then_inc(wide_free[g % WIDE], 1)
                wtaken(dve, g)
                V.tensor_tensor(x[:, t, :], x[:, t, :], buf, ALU.add).then_inc(x_new, 1)

            for s in L:
                l, n, T = s.l, s.n, s.n * P
                v = did(V.memset(upad[:, :, :, :].rearrange("p c s t -> p (c s t)"), 0.0))
                if l == 0:
                    dve.wait_ge(crow_ready, 1)
                    mod_products(s.mod_a, 0, 4 * len(s.mod_a))
                    for share in s.mod_pe:
                        modulation(*share)
                    need(junk_written[1])
                v = scales(l, 0)
                need(v)
                norm(s.norm1, 4, l, 0)
                for cc in range(2):
                    mod_products(s.mod_early, 8 * cc, 8 * cc + 8, early_junk)
                    taken(dve, s.conv_in + 2 * cc)
                    g = s.conv_in + 2 * cc + 1
                    filled(dve, g)
                    V.tensor_tensor(upad[:, cc, 0:s.sets, PAD:PAD + SEQ],
                                    bank(g)[:, 0:T].rearrange("p (s t) -> p s t", t=SEQ),
                                    sgc[:, cc, 0:T].rearrange("p (s t) -> p s t", t=SEQ), ALU.mult)\
                        .then_inc(ring_free[g % RING], 1)
                v = [0, 0]
                for k in range(TAPS):
                    for cc in range(2):
                        wc = C("w_dw", (l * 2 + cc) * TAPS + k)
                        src, dst = upad[:, cc, 0:s.sets, k:k + SEQ], cacc[:, cc, 0:s.sets, :]
                        if k == 0:
                            taken(dve, s.conv_in + 2 * cc + 1)
                            v[cc] = did(V.tensor_scalar(dst, src, wc, C("b_dw", 2 * l + cc), ALU.mult, ALU.add))
                        else:
                            need(v[cc])
                            ins = V.scalar_tensor_tensor(dst, src, wc, dst, ALU.mult, ALU.add)
                            if k == TAPS - 1:
                                ins.then_inc(conv_done, 1)
                            else:
                                v[cc] = did(ins)
                dve.wait_ge(std_ready, STD["lat", l])
                v = did(V.reciprocal(lr[:, 0:4 + n], lr[:, 0:4 + n]))
                need(v)
                for t in range(4):
                    ins = V.tensor_scalar(kvq[:, t, 0:KVL], kvq[:, t, 0:KVL], lr[:, t:t + 1], None, ALU.mult)
                    if t < n:
                        ins = V.tensor_scalar(kvq[:, t, KVR:416], kvq[:, t, KVR:416], lr[:, 4 + t:5 + t], None,
                                              ALU.mult)
                    ins.then_inc(lat_ready, 1)
                for i in range(2 * s.sets):
                    g = s.fn_f[i]
                    filled(dve, g)
                    V.tensor_copy(fT[:, i % 2, (i // 2) * SEQ:(i // 2 + 1) * SEQ], bank(g)[:, 0:SEQ])\
                        .then_inc(ring_free[g % RING], 1)
                g = s.lat_k
                filled(dve, g)
                V.tensor_scalar(ckvT, bank(g)[:, :], C("g_ckv", l), None, ALU.mult).then_inc(ring_free[g % RING], 1)
                for cc in range(2):
                    g = s.lat_q + cc
                    filled(dve, g)
                    V.tensor_scalar(cqT[:, cc, 0:T], bank(g)[:, 0:T], C("g_cq", 2 * l + cc), None, ALU.mult)\
                        .then_inc(ring_free[g % RING], 1)
                bufs = list(range(4)) + list(range(4, 4 + n))
                v = 0
                for b in bufs:
                    wtaken(dve, s.kv + b if b < 4 else s.q + b - 4)
                    if b < 4:
                        u = did(V.tensor_copy(kq[:, b, :, NOPE:QKH],
                                              bc(kvq[:, b, KVL:KVR], 1, [P, HEADS, ROPE])))
                        need(u)
                    elif v:
                        need(v)
                    u = did(V.tensor_tensor(sqb, kq[:, b, :, :], kq[:, b, :, :], ALU.mult))
                    need(u)
                    v = did(V.tensor_reduce(hss[:, 8 * b:8 * b + 8], sqb, AX_X, ALU.add))
                need(v)
                dve.nop().then_inc(stat_ready, 1)
                for t in range(n):
                    filled(dve, s.cv_t + t)
                    v = did(V.bn_stats(cst[:, 6 * t:6 * t + 6], bank(s.cv_t + t)[:, 0:CC]))
                need(v)
                for t in range(n):
                    ins = V.bn_aggr(cmv3[:, t, :], cst[:, 6 * t:6 * t + 6])
                ins.then_inc(stat_ready, 1)
                dve.wait_ge(std_ready, STD["heads", l])
                v_hr = did(V.reciprocal(hr[:, 0:32 + 8 * n], hss[:, 0:32 + 8 * n]))
                dve.wait_ge(std_ready, STD["conv", l])
                u = did(V.reciprocal(cr[:, 0:n], cr[:, 0:n]))
                need(u)
                for t in range(n):
                    g = s.cv_t + t
                    V.tensor_scalar(cn[:, t, :], bank(g)[:, 0:CC], cmv3[:, t, 0:1], cr[:, t:t + 1],
                                    ALU.subtract, ALU.mult).then_inc(ring_free[g % RING], 1)
                need(v_hr)
                dve.nop().then_inc(hr_ready, 1)
                v = head_norms(dve, V, l, range(4), rtmp, dve_order, order, kn_ready)
                def head_columns(h):
                    for g, dst, k in ((s.gk[h], kTb, 4), (s.gq[h], qTb, n)):
                        filled(dve, g)
                        V.tensor_copy(dst[0:QKH, h % 2, 0:k * P], bank(g)[0:QKH, 0:k * P])\
                            .then_inc(ring_free[g % RING], 1)

                head_columns(0)
                for i in range(s.N + 1):
                    if i < s.N:
                        t = i % n
                        g = s.gs[i]
                        kk = 512 if t < 2 else 256
                        filled(dve, g)
                        if i >= 4:
                            taken(dve, s.gs[i - 4])
                        v = did(V.tensor_reduce(nmax[:, i % 4:i % 4 + 1], bank(g)[:, 0:kk], AX_X, ALU.max,
                                                negate=True))
                        need(v)
                        V.tensor_scalar(nms[:, i % 4:i % 4 + 1], nmax[:, i % 4:i % 4 + 1], ATT_SCALE, None,
                                        ALU.mult).then_inc(max_ready, 1)
                        if t == 0 and i // n + 1 < HEADS:
                            head_columns(i // n + 1)
                    if i >= 1:
                        j = i - 1
                        kk = 512 if j % n < 2 else 256
                        taken(dve, s.gs[j])
                        v = did(V.reciprocal(rinv[:, j % 4:j % 4 + 1], rsum[:, j % 4:j % 4 + 1]))
                        need(v)
                        V.tensor_scalar(prob[:, j % 3, 0:kk], prob[:, j % 3, 0:kk], rinv[:, j % 4:j % 4 + 1],
                                        None, ALU.mult).then_inc(p_ready, 1)
                        mod_products(s.mod_b, j, j + 1)
                vs = {}
                for j in range(DC):
                    for b in range(BRANCH):
                        g = s.merge[j][1] + 2 * b
                        k = BRANCH * j + b
                        taken(dve, g)
                        filled(dve, g + 1)
                        if b and (b - 1, j - 1) in vs:
                            need(vs[b - 1, j - 1])
                        V.tensor_tensor(mT[:, j, 0:T] if b == 0 else mtmp[:, b - 1, 0:T], bank(g + 1)[:, 0:T],
                                        sgm[:, k % 2, 0:T], ALU.mult).then_inc(ring_free[(g + 1) % RING], 1)
                        if b:
                            taken(dve, g + 1)
                            if b == 2:
                                need(vs[0, j])
                            ins = V.tensor_tensor(mT[:, j, 0:T], mT[:, j, 0:T], mtmp[:, b - 1, 0:T], ALU.add)
                            if b == 2:
                                ins.then_inc(m_ready, 1)
                                dve.wait_ge(m_ready, DC * l + j + 1)
                            else:
                                vs[0, j] = did(ins)
                        mod_products(s.mods[j], (0, 5, 10)[b], (5, 10, 16)[b])
                if l == 0:
                    need(junk_written[1])
                    v = scales(0, 1)
                    v = scales(1, 0)
                    v = scales(1, 1)
                    need(v)
                gate_rows(2, l, s.sets, s.grow1)
                for g0 in s.grow1:
                    taken(dve, g0)
                    taken(dve, g0 + 1)
                for t in range(n):
                    add_to_x(s.out + t, t, xtmp[:, t % 2, :])
                norm(s.norm2, n, l, 1)
                gate_rows(5, l, s.sets, s.grow2)
                for g0 in s.grow2:
                    taken(dve, g0)
                    taken(dve, g0 + 1)

                q0 = SELQ[l]

                def hold():
                    dve.nop(nofuse=True)

                class Steps:

                    def __init__(self, i, base, par):
                        self.i, self.at = i, base + par * SEL_STEPS
                        self.end = self.at + SEL_STEPS

                    def did(self, ins):
                        ins.then_inc(sel_order, 1)
                        self.at += 1

                    def need(self):
                        dve.wait_ge(sel_order, self.i * (2 * SEL_STEPS) + self.at)
                        hold()

                def best_halves(st, par, it, sc):
                    dve.wait_ge(sel_full[par], it + 1)
                    hold()
                    for p_ in range(2):
                        st.did(V.max(sval[:, p_, 0:8], sc[p_]))
                    st.need()
                    for p_ in range(2):
                        st.did(V.max_index(sidx[:, p_, 0:8], sval[:, p_, 0:8], sc[p_]))
                        ins = V.match_replace(s2[:, p_, :], sval[:, p_, 0:8], sc[p_], NEG)
                        if p_ == 0:
                            st.did(ins)
                        else:
                            ins.then_inc(sel_free[par], 1)
                    dve.wait_ge(sel_free[par], it + 2)
                    hold()

                def rest_halves(st):
                    for p_ in range(2):
                        st.did(V.max(sval[:, p_, 8:16], s2[:, p_, :]))
                    st.need()
                    for p_ in range(2):
                        st.did(V.max_index(sidx[:, p_, 8:16], sval[:, p_, 8:16], s2[:, p_, :]))
                    st.did(V.tensor_tensor(cand, bc(sval[:, 0, :], 2, [P, TOPK, TOPK]),
                                           bc(sval[:, 1, :], 1, [P, TOPK, TOPK]), ALU.add))
                    st.need()

                def best_pairs(st, i, head):
                    cf = cand.rearrange("p a b -> p (a b)")
                    st.did(V.max(best[:, 0:8], cf))
                    st.need()
                    st.did(V.max_index(pos[:, 0:8], best[:, 0:8], cf))
                    st.did(V.match_replace(cand2, best[:, 0:8], cf, NEG))
                    st.did(V.tensor_scalar(nbest, best[:, 0:1], -1.0, None, ALU.mult))
                    st.need()
                    V.max(best[:, 8:16], cand2).then_inc(best_ready, 1)
                    dve.wait_ge(best_ready, i * 2 + (head + 1))
                    hold()
                    st.did(V.max_index(pos[:, 8:16], best[:, 8:16], cand2))
                    st.did(V.tensor_copy(sidf, sidx))
                    st.need()

                def pair_keys(st):
                    st.did(V.tensor_scalar(posu[:, 0, :], pos, 4, None, ALU.logical_shift_right))
                    st.did(V.tensor_scalar(posu[:, 1, :], pos, 15, None, ALU.bitwise_and))
                    st.need()
                    st.did(V.tensor_copy(posf, posu))
                    st.need()
                    pf = posf.rearrange("p b c -> p (b c)")
                    st.did(V.tensor_tensor(eq.rearrange("p b i j -> p (b i) j"), bc(pf, 2, [P, 2 * TOPK, TOPK]),
                                           bc(K("iota"), 1, [P, 2 * TOPK, TOPK]), ALU.is_equal))
                    st.need()
                    st.did(V.tensor_tensor(eqm, eq, bc(sidf, 2, [P, 2, TOPK, TOPK]), ALU.mult))
                    st.need()
                    st.did(V.tensor_reduce(rr, eqm, AX_X, ALU.add))
                    st.need()
                    st.did(V.tensor_scalar(ebase, rr[:, 0, :], float(NK), float(l * EXPERTS), ALU.mult, ALU.add))
                    st.need()

                def selected(st, i, head, at):
                    V.tensor_tensor(eid[:, bass.ds(i * 32 + at, TOPK)], ebase, rr[:, 1, :],
                                    ALU.add).then_inc(eid_ready, 1)
                    dve.wait_ge(gate_exp, i * 2 + (head + 1))
                    st.did(V.reciprocal(ginv, gsum))
                    st.need()
                    st.did(V.tensor_scalar(gate[:, bass.ds(i * 32 + at, TOPK)], gexp, ginv, None,
                                           ALU.mult))
                    assert st.at == st.end, (st.at, st.end)
                    st.need()

                def select(i, pair, par, it, at, sc):
                    st = Steps(i, 2 * SEL_STEPS * pair, par)
                    best_halves(st, par, it, sc)
                    rest_halves(st)
                    best_pairs(st, i, 2 * pair + par)
                    pair_keys(st)
                    selected(st, i, 2 * pair + par, at)

                for par in range(2):
                    dve.wait_ge(sel_full[1], 4 * q0 + 1)
                    select(0, 4 * q0, par, 4 * q0, TOPK * par, [first_scores(s, par, p_) for p_ in range(2)])
                for t in range(n):
                    q = q0 + t

                    def weights(i, par, nxt):
                        head = 8 * q + par
                        for k in range(TOPK):
                            dve.wait_ge(u_in[k % UB], i * (32 * 16 // UB) + 16 * ((16 * head + k) // UB + 1))
                            V.tensor_tensor_reduce(ub[k % UB], ub[k % UB], xn[:, t, :], 1.0, 0.0,
                                                   ALU.mult, ALU.add, dots[:, par, k:k + 1]).then_inc(u_free, 1)
                        dve.wait_ge(gelu_done, i * 2 + (head + 1))
                        V.tensor_tensor(actv[:, par, :], gel[:, par, :], gate[:, bass.ds(i * 32 + par * 16, TOPK)],
                                        ALU.mult).then_inc(act_ready, 1)
                        if nxt:
                            select(i, 4 * q + 1, par, i + (4 * q + 1), 2 * TOPK + TOPK * par,
                                   [ring[2 * par + p_][:, 0:NK] for p_ in range(2)])

                    head_pairs(dve, t, n, weights)
                    if t + 1 < n:
                        dve.wait_ge(act_ready, 8 * (q + 1))
                        dve.wait_ge(eid_ready, 8 * (q + 1) + 2)
                        V.tensor_copy(eid[:, 0:2 * TOPK], eid[:, P:P + 2 * TOPK]).then_inc(eid_moved, 1)
                        v = did(V.tensor_copy(gate[:, 0:2 * TOPK], gate[:, P:P + 2 * TOPK]))
                        need(v)
                        dve.wait_ge(eid_moved, MOVES[l] + t + 1)
                    if t >= 1:
                        add_to_x(s.exp + t - 1, t - 1, ytmp)
                        dve.wait_ge(x_new, XNEW["out", l] + t)
                add_to_x(s.exp + n - 1, n - 1, ytmp)

            r = pl.lru
            dve.wait_ge(x_new, XNEW["exp", 1])
            v = did(V.memset(lpad[:, :, 0:LCONV - 1], 0.0))
            for cidx in range(DC):
                taken(dve, r.proj[cidx // 2])
                for k in range(LCONV):
                    src = lpad[:, cidx, k:k + SEQ]
                    wc = C("lru_conv_w", k * DC + cidx)
                    need(v)
                    if k == 0:
                        v = did(V.tensor_scalar(xb[:, cidx, :], src, wc, C("lru_conv_b", cidx), ALU.mult, ALU.add))
                    else:
                        ins = V.scalar_tensor_tensor(xb[:, cidx, :], src, wc, xb[:, cidx, :], ALU.mult, ALU.add)
                        if k == LCONV - 1:
                            ins.then_inc(lru_xb, 1)
                        else:
                            v = did(ins)
            dve.wait_ge(lru_act, DC)
            v = did(V.tensor_scalar(lm[:, :, :], lm[:, :, :], -1.0, 1.0, ALU.mult, ALU.add))
            need(v)
            V.tensor_scalar(lm[:, :, :], lm[:, :, :], 0.0, None, ALU.max).then_inc(lru_dve, 1)
            dve.wait_ge(lru_xb, DC)
            v = did(V.tensor_tensor(gi[:, :, :], gi[:, :, :], xb[:, :, :], ALU.mult))
            need(v)
            dve.wait_ge(lru_act, DC + 1)
            v = did(V.memset(lm[:, :, 0:1], 1.0))
            need(v)
            v = did(V.tensor_tensor(gi[:, :, :], gi[:, :, :], lm[:, :, :], ALU.mult))
            need(v)
            for h in range(DC):
                v = did(V.tensor_tensor_scan(lm[:, h, :], gr[:, h, :], gi[:, h, :], 0.0, ALU.mult, ALU.add))
                need(v)
                taken(dve, r.proj[4 + h // 2])
                V.tensor_tensor(xb[:, h, :], lm[:, h, :], yb[:, h, :], ALU.mult).then_inc(lru_h, 1)

            def layer_norm(i, g0, bias):
                for t in range(2):
                    g = g0 + t
                    wfilled(dve, g)
                    V.scalar_tensor_tensor(x[:, t, :], x[:, t, :], ALPHA, wbank(g)[:, :], ALU.mult, ALU.add)\
                        .then_inc(wide_free[g % WIDE], 1)
                    wtaken(dve, g)
                    if bias:
                        need(did(V.tensor_tensor(x[:, t, :], x[:, t, :], borow, ALU.add)))
                    for h in range(2):
                        v = did(V.bn_stats(lst[:, 12 * t + 6 * h:12 * t + 6 * h + 6],
                                           x[:, t, h * 512:(h + 1) * 512]))
                need(v)
                for t in range(2):
                    ins = V.bn_aggr(lmv3[:, t, :], lst[:, 12 * t:12 * t + 12])
                ins.then_inc(stat_ready, 1)
                dve.wait_ge(std_ready, STD["ln", i])
                v = did(V.reciprocal(lrs, lrs))
                need(v)
                V.scalar_tensor_tensor(lnb, lmv3[:, :, 0], -1.0, lrs, ALU.mult, ALU.mult).then_inc(lnb_ready, 1)
                for t in range(2):
                    dve.wait_ge(ln_scaled, 2 * i + t + 1)
                    need(did(V.tensor_tensor(x[:, t, :], x[:, t, :], lnrow[:, i, 0, :], ALU.mult)))
                    V.tensor_tensor(x[:, t, :], x[:, t, :], lnrow[:, i, 1, :], ALU.add).then_inc(x_new, 1)

            def ffn(f):
                V.memset(hpad[:, :, :, :].rearrange("p b g t -> p (b g t)"), 0.0).then_inc(ffn_pad, 1)
                for j in range(FJ + 1):
                    if j < FJ:
                        g = f.up[j]
                        taken(dve, g)
                        if j >= 2:
                            dve.wait_ge(ffn_gel, FJ * f.l + j - 1)
                            dve.wait_ge(ffn_g, FJ * f.l + j - 1)
                        v = [0, 0]
                        for k in range(FCONV):
                            for m in range(2):
                                cidx = m * FJ + j
                                src = hpad[:, j % 2, m, k:k + SEQ]
                                dst = facc[:, j % 2, m, :]
                                wc = C("ffn_conv_w", (f.l * FCONV + k) * 2 * FJ + cidx)
                                if k == 0:
                                    v[m] = did(V.tensor_scalar(dst, src, wc, C("ffn_conv_b", f.l * 2 * FJ + cidx),
                                                               ALU.mult, ALU.add))
                                else:
                                    need(v[m])
                                    ins = V.scalar_tensor_tensor(dst, src, wc, dst, ALU.mult, ALU.add)
                                    if k == FCONV - 1:
                                        ins.then_inc(ffn_acc, 1)
                                    else:
                                        v[m] = did(ins)
                    if j >= 1:
                        i = j - 1
                        dve.wait_ge(ffn_gel, FJ * f.l + i + 1)
                        dve.wait_ge(ffn_acc, 2 * (FJ * f.l + i + 1))
                        if i >= 3:
                            filled(dve, f.up[i])
                        V.tensor_tensor(fgT[:, i % 3, :], fgel[:, i % 2, :], facc[:, i % 2, 1, :], ALU.mult)\
                            .then_inc(ffn_g, 1)

            dve.wait_ge(rows_in, 32)
            layer_norm(0, r.out, True)
            ffn(pl.ffn[0])
            layer_norm(1, pl.ffn[0].down, False)
            a = pl.stick
            v1 = did(V.memset(one_row, 1.0))
            need(v1)
            NB = 2 * H2 // BATCH
            for b in range(NB + 1):
                for j in range(max(b - 1, 0) * BATCH, b * BATCH):
                    kk = (j % 2 + 1) * P
                    w_ = zs[:, j % (3 * BATCH), kk - P:kk]
                    dve.wait_ge(z_out, j + 1)
                    V.tensor_tensor(w_, w_, K("tri"), ALU.mult).then_inc(z_w, 1)
                for i in range(b * BATCH, min(b + 1, NB) * BATCH):
                    kk = (i % 2 + 1) * P
                    zi, sp_, cum = zs[:, i % (3 * BATCH), 0:kk], zl[:, i % (2 * BATCH), 0:kk], zcum[:, i % 2, 0:kk]
                    dve.wait_ge(z_ln, i + 1)
                    need(did(V.scalar_tensor_tensor(sp_, zi, 0.0, sp_, ALU.max, ALU.add)))
                    need(did(V.tensor_tensor(sp_[:, kk - P:kk], sp_[:, kk - P:kk], K("tri"), ALU.mult)))
                    need(did(V.tensor_tensor_scan(cum[:, ::-1], one_row[:, 0:kk], sp_[:, ::-1], 0.0,
                                                  ALU.mult, ALU.add)))
                    need(did(V.tensor_tensor(zi, zi, cum, ALU.subtract)))
                    V.tensor_scalar(zi, zi, 0.0, None, ALU.min).then_inc(z_arg, 1)
            layer_norm(2, a.out, False)
            ffn(pl.ffn[1])
            layer_norm(3, pl.ffn[1].down, False)


SEL_STEPS = 25


def arrange(inputs):
    f = {k: np.asarray(v) for k, v in inputs.items()}
    o = {}

    def columns(a):
        a = a.reshape(-1, a.shape[-1] // P, P)
        return a.transpose(2, 0, 1).reshape(P, -1)

    parts = {
        "c": columns(f["c"]), "c_ctx": columns(f["c_ctx"]), "b_mod": columns(f["b_mod"]),
        "g_norm1": columns(f["g_norm1"]), "g_norm2": columns(f["g_norm2"]), "g_ckv": columns(f["g_ckv"]),
        "g_cq": columns(f["g_cq"]),
        "w_dw": f["w_dw"].reshape(LAYERS, TAPS, 2, P).transpose(3, 0, 2, 1).reshape(P, -1),
        "b_dw": columns(f["b_dw"]), "g_cln": columns(f["g_cln"]), "b_cln": columns(f["b_cln"]),
        "lru_b_in": columns(f["lru_b_in_2"]), "lru_conv_w": columns(f["lru_conv_w_2"]),
        "lru_conv_b": columns(f["lru_conv_b_2"]), "lru_b_gates": columns(f["lru_b_gates_2"]),
        "lru_a_param": columns(f["lru_a_param_2"]), "ffn_conv_w": columns(f["ffn_conv_w_2"]),
        "ffn_conv_b": columns(f["ffn_conv_b_2"]),
    }
    o["cols"] = np.concatenate([parts[n] for n, _ in COLS], 1)
    o["hrow"] = np.stack([f["g_qn"], f["g_kn"]], 1).reshape(-1)
    o["lnrow"] = np.stack([f["ln_g_2"], f["ln_b_2"]], 2).reshape(-1)
    o["lru_b_out"] = f["lru_b_out_2"].reshape(-1)
    o["x"], o["ctx"] = f["x"][0], f["ctx"][0]

    def by_columns(a, width):
        L_, k, n = a.shape
        return a.reshape(L_, k // P, P, n // width, width).transpose(0, 3, 2, 1, 4).reshape(L_, n // width, P, -1)

    def by_rows(a, items):
        L_, k, n = a.shape
        return a.reshape(L_, items, k // P // items, P, n).transpose(0, 1, 3, 2, 4).reshape(L_, items, P, -1)

    w_in = f["w_in"]
    o["w_mod"] = by_columns(f["w_mod"][0:1, :, 0:D], 512)
    o["w_mod_rows"] = f["w_mod"].reshape(LAYERS, D, 3 * DC, 2, P).transpose(0, 2, 4, 3, 1).reshape(
        LAYERS, 3 * DC, P, 2 * D)
    o["crow"] = np.concatenate([f["c"].reshape(-1), f["c_ctx"].reshape(-1)])
    o["w_a"] = by_rows(w_in[:, :, 0:672], 2)
    o["w_zc"] = by_columns(w_in[:, :, 672:1184], 512)
    zg = w_in[:, :, 1184:].reshape(LAYERS, DC, P, BRANCH, DC, P).transpose(0, 4, 2, 3, 1, 5)
    zg = zg.reshape(LAYERS, DC, P, BRANCH * DC * P)
    br = [by_columns(f[k], P) for k in ("wb_attn", "wb_fnet", "wb_conv")]
    o["w_m"] = np.concatenate([zg] + br, 3)
    o["w_uk"] = np.concatenate([by_rows(f["w_ukv"], 1), by_rows(f["w_uq"], 1)], 3)
    o["w_out"] = by_rows(f["w_out"], 2)
    o["w_query"] = by_columns(f["w_query"], 512)
    sk = f["sub_keys"].transpose(0, 2, 4, 1, 3)
    o["sub_keys"] = np.concatenate([sk, sk[:, :, :, 0:2]], 3).reshape(LAYERS, 1, P, (PH + 2) * NK)
    w = f["lru_w_in_2"]
    o["lru_in"] = by_columns(np.concatenate([w[:, :, W2:], w[:, :, :W2]], 2), 512)
    o["lru_gates"] = f["lru_w_gates_2"].transpose(0, 2, 1, 3).reshape(1, 1, P, -1)
    o["lru_out"] = by_rows(f["lru_w_out_2"], 2)
    o["kv_k"] = by_columns(f["kv_w_2"][None, :, :D], 512)
    o["kv_v"] = by_rows(f["kv_w_2"][None, :, D:], 2)
    o["attn_q"] = by_columns(f["attn_w_q_2"], 512)
    o["attn_out"] = by_rows(f["attn_w_out_2"], 2)
    up = f["ffn_w_up_2"]
    o["w_ffn"] = np.concatenate([by_columns(up[:, :, :FF], P), by_columns(up[:, :, FF:], P),
                                 by_rows(f["ffn_w_down_2"], FJ)], 3)
    o["u_tab"] = f["u_tab"].reshape(LAYERS * EXPERTS, D)
    o["v_tab"] = f["v_tab"].reshape(LAYERS * EXPERTS, D)
    o["const"] = shape_constants()
    return {k: np.ascontiguousarray(v) for k, v in o.items()}


def kernel(**inputs):
    import concourse.bacc as bacc
    from concourse.bass_utils import run_bass_kernel_spmd as run

    arrays = arrange(inputs)
    nc = bacc.Bacc("TRN2", target_bir_lowering=False, num_devices=1)
    args = {k: nc.dram_tensor(f"in_{k}", a.shape, mybir.dt.from_np(a.dtype), kind="ExternalInput").ap()
            for k, a in arrays.items()}
    out = nc.dram_tensor("out_x", (SEQ, D), F32, kind="ExternalOutput").ap()
    build(nc, args, out)
    r = run(nc, [{f"in_{k}": a for k, a in arrays.items()}], core_ids=[0])
    return r.results[0]["out_x"].reshape(1, SEQ, D)
```
